# Optimizing a Trainium2 kernel written in Bass

```python
import jax, jax.numpy as jnp
from jax import lax
import numpy as np
import math
import jax
import jax.numpy as jnp

D_MODEL = 1024
BATCH = 1
SEQ = 256
DEPTH = 2

N_META = 16
BLK = 128
PAD = BLK - N_META
ROPE_THETA = 10000.0
EPS = 1e-6
NEG = -1e30

FOX_HEADS = 8
FOX_DH = 64

MLA_HEADS = 8
MLA_NOPE = 64
MLA_ROPE = 32
MLA_V = 64
MLA_QLORA = 384
MLA_KVLORA = 256

SWA_HEADS = 8
SWA_KV_HEADS = 2
SWA_DH = 64
WINDOW = 128

BRANCH_W = 512
N_BRANCH = 3

SPLIT_SIZES = (
    FOX_HEADS * FOX_DH, FOX_HEADS * FOX_DH, FOX_HEADS * FOX_DH, FOX_HEADS, BRANCH_W,
    MLA_QLORA, MLA_KVLORA, MLA_ROPE, BRANCH_W,
    SWA_HEADS * SWA_DH, SWA_KV_HEADS * SWA_DH, SWA_KV_HEADS * SWA_DH, BRANCH_W,
    N_BRANCH * D_MODEL,
)
N_IN = sum(SPLIT_SIZES)


def rmsnorm(x, g):
    xf = x.astype(jnp.float32)
    y = xf * lax.rsqrt(jnp.mean(xf * xf, axis=-1, keepdims=True) + EPS)
    return (y * g.astype(jnp.float32)).astype(x.dtype)

def rope(x, pos):
    half = x.shape[-1] // 2
    inv = ROPE_THETA ** (-jnp.arange(half, dtype=jnp.float32) / half)
    ang = pos.astype(jnp.float32)[:, None] * inv[None, :]
    cos = jnp.cos(ang)[None, :, None, :]
    sin = jnp.sin(ang)[None, :, None, :]
    xf = x.astype(jnp.float32)
    x1, x2 = xf[..., :half], xf[..., half:]
    return jnp.concatenate([x1 * cos - x2 * sin, x2 * cos + x1 * sin], axis=-1).astype(x.dtype)

def causal_block_attention(q, k, v, scale, log_cum=None):
    B, L, H, _ = q.shape
    nb = L // BLK
    kpos = jnp.arange(L)
    key_ok = kpos >= PAD
    qb = jnp.moveaxis(q.reshape(B, nb, BLK, H, q.shape[-1]), 1, 0)
    if log_cum is None:
        xs = (jnp.arange(nb), qb)
        ck = None
    else:
        cb = jnp.moveaxis(log_cum.reshape(B, nb, BLK, H), 1, 0)
        xs = (jnp.arange(nb), qb, cb)
        ck = jnp.swapaxes(log_cum, 1, 2)

    def block(args):
        i, qi = args[0], args[1]
        s = jnp.einsum('bqhd,bkhd->bhqk', qi, k).astype(jnp.float32) * scale
        if log_cum is not None:
            ci = jnp.swapaxes(args[2], 1, 2)
            s = s + (ci[..., :, None] - ck[..., None, :])
        qpos = i * BLK + jnp.arange(BLK)
        mask = (kpos[None, :] <= qpos[:, None]) & key_ok[None, :]
        s = jnp.where(mask, s, NEG)
        p = jax.nn.softmax(s, axis=-1)
        return jnp.einsum('bhqk,bkhd->bqhd', p.astype(v.dtype), v)

    o = lax.map(block, xs)
    return jnp.moveaxis(o, 0, 1).reshape(B, L, H, v.shape[-1])

def sliding_window_sink_attention(q, k, v, sinks):
    B, L, H, D = q.shape
    Hkv = k.shape[2]
    G = H // Hkv
    nb = L // BLK
    qb = q.reshape(B, nb, BLK, Hkv, G, D)

    def with_prev(t):
        prev = jnp.concatenate([jnp.zeros_like(t[:, :1]), t[:, :-1]], axis=1)
        return jnp.concatenate([prev, t], axis=2)

    kx = with_prev(k.reshape(B, nb, BLK, Hkv, D))
    vx = with_prev(v.reshape(B, nb, BLK, Hkv, D))
    s = jnp.einsum('bnqhgd,bnkhd->bnhgqk', qb, kx).astype(jnp.float32) * (D ** -0.5)
    blocks = jnp.arange(nb)[:, None]
    qpos = blocks * BLK + jnp.arange(BLK)[None, :]
    kpos = (blocks - 1) * BLK + jnp.arange(2 * BLK)[None, :]
    rel = qpos[:, :, None] - kpos[:, None, :]
    mask = (rel >= 0) & (rel < WINDOW) & (kpos >= PAD)[:, None, :]
    s = jnp.where(mask[None, :, None, None], s, NEG)
    sink = jnp.broadcast_to(sinks.astype(jnp.float32).reshape(1, 1, Hkv, G, 1, 1), s.shape[:-1] + (1,))
    p = jax.nn.softmax(jnp.concatenate([s, sink], axis=-1), axis=-1)[..., :-1]
    o = jnp.einsum('bnhgqk,bnkhd->bnqhgd', p.astype(v.dtype), vx)
    return o.reshape(B, L, H, D)

def hybrid_layer(x, pos, norm_g, w_in, b_f, g_cq, g_ckv, w_uq, w_ukv, sinks, w_branch, w_out):
    B, L, _ = x.shape
    h = rmsnorm(x, norm_g)
    proj = h @ w_in
    (a_q, a_k, a_v, a_f, a_z,
     b_cq, b_ckv, b_kr, b_z,
     c_q, c_k, c_v, c_z, gates) = jnp.split(proj, np.cumsum(SPLIT_SIZES)[:-1], axis=-1)

    log_f = jax.nn.log_sigmoid((a_f + b_f).astype(jnp.float32))
    log_cum = jnp.cumsum(log_f, axis=1)
    y_a = causal_block_attention(a_q.reshape(B, L, FOX_HEADS, FOX_DH),
                                 a_k.reshape(B, L, FOX_HEADS, FOX_DH),
                                 a_v.reshape(B, L, FOX_HEADS, FOX_DH),
                                 FOX_DH ** -0.5, log_cum)

    cq = rmsnorm(b_cq, g_cq)
    ckv = rmsnorm(b_ckv, g_ckv)
    qB = (cq @ w_uq).reshape(B, L, MLA_HEADS, MLA_NOPE + MLA_ROPE)
    q_b = jnp.concatenate([qB[..., :MLA_NOPE], rope(qB[..., MLA_NOPE:], pos)], axis=-1)
    kvB = (ckv @ w_ukv).reshape(B, L, MLA_HEADS, MLA_NOPE + MLA_V)
    k_rope = rope(b_kr.reshape(B, L, 1, MLA_ROPE), pos)
    k_b = jnp.concatenate([kvB[..., :MLA_NOPE],
                           jnp.broadcast_to(k_rope, (B, L, MLA_HEADS, MLA_ROPE))], axis=-1)
    v_b = kvB[..., MLA_NOPE:]
    y_b = causal_block_attention(q_b, k_b, v_b, (MLA_NOPE + MLA_ROPE) ** -0.5)

    qc = rope(c_q.reshape(B, L, SWA_HEADS, SWA_DH), pos)
    kc = rope(c_k.reshape(B, L, SWA_KV_HEADS, SWA_DH), pos)
    vc = c_v.reshape(B, L, SWA_KV_HEADS, SWA_DH)
    y_c = sliding_window_sink_attention(qc, kc, vc, sinks)

    branches = jnp.stack([y_a.reshape(B, L, BRANCH_W) * jax.nn.silu(a_z),
                          y_b.reshape(B, L, BRANCH_W) * jax.nn.silu(b_z),
                          y_c.reshape(B, L, BRANCH_W) * jax.nn.silu(c_z)], axis=2)
    proj_br = jnp.einsum('blnw,nwd->blnd', branches, w_branch)
    g = jax.nn.sigmoid(gates.reshape(B, L, N_BRANCH, D_MODEL))
    merged = jnp.sum(g * proj_br, axis=2)
    return x + merged @ w_out

def first_inputs(seed: int = 0) -> dict:
    key = jax.random.key(seed)
    ks = jax.random.split(key, 14)
    f32 = jnp.float32
    nrm = lambda k, shape, scale: jax.random.normal(k, shape, f32) * scale
    return {
        "x": nrm(ks[0], (BATCH, SEQ, D_MODEL), 1.0),
        "meta_tokens": nrm(ks[1], (N_META, D_MODEL), 1.0),
        "norm_g": 1.0 + nrm(ks[2], (DEPTH, D_MODEL), 0.02),
        "w_in": nrm(ks[3], (DEPTH, D_MODEL, N_IN), D_MODEL ** -0.5),
        "b_f": jax.random.uniform(ks[4], (DEPTH, FOX_HEADS), f32, 1.0, 4.0),
        "g_cq": 1.0 + nrm(ks[5], (DEPTH, MLA_QLORA), 0.02),
        "g_ckv": 1.0 + nrm(ks[6], (DEPTH, MLA_KVLORA), 0.02),
        "w_uq": nrm(ks[7], (DEPTH, MLA_QLORA, MLA_HEADS * (MLA_NOPE + MLA_ROPE)), MLA_QLORA ** -0.5),
        "w_ukv": nrm(ks[8], (DEPTH, MLA_KVLORA, MLA_HEADS * (MLA_NOPE + MLA_V)), MLA_KVLORA ** -0.5),
        "sinks": nrm(ks[9], (DEPTH, SWA_HEADS), 0.5),
        "w_branch": nrm(ks[10], (DEPTH, N_BRANCH, BRANCH_W, D_MODEL), BRANCH_W ** -0.5),
        "w_out": nrm(ks[11], (DEPTH, D_MODEL, D_MODEL), D_MODEL ** -0.5),
        "final_g": 1.0 + nrm(ks[12], (D_MODEL,), 0.02),
    }

def first_block(x, meta_tokens, norm_g, w_in, b_f, g_cq, g_ckv, w_uq, w_ukv, sinks, w_branch, w_out, final_g):
    B = x.shape[0]
    pad = jnp.zeros((B, PAD, D_MODEL), x.dtype)
    meta = jnp.broadcast_to(meta_tokens.astype(x.dtype)[None], (B, N_META, D_MODEL))
    h = jnp.concatenate([pad, meta, x], axis=1)
    pos = jnp.arange(h.shape[1]) - PAD
    for l in range(DEPTH):
        h = hybrid_layer(h, pos, norm_g[l], w_in[l], b_f[l], g_cq[l], g_ckv[l],
                         w_uq[l], w_ukv[l], sinks[l], w_branch[l], w_out[l])
    h = rmsnorm(h, final_g)
    return h[:, BLK:]


MIX_W = D_MODEL // 4
N_BRANCH_2 = 4
CHUNK = 64
ROPE_BASE = 10000.0
CONV_K = 4

RET_HEADS = 4
RET_DK = MIX_W // RET_HEADS
RET_DV = MIX_W // RET_HEADS

SSD_HEADS = 4
SSD_P = MIX_W // SSD_HEADS
SSD_N = 128
SSD_GROUPS = 2
SSD_CONV_CH = MIX_W + 2 * SSD_GROUPS * SSD_N

GLA_HEADS = 4
GLA_DK = MIX_W // (2 * GLA_HEADS)
GLA_DV = MIX_W // GLA_HEADS
GLA_RANK = 16
GLA_TAU = 16.0

ML_HEADS = 4
ML_DK = MIX_W // ML_HEADS
ML_DV = MIX_W // ML_HEADS

D_FF = 2816
N_EXPERTS = 8
TOP_K = 2
EXPERT_FF = 2816

IN_SIZES = (
    MIX_W, MIX_W, MIX_W, MIX_W,
    MIX_W, SSD_CONV_CH, SSD_HEADS,
    GLA_HEADS * GLA_DK, GLA_HEADS * GLA_DK, MIX_W, MIX_W, GLA_RANK,
    2 * MIX_W, MIX_W, MIX_W, ML_HEADS, ML_HEADS,
    N_BRANCH_2 * D_MODEL,
)
IN_COLS = sum(IN_SIZES)


def rmsnorm_2(x, g):
    xf = x.astype(jnp.float32)
    y = xf * lax.rsqrt(jnp.mean(xf * xf, axis=-1, keepdims=True) + EPS)
    return (y * g.astype(jnp.float32)).astype(x.dtype)

def head_rmsnorm(t, g):
    nh, d = t.shape[-2], t.shape[-1]
    return rmsnorm_2(t, g.reshape(nh, d))

def rotary(t, pos):
    half = t.shape[-1] // 2
    inv = ROPE_BASE ** (-jnp.arange(half, dtype=jnp.float32) / half)
    ang = pos.astype(jnp.float32)[:, None] * inv[None, :]
    cos = jnp.cos(ang)[None, :, None, :]
    sin = jnp.sin(ang)[None, :, None, :]
    t1 = t[..., :half].astype(jnp.float32)
    t2 = t[..., half:].astype(jnp.float32)
    return jnp.concatenate([t1 * cos - t2 * sin, t1 * sin + t2 * cos], axis=-1)

def causal_dwconv(u, w, b):
    ch = u.shape[-1]
    y = lax.conv_general_dilated(u, w[:, None, :].astype(u.dtype), window_strides=(1,),
                                 padding=[(CONV_K - 1, 0)],
                                 dimension_numbers=('NWC', 'WIO', 'NWC'),
                                 feature_group_count=ch)
    return y + b

def _chunk(t):
    t = t.astype(jnp.float32)
    bsz, seq, nh = t.shape[:3]
    t = t.reshape((bsz, seq // CHUNK, CHUNK, nh) + t.shape[3:])
    return jnp.moveaxis(t, (1, 3), (0, 2))

def _unchunk(t):
    t = jnp.moveaxis(t, (0, 2), (1, 3))
    return t.reshape((t.shape[0], t.shape[1] * t.shape[2]) + t.shape[3:])

def _tri():
    return jnp.tril(jnp.ones((CHUNK, CHUNK), dtype=bool))

def retention_scan(q, k, v, log_gamma):
    bsz, _, nh, dk = q.shape
    dv = v.shape[-1]
    idx = jnp.arange(CHUNK, dtype=jnp.float32)
    rel = idx[:, None] - idx[None, :]
    tri = rel >= 0
    decay = jnp.where(tri[None], jnp.exp(jnp.where(tri, rel, 0.0)[None] * log_gamma[:, None, None]), 0.0)
    q_decay = jnp.exp((idx + 1.0)[None, :] * log_gamma[:, None])
    k_decay = jnp.exp((CHUNK - 1.0 - idx)[None, :] * log_gamma[:, None])
    chunk_decay = jnp.exp(CHUNK * log_gamma)

    def step(state, inp):
        qc, kc, vc = inp
        s = jnp.einsum('bhid,bhjd->bhij', qc, kc) * decay
        o = (jnp.einsum('bhij,bhjv->bhiv', s, vc)
             + jnp.einsum('bhid,bhdv->bhiv', qc, state) * q_decay[:, :, None])
        state = (state * chunk_decay[:, None, None]
                 + jnp.einsum('bhjd,bhjv->bhdv', kc * k_decay[:, :, None], vc))
        return state, o

    s0 = jnp.zeros((bsz, nh, dk, dv), jnp.float32)
    _, o = lax.scan(step, s0, (_chunk(q), _chunk(k), _chunk(v)))
    return _unchunk(o)

def ssd_scan(x, dt, bmat, cmat, a):
    bsz, _, nh, p = x.shape
    n = bmat.shape[-1]
    tri = _tri()

    def step(state, inp):
        xc, dtc, bc, cc = inp
        acs = jnp.cumsum(dtc * a[None, :, None], axis=-1)
        seg = jnp.exp(jnp.where(tri, acs[..., :, None] - acs[..., None, :], -jnp.inf))
        scores = jnp.einsum('bhin,bhjn->bhij', cc, bc) * seg
        xdt = xc * dtc[..., None]
        y = (jnp.einsum('bhij,bhjp->bhip', scores, xdt)
             + jnp.einsum('bhin,bhpn->bhip', cc, state) * jnp.exp(acs)[..., None])
        w_end = jnp.exp(acs[..., -1:] - acs)
        state = (state * jnp.exp(acs[..., -1])[..., None, None]
                 + jnp.einsum('bhjp,bhjn->bhpn', xdt * w_end[..., None], bc))
        return state, y

    s0 = jnp.zeros((bsz, nh, p, n), jnp.float32)
    _, y = lax.scan(step, s0, (_chunk(x), _chunk(dt), _chunk(bmat), _chunk(cmat)))
    return _unchunk(y)

def gla_scan(q, k, v, log_alpha):
    bsz, _, nh, dk = q.shape
    dv = v.shape[-1]
    tri = _tri()

    def step(state, inp):
        qc, kc, vc, gc = inp
        g = jnp.cumsum(gc, axis=2)
        seg = jnp.exp(jnp.where(tri[:, :, None], g[:, :, :, None, :] - g[:, :, None, :, :], -jnp.inf))
        att = jnp.sum(qc[:, :, :, None, :] * kc[:, :, None, :, :] * seg, axis=-1)
        o = (jnp.einsum('bhij,bhjv->bhiv', att, vc)
             + jnp.einsum('bhid,bhdv->bhiv', qc * jnp.exp(g), state))
        g_end = g[:, :, -1:, :]
        state = (state * jnp.exp(g_end[:, :, 0, :])[..., None]
                 + jnp.einsum('bhjd,bhjv->bhdv', kc * jnp.exp(g_end - g), vc))
        return state, o

    s0 = jnp.zeros((bsz, nh, dk, dv), jnp.float32)
    _, o = lax.scan(step, s0, (_chunk(q), _chunk(k), _chunk(v), _chunk(log_alpha)))
    return _unchunk(o)

def mlstm_scan(q, k, v, i_pre, log_f):
    bsz, _, nh, dk = q.shape
    dv = v.shape[-1]
    tri = _tri()

    def step(carry, inp):
        c_st, n_st, m = carry
        qc, kc, vc, ic, fc = inp
        b = jnp.cumsum(fc, axis=-1)
        dlog = jnp.where(tri, b[..., :, None] - b[..., None, :] + ic[..., None, :], -jnp.inf)
        inter = b + m[..., None]
        m_t = jnp.maximum(inter, jnp.max(dlog, axis=-1))
        s = jnp.einsum('bhid,bhjd->bhij', qc, kc) * jnp.exp(dlog - m_t[..., None])
        inter_w = jnp.exp(inter - m_t)
        num = (jnp.einsum('bhij,bhjv->bhiv', s, vc)
               + jnp.einsum('bhid,bhdv->bhiv', qc, c_st) * inter_w[..., None])
        den = jnp.sum(s, axis=-1) + jnp.einsum('bhid,bhd->bhi', qc, n_st) * inter_w
        h = num / jnp.maximum(jnp.abs(den), jnp.exp(-m_t))[..., None]
        b_end = b[..., -1]
        w_log = b_end[..., None] - b + ic
        m_new = jnp.maximum(b_end + m, jnp.max(w_log, axis=-1))
        w = jnp.exp(w_log - m_new[..., None])
        carry_decay = jnp.exp(b_end + m - m_new)
        kw = kc * w[..., None]
        c_st = c_st * carry_decay[..., None, None] + jnp.einsum('bhjd,bhjv->bhdv', kw, vc)
        n_st = n_st * carry_decay[..., None] + jnp.sum(kw, axis=2)
        return (c_st, n_st, m_new), h

    init = (jnp.zeros((bsz, nh, dk, dv), jnp.float32),
            jnp.zeros((bsz, nh, dk), jnp.float32),
            jnp.zeros((bsz, nh), jnp.float32))
    _, h = lax.scan(step, init, (_chunk(q), _chunk(k), _chunk(v), _chunk(i_pre), _chunk(log_f)))
    return _unchunk(h)

def _split_cols(u):
    outs, start = [], 0
    for width in IN_SIZES:
        outs.append(u[..., start:start + width])
        start += width
    return outs

def token_mixers(h, pos, w_in, ret_norm_g, ssd_conv_w, ssd_conv_b, ssd_dt_bias, ssd_a_log, ssd_d,
                 ssd_norm_g, gla_w_alpha, gla_b_alpha, gla_norm_g, ml_conv_w, ml_conv_b, ml_b_i,
                 ml_b_f, ml_norm_g, w_branch, w_out):
    bsz, seq, _ = h.shape
    u = h @ w_in
    (rq, rk, rv, rg, sz, sxbc, sdt, gq, gk, gv, gr, ga,
     mqk, mv, mo, mi, mf, mgate) = _split_cols(u)

    def heads(t, nh):
        return t.reshape(bsz, seq, nh, -1)

    log_gamma = jnp.log1p(-jnp.exp2(-5.0 - jnp.arange(RET_HEADS, dtype=jnp.float32)))
    q = rotary(heads(rq, RET_HEADS), pos)
    k = rotary(heads(rk, RET_HEADS), pos) * (RET_DK ** -0.5)
    o = retention_scan(q, k, heads(rv, RET_HEADS), log_gamma)
    y_ret = (head_rmsnorm(o, ret_norm_g).reshape(bsz, seq, MIX_W) * jax.nn.silu(rg)).astype(h.dtype)

    xbc = jax.nn.silu(causal_dwconv(sxbc, ssd_conv_w, ssd_conv_b))
    sx = xbc[..., :MIX_W]
    sb = xbc[..., MIX_W:MIX_W + SSD_GROUPS * SSD_N].reshape(bsz, seq, SSD_GROUPS, SSD_N)
    sc = xbc[..., MIX_W + SSD_GROUPS * SSD_N:].reshape(bsz, seq, SSD_GROUPS, SSD_N)
    rep = SSD_HEADS // SSD_GROUPS
    bh = jnp.repeat(sb, rep, axis=2)
    ch = jnp.repeat(sc, rep, axis=2)
    dt = jax.nn.softplus(sdt.astype(jnp.float32) + ssd_dt_bias.astype(jnp.float32))
    a = -jnp.exp(ssd_a_log.astype(jnp.float32))
    xs = heads(sx, SSD_HEADS).astype(jnp.float32)
    y = ssd_scan(xs, dt, bh, ch, a) + ssd_d.astype(jnp.float32)[:, None] * xs
    y_ssd = rmsnorm_2(y.reshape(bsz, seq, MIX_W) * jax.nn.silu(sz), ssd_norm_g).astype(h.dtype)

    alpha_pre = (ga @ gla_w_alpha + gla_b_alpha).astype(jnp.float32)
    log_alpha = heads(jax.nn.log_sigmoid(alpha_pre) / GLA_TAU, GLA_HEADS)
    q = heads(gq, GLA_HEADS) * (GLA_DK ** -0.5)
    o = gla_scan(q, heads(gk, GLA_HEADS), heads(gv, GLA_HEADS), log_alpha)
    y_gla = (head_rmsnorm(o, gla_norm_g).reshape(bsz, seq, MIX_W) * jax.nn.silu(gr)).astype(h.dtype)

    qk = jax.nn.silu(causal_dwconv(mqk, ml_conv_w, ml_conv_b))
    q = heads(qk[..., :MIX_W], ML_HEADS)
    k = heads(qk[..., MIX_W:], ML_HEADS) * (ML_DK ** -0.5)
    i_pre = mi.astype(jnp.float32) + ml_b_i.astype(jnp.float32)
    log_f = jax.nn.log_sigmoid(mf.astype(jnp.float32) + ml_b_f.astype(jnp.float32))
    o = mlstm_scan(q, k, heads(mv, ML_HEADS), i_pre, log_f)
    y_ml = (head_rmsnorm(o, ml_norm_g).reshape(bsz, seq, MIX_W) * jax.nn.sigmoid(mo)).astype(h.dtype)

    ybr = jnp.stack([y_ret, y_ssd, y_gla, y_ml], axis=2)
    gates = jax.nn.sigmoid(mgate.reshape(bsz, seq, N_BRANCH_2, D_MODEL))
    merged = jnp.sum(gates * jnp.einsum('bsnv,nvd->bsnd', ybr, w_branch), axis=2)
    return merged @ w_out

def swiglu(h, w1, w3, w2):
    return (jax.nn.silu(h @ w1) * (h @ w3)) @ w2

def moe_ffn(h, router_w, w1, w3, w2):
    logits = (h @ router_w).astype(jnp.float32)
    top_vals, top_idx = lax.top_k(logits, TOP_K)
    top_w = jax.nn.softmax(top_vals, axis=-1)
    gate = jnp.sum(jax.nn.one_hot(top_idx, N_EXPERTS, dtype=jnp.float32) * top_w[..., None], axis=-2)
    out = jnp.zeros_like(h)
    for e in range(N_EXPERTS):
        out = out + gate[..., e:e + 1].astype(h.dtype) * swiglu(h, w1[e], w3[e], w2[e])
    return out

def second_inputs(seed: int = 0) -> dict:
    key = jax.random.key(seed)
    ks = jax.random.split(key, 40)
    f32 = jnp.float32

    def nrm(i, shape, scale):
        return scale * jax.random.normal(ks[i], shape, f32)

    def gain(i, shape):
        return 1.0 + nrm(i, shape, 0.02)

    nl = DEPTH
    nd = (DEPTH + 1) // 2
    nm = DEPTH // 2
    res = (2.0 * DEPTH) ** -0.5
    dt = jnp.exp(jax.random.uniform(ks[8], (nl, SSD_HEADS), f32, math.log(1e-3), math.log(1e-1)))
    return {
        'x': nrm(0, (BATCH, SEQ, D_MODEL), 1.0),
        'mix_norm_g': gain(1, (nl, D_MODEL)),
        'w_in': nrm(2, (nl, D_MODEL, IN_COLS), D_MODEL ** -0.5),
        'ret_norm_g': gain(3, (nl, MIX_W)),
        'ssd_conv_w': nrm(4, (nl, CONV_K, SSD_CONV_CH), CONV_K ** -0.5),
        'ssd_conv_b': nrm(5, (nl, SSD_CONV_CH), 0.02),
        'ssd_dt_bias': dt + jnp.log(-jnp.expm1(-dt)),
        'ssd_a_log': jnp.log(jax.random.uniform(ks[9], (nl, SSD_HEADS), f32, 1.0, 16.0)),
        'ssd_d': 1.0 + nrm(10, (nl, SSD_HEADS), 0.1),
        'ssd_norm_g': gain(11, (nl, MIX_W)),
        'gla_w_alpha': nrm(12, (nl, GLA_RANK, GLA_HEADS * GLA_DK), GLA_RANK ** -0.5),
        'gla_b_alpha': nrm(13, (nl, GLA_HEADS * GLA_DK), 0.1),
        'gla_norm_g': gain(14, (nl, MIX_W)),
        'ml_conv_w': nrm(15, (nl, CONV_K, 2 * MIX_W), CONV_K ** -0.5),
        'ml_conv_b': nrm(16, (nl, 2 * MIX_W), 0.02),
        'ml_b_i': nrm(17, (nl, ML_HEADS), 0.1),
        'ml_b_f': jnp.linspace(3.0, 6.0, ML_HEADS, dtype=f32)[None, :] + nrm(18, (nl, ML_HEADS), 0.1),
        'ml_norm_g': gain(19, (nl, MIX_W)),
        'w_branch': nrm(20, (nl, N_BRANCH_2, MIX_W, D_MODEL), MIX_W ** -0.5),
        'w_out': nrm(21, (nl, D_MODEL, D_MODEL), res * D_MODEL ** -0.5),
        'ffn_norm_g': gain(22, (nl, D_MODEL)),
        'ffn_w1': nrm(23, (nd, D_MODEL, D_FF), D_MODEL ** -0.5),
        'ffn_w3': nrm(24, (nd, D_MODEL, D_FF), D_MODEL ** -0.5),
        'ffn_w2': nrm(25, (nd, D_FF, D_MODEL), res * D_FF ** -0.5),
        'router_w': nrm(26, (nm, D_MODEL, N_EXPERTS), D_MODEL ** -0.5),
        'moe_w1': nrm(27, (nm, N_EXPERTS, D_MODEL, EXPERT_FF), D_MODEL ** -0.5),
        'moe_w3': nrm(28, (nm, N_EXPERTS, D_MODEL, EXPERT_FF), D_MODEL ** -0.5),
        'moe_w2': nrm(29, (nm, N_EXPERTS, EXPERT_FF, D_MODEL), res * EXPERT_FF ** -0.5),
        'final_norm_g': gain(30, (D_MODEL,)),
    }

def second_block(x, mix_norm_g, w_in, ret_norm_g, ssd_conv_w, ssd_conv_b, ssd_dt_bias, ssd_a_log, ssd_d,
              ssd_norm_g, gla_w_alpha, gla_b_alpha, gla_norm_g, ml_conv_w, ml_conv_b, ml_b_i, ml_b_f,
              ml_norm_g, w_branch, w_out, ffn_norm_g, ffn_w1, ffn_w3, ffn_w2, router_w, moe_w1, moe_w3,
              moe_w2, final_norm_g):
    pos = jnp.arange(x.shape[1], dtype=jnp.int32)
    for l in range(DEPTH):
        h = rmsnorm_2(x, mix_norm_g[l])
        x = x + token_mixers(h, pos, w_in[l], ret_norm_g[l], ssd_conv_w[l], ssd_conv_b[l], ssd_dt_bias[l],
                             ssd_a_log[l], ssd_d[l], ssd_norm_g[l], gla_w_alpha[l], gla_b_alpha[l],
                             gla_norm_g[l], ml_conv_w[l], ml_conv_b[l], ml_b_i[l], ml_b_f[l], ml_norm_g[l],
                             w_branch[l], w_out[l]).astype(x.dtype)
        h = rmsnorm_2(x, ffn_norm_g[l])
        if l % 2 == 0:
            x = x + swiglu(h, ffn_w1[l // 2], ffn_w3[l // 2], ffn_w2[l // 2]).astype(x.dtype)
        else:
            x = x + moe_ffn(h, router_w[l // 2], moe_w1[l // 2], moe_w3[l // 2], moe_w2[l // 2]).astype(x.dtype)
    return rmsnorm_2(x, final_norm_g)


def setup_inputs(seed=0):
    out = dict(first_inputs(seed))
    for name, value in second_inputs(seed + 1).items():
        if name != "x":
            out[name + "_2"] = value
    return out


def reference(
    x, meta_tokens, norm_g, w_in, b_f, g_cq, g_ckv, w_uq, w_ukv, sinks, w_branch, w_out,
    final_g, mix_norm_g_2, w_in_2, ret_norm_g_2, ssd_conv_w_2, ssd_conv_b_2, ssd_dt_bias_2,
    ssd_a_log_2, ssd_d_2, ssd_norm_g_2, gla_w_alpha_2, gla_b_alpha_2, gla_norm_g_2, ml_conv_w_2,
    ml_conv_b_2, ml_b_i_2, ml_b_f_2, ml_norm_g_2, w_branch_2, w_out_2, ffn_norm_g_2, ffn_w1_2,
    ffn_w3_2, ffn_w2_2, router_w_2, moe_w1_2, moe_w3_2, moe_w2_2, final_norm_g_2,
):
    x = first_block(
        x, meta_tokens, norm_g, w_in, b_f, g_cq, g_ckv, w_uq, w_ukv, sinks, w_branch, w_out,
        final_g,
    )
    return second_block(
        x, mix_norm_g_2, w_in_2, ret_norm_g_2, ssd_conv_w_2, ssd_conv_b_2, ssd_dt_bias_2,
        ssd_a_log_2, ssd_d_2, ssd_norm_g_2, gla_w_alpha_2, gla_b_alpha_2, gla_norm_g_2,
        ml_conv_w_2, ml_conv_b_2, ml_b_i_2, ml_b_f_2, ml_norm_g_2, w_branch_2, w_out_2,
        ffn_norm_g_2, ffn_w1_2, ffn_w3_2, ffn_w2_2, router_w_2, moe_w1_2, moe_w3_2, moe_w2_2,
        final_norm_g_2,
    )


_drawn_inputs = setup_inputs


def setup_inputs(seed=0):
    import zlib

    import numpy as np

    out = dict(_drawn_inputs(seed))
    spreads = {}
    factors = {'norm_g': 3.106,
     'g_cq': 8.0,
     'g_ckv': 6.299,
     'sinks': 5.607,
     'ret_norm_g_2': 20.437,
     'ssd_conv_b_2': 3.099,
     'ssd_norm_g_2': 11.948,
     'gla_b_alpha_2': 3.5,
     'gla_norm_g_2': 21.0,
     'ml_conv_b_2': 7.532,
     'ml_b_i_2': 64.0,
     'ml_norm_g_2': 22.315,
     'final_norm_g_2': 7.742,
     'ffn_norm_g_2': 6.651}
    for name, (base, spread) in spreads.items():
        noise = np.random.default_rng([zlib.crc32(name.encode()), seed]).standard_normal(out[name].shape)
        drawn = base * np.exp(spread * noise) if base else spread * noise
        out[name] = jnp.asarray(drawn.astype(out[name].dtype))
    for name, factor in factors.items():
        out[name] = (out[name] * factor).astype(out[name].dtype)
    return out
```

```python
from contextlib import ExitStack

import numpy as np

import concourse.bass as bass
from concourse import mybir

F32 = mybir.dt.float32
U32 = mybir.dt.uint32
ALU = mybir.AluOpType
ACT = mybir.ActivationFunctionType
AX = mybir.AxisListType

P = 128
D = 1024
KT = D // P
DEPTH = 2
META = 16
SEQ = 256
TA = META + SEQ
EPS = 1e-6
NEG = -1e30
THETA = 10000.0
SLOT = 4160
NSLOT = 3
TT = [(0, META), (META, P), (META + P, P)]
HEADS = 8
LV = [64, 32, 16, 8, 4, 2, 1]
FF = 2816
EXPERTS = 8
NF = FF // P
CAP = 104
PASSES = -(-SEQ // CAP)
W2B = 384


def constants():
    f = np.float32
    cols, parts = {}, []

    def put(name, a):
        full = np.zeros((P, a.shape[1]), f)
        full[:a.shape[0]] = a
        at = sum(x.shape[1] for x in parts)
        cols[name] = (at, a.shape[1])
        parts.append(full)

    def rotation(n, half, lo):
        r = np.zeros((n, n), f)
        for base in range(lo, n, 2 * half):
            for i in range(half):
                r[base + half + i, base + i] = -1.0
                r[base + i, base + half + i] = 1.0
        return r

    def angles(half, n):
        inv = f(THETA) ** (-np.arange(half, dtype=f) / f(half))
        return np.arange(n, dtype=f)[None, :] * inv.astype(f)[:, None]

    i = np.arange(P)
    put("ident", np.eye(P, dtype=f))
    put("ones", np.ones((P, P), f))
    put("rot64", rotation(P, 32, 0))
    a64 = np.tile(angles(32, TA), (4, 1))
    put("cos64", np.cos(a64))
    put("sin64", np.sin(a64))
    shared = sum(x.shape[1] for x in parts)
    put("rotm", rotation(96, 16, 64))
    a32 = np.tile(angles(16, TA), (2, 1))
    put("cosm", np.concatenate([np.ones((64, TA), f), np.cos(a32)]))
    put("sinm", np.concatenate([np.zeros((64, TA), f), np.sin(a32)]))
    put("rot32", rotation(32, 16, 0))
    put("cos32", np.cos(a32))
    put("sin32", np.sin(a32))
    for name, window in (("causal", TA), ("band", P)):
        m = np.zeros((P, 0), f)
        for q0, nq in TT:
            rel = (q0 + i)[:, None] - np.arange(q0 + nq)[None, :]
            m = np.concatenate([m, np.where((rel >= 0) & (rel < window), 0, NEG).astype(f)], 1)
        put(name, m)
    first = sum(x.shape[1] for x in parts)
    put("blk64", np.kron(np.eye(2, dtype=f), np.ones((64, 64), f)))
    rel = np.arange(SEQ)[None, :] - i[:, None]
    put("segmask", np.where(rel >= 0, 0, NEG).astype(f))
    lg = np.log1p(-np.exp2(-5.0 - np.arange(4)))
    put("decay", np.concatenate([np.where(rel >= 0, np.exp(np.maximum(rel, 0) * g), 0) for g in lg], 1).astype(f))
    put("sel", np.kron(np.eye(4, dtype=f), np.ones((1, P), f)))
    put("selpair", np.kron(np.eye(4, dtype=f), np.ones((1, 64), f)))
    put("iota", np.tile(np.arange(1, CAP + 1, dtype=f), (P, 1)))
    put("first", np.tile(np.arange(8, 0, -1, dtype=f), (P, 1)))
    levels = [np.eye(P, dtype=f)]
    for s in LV:
        levels.append(((i[:, None] // (2 * s) == i[None, :] // (2 * s)) & (i[:, None] // s % 2 == 0)
                       & (i[None, :] // s % 2 == 1)).astype(f))
    put("levels", np.concatenate(levels, 1))
    return cols, np.concatenate(parts, 1), shared, first


def build(nc, a, consts, out, events, moe_on=True):
    ccols, _, c_shared, c_first = constants()
    with ExitStack() as ctx:
        new = {}

        mem = ctx.enter_context(nc.sbuf_tensor("mem", [P, nc.sbuf_bytes_remaining // 4 - 16], F32))
        limit = mem.shape[1]
        top = [0]

        def carve(*shape):
            n = int(np.prod(shape))
            v = mem[:, top[0]:top[0] + n]
            top[0] += n
            assert top[0] <= limit, (top[0], limit)
            if len(shape) == 2:
                v = v.rearrange("p (a b) -> p a b", a=shape[0])
            if len(shape) == 3:
                v = v.rearrange("p (a b c) -> p a b c", a=shape[0], b=shape[1])
            return v

        wring = [carve(SLOT) for _ in range(NSLOT)]
        x = carve(KT, TA)
        h = carve(KT, TA)
        sq = carve(KT, TA)
        rstd = carve(2, TA)
        eps = carve(1)
        cs = carve(c_shared)
        par = carve(80)
        tsc = carve(4, TA)
        asc = carve(4, TA)
        stat = carve(2, 16)
        mark = top[0]

        def const(name, parts=P):
            at, n = ccols[name]
            if at < c_shared:
                return cs[0:parts, at:at + n]
            if at < c_first:
                return cs1[0:parts, at - c_shared:at - c_shared + n]
            return cs2[0:parts, at - c_first:at - c_first + n]

        cs1 = carve(c_first - c_shared)
        gates = carve(24, TA)
        zs = carve(12, TA)
        after_z = top[0]
        qf, kf = carve(HEADS, TA), carve(HEADS, TA)
        qm, km = carve(HEADS, TA), carve(HEADS, TA)
        qw, kw = carve(HEADS, TA), carve(2, TA)
        vf, vm, vw = carve(3, 512), carve(3, 512), carve(3, P)
        cqkv = gates[:, 0:5, :]
        sm = [carve(432) for _ in range(2)]
        ptm = [carve(W2B) for _ in range(2)]
        ptx = [carve(TA) for _ in range(2)]
        end1 = top[0]
        top[0] = mark
        T = SEQ
        c_all = sum(n for _, n in ccols.values())
        gates2 = carve(32, T)
        zs2 = carve(8, T)
        ret_q, ret_k = carve(2, T), carve(2, T)
        lg = carve(T)
        assert top[0] <= after_z
        top[0] = after_z
        cs2 = carve(c_all - c_first)
        par2 = carve(620)
        upper = top[0]
        vtok = carve(4, 2, 256)
        xbc = carve(6, T + 3)
        mqk = carve(4, T + 3)
        conv = carve(10, T)
        squ = conv[:, 0:8, :]
        gla_q, gla_k = carve(T), carve(T)
        roots = mem[:, top[0]:top[0] + 7 * T].rearrange("p (a b) -> p a b", a=7)
        lx = [carve(T) for _ in range(2)]
        lq = [carve(T) for _ in range(2)]
        lk = [carve(T) for _ in range(2)]
        aw = [carve(W2B) for _ in range(2)]
        seg = [carve(W2B) for _ in range(2)]
        agla = carve(4, W2B)
        rowa, rowm, rowe, rowb = carve(T), carve(T), carve(T), carve(T)
        rows = carve(T)
        cols2 = carve(2, 68)
        o2 = sq[:, :, 0:T]
        ytok = sq.rearrange("p a b -> p (a b)")[:, 0:2 * D].rearrange("p (t d) -> p t d", t=2)
        x2, h2 = h[:, :, 0:T], x[:, :, 0:T]
        top[0] = mark
        mring = [carve(6144)]
        actb = carve(NF, T)
        assert top[0] <= after_z
        top[0] = upper
        mring += [carve(6144), carve(6144)]
        hid = [carve(T) for _ in range(4)]
        top[0] = mark + 6144
        act_e = carve(NF, CAP)
        htok = carve(2, D)
        assert top[0] <= after_z
        top[0] = 0
        ring4 = mring + [carve(6144)]
        pall = carve(EXPERTS + 1, 2, CAP)
        gall = carve(EXPERTS, 2, CAP)
        gt = carve(EXPERTS, T)
        route = carve(18, 16)
        assert top[0] <= NSLOT * SLOT
        top[0] = upper + 2 * 6144 + 4 * T
        he = carve(KT, CAP)
        ye = asc.rearrange("p a b -> p (a b)")[:, 0:D]
        passes = route[:, 17, 0:1].bitcast(mybir.dt.int32)

        banks = [ctx.enter_context(nc.psum_tensor(f"bank{i}", [P, 512], F32)) for i in range(8)]
        ACC = banks[0:2]
        SB = banks[2:4]
        TB = banks[4:6]
        XB = banks[6]
        OB = banks[7]

        sems, counts = {}, {}
        value_of = [None]

        def family(name):
            if name not in sems:
                sems[name] = ctx.enter_context(nc.semaphore(name))
                counts[name] = 0
            return sems[name]

        def sig(name, *key, by=1):
            s = family(name)
            counts[name] += by
            new[(name, *key)] = counts[name]
            value_of[0] = s, counts[name]
            return s, by

        def at(name, *key):
            return family(name), events.get((name, *key), 1)

        w_loaded = [family(f"w_loaded{i}") for i in range(NSLOT)]
        block = ctx.enter_context(nc.Block())

        unit = {}
        chunks_before_ffn = [0]
        chunks = []
        last_use = {}

        def full(eng, *name):
            n = unit[name]
            eng.wait_ge(*at(f"acc_full{n % 2}", *name))
            return ACC[n % 2]

        def free(*name):
            n = unit[name]
            s = family(f"acc_free{n % 2}")
            value_of[0] = s, n // 2 + 1
            return s, 1

        def evacuated(*name):
            n = unit[name]
            return family(f"acc_free{n % 2}"), n // 2 + 1

        class Steps:

            def __init__(self, eng, own):
                self.eng, self.own, self.last = eng, own, None

            def __call__(self, ins, signal=None):
                s, by = signal or sig(self.own)
                ins.then_inc(s, by)
                self.last = value_of[0]

            def settle(self):
                if self.last:
                    self.eng.wait_ge(*self.last)

        pcol, pcol2, param_dmas = {}, {}, []

        def pput(name, n):
            pcol[name] = sum(k for _, k in pcol.values()), n
            assert sum(pcol[name]) <= par.shape[1], pcol[name]

        def pc(name, i=0, parts=P, at_=0):
            c, par_ = (pcol1[name][0] + i, par1) if name in pcol1 else (pcol2[name][0] + i, par2)
            return par_[at_:at_ + parts, c:c + 1]

        def vec(name, src, n):
            pput(name, n)
            c = pcol[name][0]
            param_dmas.append((par[:, c:c + n], src.rearrange("(n p) -> p n", p=P)))

        def small(name, src, n, at_=0):
            pput(name, 1)
            c = pcol[name][0]
            param_dmas.append((par[at_:at_ + n, c:c + 1], src.rearrange("(p o) -> p o", o=1)))

        for l in range(DEPTH):
            vec(f"norm_g{l}", a["norm_g"][l], 8)
            vec(f"g_cq{l}", a["g_cq"][l], 3)
            vec(f"g_ckv{l}", a["g_ckv"][l], 2)
            small(f"b_f{l}", a["b_f"][l], 8)
            pput(f"sinks{l}", 8)
            c = pcol[f"sinks{l}"][0]
            param_dmas.append((par[:, c:c + 8], a["sinks"][l:l + 1].broadcast_to((P, 8))))
            pput(f"negsink{l}", 8)
        vec("final_g", a["final_g"], 8)

        n1, par1, pcol1 = len(param_dmas), par, pcol
        par, pcol = par2, pcol2
        for l in range(DEPTH):
            vec(f"mix_g{l}", a["mix_norm_g_2"][l], 8)
            for nm in ("ret", "ssd", "gla", "ml"):
                vec(f"{nm}_g{l}", a[f"{nm}_norm_g_2"][l], 2)
            for i in range(4):
                vec(f"ssd_w{l}{i}", a["ssd_conv_w_2"][l, i], 6)
                vec(f"ml_w{l}{i}", a["ml_conv_w_2"][l, i], 4)
            vec(f"ssd_b{l}", a["ssd_conv_b_2"][l], 6)
            vec(f"ml_b{l}", a["ml_conv_b_2"][l], 4)
            small(f"dt_bias{l}", a["ssd_dt_bias_2"][l], 4)
            small(f"a_log{l}", a["ssd_a_log_2"][l], 4)
            small(f"b_i{l}", a["ml_b_i_2"][l], 4)
            small(f"b_f2{l}", a["ml_b_f_2"][l], 4)
            small(f"b_alpha{l}", a["gla_b_alpha_2"][l], P)
            pput(f"d{l}", 2)
            c = pcol[f"d{l}"][0]
            for hd in range(4):
                param_dmas.append((par[64 * (hd % 2):64 * (hd % 2) + 64, c + hd // 2:c + hd // 2 + 1],
                                   a["ssd_d_2"][l:l + 1, hd:hd + 1].broadcast_to((64, 1))))
            pput(f"w_alpha{l}", P)
            c = pcol[f"w_alpha{l}"][0]
            param_dmas.append((par[0:16, c:c + P], a["gla_w_alpha_2"][l]))
            vec(f"ffn_g{l}", a["ffn_norm_g_2"][l], 8)
        vec("final_g2", a["final_norm_g_2"], 8)
        pput("router", 64)
        c = pcol["router"][0]
        for k in range(KT):
            param_dmas.append((par[:, c + 8 * k:c + 8 * k + 8], a["router_w_2"][0, k * P:(k + 1) * P, :]))

        def ropes(l):
            return [(("wq", l, j), P) for j in range(4)] + [(("wk", l), P)] + [(("mq", l, j), 96) for j in range(HEADS)]

        def ropes2(l):
            return [((nm, l, j), P) for nm in ("rq", "rk") for j in range(2)]

        R = [r for l in range(DEPTH) for r in ropes(l)] + [r for l in range(DEPTH) for r in ropes2(l)]
        rope_no = {name: i for i, (name, _) in enumerate(R)}

        GATES_LEVEL = (2, 2, 1, 1, 1, 1, 1, 1, 1)
        NORMS = [("blk64", (0,)), ("blk64", (1,)), ("ones", (2, 3)), ("blk64", (4,)), ("blk64", (5,)),
                 ("blk64", (6,)), ("blk64", (7,))]
        ORDER2 = (0, 1, 3, 2)

        def scores2(pe, l, i):
            g, m, hd = 12 * l + i, ORDER2[i // 4], i % 4
            if g >= 2:
                pe.wait_ge(*at("a_ready", g - 2))
            elif l == 0:
                pe.wait_ge(*at("y_ready", 12 * DEPTH - 1))
            lo = 64 * (hd % 2)
            k_, q_ = {0: (ret_k[lo:lo + 64, hd // 2, :], ret_q[lo:lo + 64, hd // 2, :]),
                      1: (conv[:, 2 + hd // 2, :], conv[:, 4 + hd // 2, :]),
                      3: (conv[lo:lo + 64, 8 + hd // 2, :], conv[lo:lo + 64, 6 + hd // 2, :])}[m]
            for c, j0, i0 in ((0, 0, 0), (256, P, P)):
                ins = pe.matmul(SB[g % 2][:, c:c + T - i0], k_[:, j0:j0 + P], q_[:, i0:T], start=True, stop=True)
            if m:
                row = (rowa, None, rowm)[m - 1]
                for c, i0 in ((0, 0), (256, P)):
                    ins = pe.matmul(TB[g % 2][:, c:c + T - i0], const("sel", 4)[:, hd * P:(hd + 1) * P],
                                    row[0:4, i0:T], start=True, stop=True)
            ins.then_inc(*sig("s2_full", g))

        def pv2(pe, l, i):
            m, hd = ORDER2[i // 4], i % 4
            g = 16 * l + i
            if m == 2:
                w = agla[:, hd, :]
            else:
                pe.wait_ge(*at("a_ready", 12 * l + i))
                w = aw[(12 * l + i) % 2]
            if hd % 2 == 0 and g >= 2:
                pe.wait_ge(*at("o2_read", g // 2 - 1))
            o0 = 64 * (hd % 2)
            for bank, lhs in ((OB, lambda t: vtok[:, m, t, 64 * hd:64 * hd + 64]), (XB, lambda t: const("ones")[:, 0:64])):
                if bank is OB or m == 3:
                    for t, c, i0 in ((0, 0, 0), (1, 256, P)):
                        ins = pe.matmul(bank[o0:o0 + 64, i0:T], lhs(t), w[:, c:c + T - i0],
                                        start=(t == 0), stop=(t == 1), skip_group_check=True)
            if hd % 2:
                if m == 3:
                    ins = pe.matmul(XB[:, 256:512], const("selpair", 4)[:, (hd // 2) * P:(hd // 2 + 1) * P],
                                    rowe[0:4, :], start=True, stop=True, skip_group_check=True)
                ins.then_inc(*sig("o2_full", g // 2))

        def levels2(pe, l, n):
            pe.wait_ge(*at("level_ready", l, n))
            if n:
                pe.wait_ge(*at("gla_picked", l, n - 1))
            else:
                pe.wait_ge(*at("a_ready", 12 * l + 11))
            for t in range(2 if n < 8 else 1):
                for hd in range(4):
                    k_, q_ = lk[n % 2][32 * hd:32 * hd + 32, :], lq[n % 2][32 * hd:32 * hd + 32, :]
                    q0 = t * P if n < 8 else P
                    ins = pe.matmul((*SB, *TB)[hd][:, t * P:(t + 1) * P], k_[:, t * P:(t + 1) * P], q_[:, q0:q0 + P],
                                    start=True, stop=True)
            ins.then_inc(*sig("level_full", l, n))

        YB = [*SB, *TB]
        UB = [(ACC[0], ACC[1]), (XB, OB)]
        STEPS = [(2 * c, 2) for c in range(10)] + [(20, 1), (21, 1)]

        def mlp(pe, l):
            def down(c):
                f0, nf = STEPS[c]
                w = mring[c % 3][:, 4096:4096 + nf * D].rearrange("p (k c) -> p k c", k=nf)
                pe.wait_ge(*at(f"mlp_w2_{c % 3}", c))
                for f in range(nf):
                    pe.wait_ge(*at("hidden", f0 + f))
                    for j in range(KT):
                        ins = pe.matmul(YB[j // 2][:, (j % 2) * T:(j % 2 + 1) * T], w[:, f, j * P:(j + 1) * P],
                                        actb[:, f0 + f, :], start=(f0 + f == 0 and j % 2 == 0),
                                        stop=(f0 + f == NF - 1), skip_group_check=True)
                ins.then_inc(*sig("mlp_down", c))
            for c, (f0, nf) in enumerate(STEPS):
                pe.wait_ge(*at(f"mlp_w13_{c % 3}", c))
                for f in range(nf):
                    F = f0 + f
                    if F >= 2:
                        pe.wait_ge(*at("hidden", F - 2))
                    for m in range(2):
                        w = mring[c % 3][:, 2048 * m:2048 * m + KT * nf * P].rearrange("p (k c) -> p k c", k=KT)
                        for k in range(KT):
                            if F == 0 and m == 0:
                                pe.wait_ge(*at("h_ready", ("ffn", l), k))
                            ins = pe.matmul(UB[F % 2][m][:, 0:T], w[:, k, f * P:(f + 1) * P], h2[:, k, :],
                                            start=(k == 0), stop=(k == KT - 1))
                        ins.then_inc(*sig(f"up{m}", F))
                if c:
                    down(c - 1)
            down(11)

        def transposes(pe, g):
            pe.wait_ge(*at("p_ready", g))
            if g >= 1:
                pe.wait_ge(*at("pt_dve", g - 1))
            if g >= 2:
                pe.wait_ge(*at("pt_act", g - 2))
            c = 0
            p = sm[g % 2]
            for qt, (q0, nq) in enumerate(TT):
                for kt in range(qt + 1):
                    k0, nk = TT[kt]
                    dst = (XB[0:nk, q0:q0 + nq], TB[g % 2][0:nk, q0 - META:q0 - META + nq],
                           TB[g % 2][0:nk, 256:384])[kt]
                    ins = pe.transpose(dst, p[0:nq, c + k0:c + k0 + nk], const("ident", nq)[:, 0:nq])
                c += q0 + nq
            ins.then_inc(*sig("pt_full", g))

        def pv(pe, g):
            kind, hd = g % 24 // 8, g % 8
            pe.wait_ge(*at("pt_act", g))
            pe.wait_ge(*at("pt_dve", g))
            if g % 2 == 0 and g >= 2:
                pe.wait_ge(*at("y_ready", g // 2 - 1))
            v, v0 = ((vf, 64 * hd), (vm, 64 * hd), (vw, 64 * (hd // 4)))[kind]
            o0 = 64 * (hd % 2)
            for nk, t, rhs, q0 in ((META, 0, ptx[g % 2][0:META, :], 0), (P, 1, ptm[g % 2][:, 0:256], META),
                                   (P, 2, ptm[g % 2][:, 256:384], META + P)):
                ins = pe.matmul(OB[o0:o0 + 64, q0:TA], v[0:nk, t, v0:v0 + 64], rhs,
                                start=(t == 0), stop=(t == 2), skip_group_check=True)
            if hd % 2:
                ins.then_inc(*sig("o_full", g // 2))

        F2 = NF
        BANKS2, SLOTS4 = 2, 4

        def turns(eng, prologue, body):
            eng.wait_ge(*at("passes_known"))
            n = eng.value_load(passes[0:1, :], min_val=1, max_val=PASSES)
            with eng.Fori(0, n) as p:
                if prologue:
                    prologue(p)
                with eng.Fori(0, EXPERTS) as e:
                    body(p * EXPERTS + e, e, p)
            return n

        def moe_pe(pe, gemm, open_group):
            for t in range(2):
                gemm(("logit", t), [(h2[:, k, t * P:(t + 1) * P], par2[:, pcol2["router"][0] + 8 * k:pcol2["router"][0] + 8 * k + 8])
                                    for k in range(KT)], lambda b: b[:, 0:8])
            pe.sem_inc(family("m_slot_free"), 1)
            for t in range(2):
                for c in range(2):
                    bank = open_group(("htok", t, c))
                    for k in range(4):
                        ins = pe.transpose(bank[:, k * P:(k + 1) * P], h2[:, 4 * c + k, t * P:(t + 1) * P], const("ident"))
                    ins.then_inc(*sig(f"acc_full{unit['htok', t, c] % 2}", "htok", t, c))
            pe.wait_ge(*at("chosen"))
            sel0, sel1, tri = route[:, 4, 0:8], route[:, 4, 8:16], gt[:, 0, 0:P]
            gemm(("place", 0), [(tri, sel0)], lambda b: b[:, 0:8])
            gemm(("place", 1), [(const("ones"), sel0), (tri, sel1)], lambda b: b[:, 0:8])
            gemm(("total",), [(const("ones"), sel0), (const("ones"), sel1)], lambda b: b[:, 0:8])
            pe.wait_ge(*evacuated("total"))
            pe.wait_ge(*evacuated("htok", 1, 1))

            def prologue(p):
                for e in range(EXPERTS):
                    pe.wait_ge(family("m_placed"), p * EXPERTS + e + 1)
                    if e == 0:
                        gather(0)
                    pe.wait_ge(family("m_gt"), p * EXPERTS + e + 1)
                    for t in range(2):
                        ins = pe.transpose((XB, OB)[e % 2][0:CAP, t * P:(t + 1) * P], gall[:, e, t, :], const("ident"))
                    ins.then_inc(family("m_gt_full"), 1)

            def gather(e):
                for k in range(KT):
                    for t in range(2):
                        ins = pe.matmul(TB[k // 4][:, (k % 4) * CAP:(k % 4 + 1) * CAP], htok[:, t, k * P:(k + 1) * P],
                                        pall[:, bass.ds(e, 1), t, :], start=(t == 0), stop=(t == 1))
                ins.then_inc(family("m_gathered"), 1)

            def body(it, e, p):
                pe.wait_ge(family("m_he"), it + p + 1)

                def down(c):
                    f0, nf = STEPS[c]
                    w = ring4[c % 4][:, 4096:4096 + nf * D].rearrange("p (k c) -> p k c", k=nf)
                    pe.wait_ge(family(f"m_w2_{c % 4}"), it * 48 + 16 * (c // 4 + 1))
                    pe.wait_ge(family("m_hidden"), it * F2 + f0 + nf + BANKS2)
                    if c == 0:
                        pe.wait_ge(family("m_ya"), it + 1)
                        pe.wait_ge(family("m_yd"), it + 1)
                    for f in range(nf):
                        for half in range(2):
                            ins = pe.matmul(SB[half][0:CAP, :], act_e[:, f0 + f, :], w[:, f, 512 * half:512 * half + 512],
                                            start=(f0 + f == 0), stop=(f0 + f == NF - 1))
                    ins.then_inc(family("m_slot_free"), 1)
                for c, (f0, nf) in enumerate(STEPS):
                    pe.wait_ge(family(f"m_w13_{c % 4}"), it * 96 + 32 * (c // 4 + 1))
                    for f in range(nf):
                        F = f0 + f
                        pe.wait_ge(family("m_hidden"), it * F2 + F + 1)
                        for m in range(2):
                            w = ring4[c % 4][:, 2048 * m:2048 * m + KT * nf * P].rearrange("p (k c) -> p k c", k=KT)
                            for k in range(KT):
                                ins = pe.matmul(ACC[F % 2][:, m * CAP:(m + 1) * CAP], w[:, k, f * P:(f + 1) * P],
                                                he[:, k, :], start=(k == 0), stop=(k == KT - 1))
                        ins.then_inc(family("m_up"), 1)
                    if c:
                        down(c - 1)
                down(11)
                gather(e + 1)
                pe.wait_ge(family("m_gt"), p * EXPERTS + EXPERTS + BANKS2)
                pe.wait_ge(family("m_ya"), it + 2)
                pe.wait_ge(family("m_yd"), it + 2)
                for r in range(4):
                    pe.wait_ge(family("m_added"), it * 4 + r + 1)
                    for j in range(2):
                        ins = pe.matmul((XB, OB)[r % 2][:, j * T:(j + 1) * T], ye[0:CAP, (2 * r + j) * P:(2 * r + j + 1) * P],
                                        gt[0:CAP, bass.ds(e, 1), :], start=True, stop=True)
                    ins.then_inc(family("m_scattered"), 1)
            turns(pe, prologue, body)

        def moe_sync(sp):
            def body(it, e, p):
                for c, (f0, nf) in enumerate(STEPS):
                    sp.wait_ge(family("m_slot_free"), it * 12 + c + 1)
                    lo, hi = f0 * P, (f0 + nf) * P
                    for m, w in enumerate((a["moe_w1_2"], a["moe_w3_2"])):
                        sp.dma_start(ring4[c % 4][:, 2048 * m:2048 * m + KT * nf * P].rearrange("p (k c) -> p k c", k=KT),
                                     w[0, bass.ds(e, 1), :, lo:hi].rearrange("e (k p) c -> p (e k) c", p=P))\
                            .then_inc(family(f"m_w13_{c % 4}"), 16)
                    sp.dma_start(ring4[c % 4][:, 4096:4096 + nf * D].rearrange("p (k c) -> p k c", k=nf),
                                 a["moe_w2_2"][0, bass.ds(e, 1), lo:hi, :].rearrange("e (k p) c -> p (e k) c", p=P))\
                        .then_inc(family(f"m_w2_{c % 4}"), 16)
            turns(sp, None, body)

        def moe_act(act):
            A, cp = nc.scalar.activation, nc.scalar.copy
            for t in range(2):
                for c in range(2):
                    b = full(act, "htok", t, c)
                    cp(htok[:, t, 512 * c:512 * c + 512], b[:, :]).then_inc(*free("htok", t, c))
            act.wait_ge(*at("top_diff"))
            A(route[:, 7, 0:2], route[:, 6, 0:2], ACT.Exp).then_inc(*sig("top_exp"))

            def prologue(p):
                for e in range(EXPERTS):
                    act.wait_ge(family("m_gt_full"), p * EXPERTS + e + 1)
                    cp(gt[0:CAP, e, :], (XB, OB)[e % 2][0:CAP, 0:T]).then_inc(family("m_gt"), 1)

            def body(it, e, p):
                for F in range(NF):
                    act.wait_ge(family("m_up"), it * F2 + F + 1)
                    A(hid[F % 2][:, 0:CAP], ACC[F % 2][:, 0:CAP], ACT.Tanh, scale=0.5).then_inc(family("m_tanh"), 1)
                act.wait_ge(family("m_slot_free"), it * 12 + 12 + SLOTS4)
                cp(ye[0:CAP, 0:512], SB[0][0:CAP, :]).then_inc(family("m_ya"), 1)
            turns(act, prologue, body)

        def moe_dve(dve, st):
            V = nc.vector
            S3, TS, TTn = V.scalar_tensor_tensor, V.tensor_scalar, V.tensor_tensor

            def both(i):
                return route[:, i, :].rearrange("p (t e) -> p t e", t=2)
            lt, eq, oh1, oh2, sel, gate, pos = both(0), both(1), both(2), both(3), both(4), both(5), both(8)
            m1, m2, dd, fm = route[:, 9, 0:2], route[:, 10, 0:2], route[:, 6, 0:2], route[:, 11, 0:2]

            def wide(v):
                return v.unsqueeze(2).broadcast_to((P, 2, 8))
            for t in range(2):
                b = full(dve, "logit", t)
                st(V.tensor_copy(lt[:, t, :], b[:, 0:8]), free("logit", t))

            def first_max(best, onehot):
                st.settle()
                st(V.tensor_reduce(best, lt, AX.X, ALU.max))
                st.settle()
                st(TTn(eq, lt, wide(best), ALU.is_equal))
                st.settle()
                for t in range(2):
                    st(TTn(eq[:, t, :], eq[:, t, :], const("first"), ALU.mult))
                st.settle()
                st(V.tensor_reduce(fm, eq, AX.X, ALU.max))
                st.settle()
                st(TTn(onehot, eq, wide(fm), ALU.is_equal))
                st.settle()
            first_max(m1, oh1)
            st(S3(out=lt, in0=oh1, scalar=NEG, in1=lt, op0=ALU.mult, op1=ALU.add))
            first_max(m2, oh2)
            st(TTn(dd, m2, m1, ALU.subtract), sig("top_diff"))
            st(TS(gt[:, 0, 0:P], const("segmask")[:, 0:P], 0.0, None, ALU.is_equal))
            st(TTn(sel, oh1, oh2, ALU.add), sig("chosen"))
            dve.wait_ge(*at("top_exp"))
            st(TS(route[:, 12, 0:2], route[:, 7, 0:2], 1.0, None, ALU.add))
            st.settle()
            st(V.reciprocal(route[:, 13, 0:2], route[:, 12, 0:2]))
            st.settle()
            st(TTn(route[:, 14, 0:2], route[:, 13, 0:2], route[:, 7, 0:2], ALU.mult))
            st.settle()
            st(TTn(gate, oh1, wide(route[:, 13, 0:2]), ALU.mult))
            st(TTn(eq, oh2, wide(route[:, 14, 0:2]), ALU.mult))
            st.settle()
            st(TTn(gate, gate, eq, ALU.add))
            for t in range(2):
                b = full(dve, "place", t)
                st(TTn(pos[:, t, :], sel[:, t, :], b[:, 0:8], ALU.mult), free("place", t))
            b = full(dve, "total")
            st(V.tensor_reduce(route[:, 15, 0:1], b[:, 0:8], AX.X, ALU.max), free("total"))
            st.settle()
            st(TS(route[:, 15, 1:2], route[:, 15, 0:1], CAP + 0.5, 1.0, ALU.is_gt, ALU.add))
            st(TS(route[:, 15, 2:3], route[:, 15, 0:1], 2 * CAP + 0.5, None, ALU.is_gt))
            st.settle()
            st(TTn(passes, route[:, 15, 1:2], route[:, 15, 2:3], ALU.add), sig("passes_known"))
            assert PASSES == 3
            for name, n in (("m_hidden", 2), ("m_added", 2), ("m_gt", 2), ("m_ya", 1), ("m_yd", 1)):
                st.settle()
                st(V.memset(route[:, 16, 0:1], 0.0))
                dve.sem_inc(family(name), n)

            st(V.memset(pall[:, EXPERTS, :, :], 0.0))

            def prologue(p):
                for e in range(EXPERTS):
                    for t in range(2):
                        st0 = TS(pall[:, e, t, :], const("iota"), pos[:, t, e:e + 1], None, ALU.is_equal)
                        st1 = TS(gall[:, e, t, :], const("iota"), pos[:, t, e:e + 1], gate[:, t, e:e + 1],
                                 ALU.is_equal, ALU.mult)
                    st1.then_inc(family("m_placed"), 1)
                dve.wait_ge(family("m_placed"), p * EXPERTS + EXPERTS)
                TS(pos, pos, -float(CAP), None, ALU.add).then_inc(family("m_moved"), 1)
                gathered(p * (EXPERTS + 1) + 1)

            def gathered(n):
                dve.wait_ge(family("m_gathered"), n)
                for c in range(2):
                    ins = V.tensor_copy(he[:, 4 * c:4 * c + 4, :], TB[c][:, 0:4 * CAP].rearrange("p (k c) -> p k c", k=4))
                ins.then_inc(family("m_he"), 1)

            def body(it, e, p):
                for F in range(NF):
                    dve.wait_ge(family("m_tanh"), it * F2 + F + 1)
                    S3(out=hid[2 + F % 2][:, 0:CAP], in0=hid[F % 2][:, 0:CAP], scalar=1.0, in1=ACC[F % 2][:, 0:CAP],
                       op0=ALU.add, op1=ALU.mult).then_inc(family("m_silu"), 1)
                    dve.wait_ge(family("m_silu"), it * F2 + F + 1)
                    S3(out=act_e[:, F, :], in0=hid[2 + F % 2][:, 0:CAP], scalar=0.5, in1=ACC[F % 2][:, CAP:2 * CAP],
                       op0=ALU.mult, op1=ALU.mult).then_inc(family("m_hidden"), 1)
                dve.wait_ge(family("m_slot_free"), it * 12 + 12 + SLOTS4)
                V.tensor_copy(ye[0:CAP, 512:1024], SB[1][0:CAP, :]).then_inc(family("m_yd"), 1)
                gathered(it + p + 2)
                for r in range(4):
                    dve.wait_ge(family("m_scattered"), it * 4 + r + 1)
                    v = x2[:, 2 * r:2 * r + 2, :]
                    TTn(v, (XB, OB)[r % 2][:, :].rearrange("p (j c) -> p j c", j=2), v, ALU.add)\
                        .then_inc(family("m_added"), 1)
            n = turns(dve, prologue, body)
            dve.wait_ge(family("m_added"), n * (EXPERTS * 4) + BANKS2)
            V.memset(route[:, 16, 1:2], 0.0).then_inc(*sig("moe_added"))

        fresh = []

        @block.tensor
        def _(pe):
            def open_group(name):
                n = unit[name] = len(unit)
                if n >= 2:
                    old = next(k for k, v in unit.items() if v == n - 2)
                    pe.wait_ge(*evacuated(*old))
                return ACC[n % 2]

            def gemm(name, mms, out, chunk=None):
                bank = open_group(name)
                key = fresh.pop() if fresh else None
                for i, (lhsT, rhs) in enumerate(mms):
                    if key is not None:
                        pe.wait_ge(*at("h_ready", key, i))
                    ins = pe.matmul(out(bank), lhsT, rhs, start=(i == 0), stop=(i == len(mms) - 1))
                ins.then_inc(*sig(f"acc_full{unit[name] % 2}", *name))
                if chunk is not None:
                    last_use[chunk] = (f"acc_full{unit[name] % 2}", *name)

            def chunk(pieces):
                n = len(chunks)
                chunks.append(pieces)
                pe.wait_ge(*at(f"w_loaded{n % NSLOT}", n))
                return n, [wring[n % NSLOT][:, o:o + k * c].rearrange("p (k c) -> p k c", k=k) for o, k, c, _ in pieces]

            def w_cols(w, l, lo, hi):
                return [(0, KT, hi - lo, w[l][:, lo:hi].rearrange("(k p) c -> p k c", p=P))]

            def feat(name, ch, w, c0, m, src, n, kt=KT):
                gemm(name, [(w[:, k, c0:c0 + m], src[:, k, 0:n]) for k in range(kt)], lambda b: b[0:m, 0:n], ch)

            pe.wait_ge(*at("tables"))
            pe.wait_ge(*at("x_loaded", 2))
            xs = gates.rearrange("p a b -> p (a b)")
            for j in range(KT):
                bank = open_group(("xt", j))
                for t, (t0, nt) in enumerate(TT):
                    ins = pe.transpose(bank[:, t0:t0 + nt], xs[0:nt, t * D + j * P:t * D + (j + 1) * P],
                                       const("ident", nt)[:, 0:nt])
                ins.then_inc(*sig(f"acc_full{j % 2}", "xt", j))

            def rope2(name):
                pe.wait_ge(*evacuated(*name))
                gemm(("rot", *name), [(const("rot64"), asc[:, rope_no[name] % 2, 0:T])], lambda b: b[:, 0:T])

            def sum_squares(name, key, n):
                bank = open_group(name)
                for k in range(KT):
                    pe.wait_ge(*at("squares", key, k))
                    ins = pe.matmul(bank[:, 0:n], const("ones"), sq[:, k, 0:n], start=(k == 0), stop=(k == KT - 1))
                ins.then_inc(*sig(f"acc_full{unit[name] % 2}", *name))
                fresh.append(key)

            for l in range(DEPTH):
                sum_squares(("ss", l), l, TA)
                win = a["w_in"]
                for nm, lo in (("fq", 0), ("fk", 512)):
                    ch, (w,) = chunk(w_cols(win, l, lo, lo + 512))
                    for j in range(4):
                        feat((nm, l, j), ch, w, j * P, P, h, TA)
                ch, (w,) = chunk(w_cols(win, l, 1024, 1536))
                for t, (t0, nt) in enumerate(TT):
                    gemm(("fv", l, t), [(h[:, k, t0:t0 + nt], w[:, k, :]) for k in range(KT)],
                         lambda b: b[0:nt, 0:512], ch)
                ch, (w,) = chunk(w_cols(win, l, 1536, 2056))
                feat(("ff", l), ch, w, 0, 8, h, TA)
                for j in range(4):
                    feat(("z", l, j), ch, w, 8 + j * P, P, h, TA)
                ch, (w,) = chunk(w_cols(win, l, 2056, 2440))
                for j in range(3):
                    feat(("cq", l, j), ch, w, j * P, P, h, TA)
                ch, (w,) = chunk(w_cols(win, l, 2440, 2728))
                for j in range(2):
                    feat(("cq", l, 3 + j), ch, w, j * P, P, h, TA)
                feat(("kr", l), ch, w, 256, 32, h, TA)
                ch, (w,) = chunk(w_cols(win, l, 2728, 3240))
                for j in range(4):
                    feat(("z", l, 4 + j), ch, w, j * P, P, h, TA)
                    if j == 1:
                        if l == 0:
                            pe.wait_ge(*at("tables1"))
                        pe.wait_ge(*evacuated("kr", l))
                        gemm(("krr", l), [(const("rot32", 32), asc[0:32, 3, :])], lambda b: b[0:32, 0:TA])
                        pe.wait_ge(*evacuated("cq", l, 4))
                        gemm(("sscq", l), [(const("ones"), sq[:, k, :]) for k in range(3)], lambda b: b[:, 0:TA])
                        gemm(("ssckv", l), [(const("ones"), sq[:, k, :]) for k in (3, 4)], lambda b: b[:, 0:TA])

                def rope_group(name, m, mat):
                    pe.wait_ge(*evacuated(*name))
                    gemm(("rot", *name), [(const(mat, m), asc[0:m, rope_no[name] % 2, :])], lambda b: b[0:m, 0:TA])

                ch, (w,) = chunk(w_cols(win, l, 3240, 3752))
                for j in range(4):
                    feat(("wq", l, j), ch, w, j * P, P, h, TA)
                    if j:
                        rope_group(("wq", l, j - 1), P, "rot64")
                ch, (w,) = chunk(w_cols(win, l, 3752, 4008))
                feat(("wk", l), ch, w, 0, P, h, TA)
                rope_group(("wq", l, 3), P, "rot64")
                for t, (t0, nt) in enumerate(TT):
                    gemm(("wv", l, t), [(h[:, k, t0:t0 + nt], w[:, k, P:2 * P]) for k in range(KT)],
                         lambda b: b[0:nt, 0:P], ch)
                rope_group(("wk", l), P, "rot64")
                ch, (w,) = chunk(w_cols(win, l, 4008, 4520))
                for j in range(4):
                    feat(("z", l, 8 + j), ch, w, j * P, P, h, TA)
                pe.wait_ge(*at("lowrank_ready", l))
                ch, (w,) = chunk([(0, 3, 768, a["w_uq"][l].rearrange("(k p) c -> p k c", p=P))])
                for j in range(HEADS):
                    feat(("mq", l, j), ch, w, j * 96, 96, cqkv, TA, kt=3)
                    if j:
                        rope_group(("mq", l, j - 1), 96, "rotm")
                ch, (w,) = chunk([(0, 2, 1024, a["w_ukv"][l].rearrange("(k p) c -> p k c", p=P))])
                for j in range(HEADS):
                    gemm(("mk", l, j), [(w[:, k, j * P:j * P + 64], cqkv[:, 3 + k, :]) for k in range(2)],
                         lambda b: b[0:64, 0:TA], ch)
                    if j == 0:
                        rope_group(("mq", l, 7), 96, "rotm")
                for t, (t0, nt) in enumerate(TT):
                    gemm(("mv", l, t), [(cqkv[:, 3 + k, t0:t0 + nt],
                                         w[:, k, :].rearrange("p (h c) -> p h c", h=HEADS)[:, :, 64:128])
                                        for k in range(2)],
                         lambda b: b[0:nt, 0:512].rearrange("p (h c) -> p h c", h=HEADS), ch)
                pe.wait_ge(*evacuated("mv", l, 2))
                pe.wait_ge(*at("rope_done", len(ropes(l)) * (l + 1) - 1))
                pe.wait_ge(*at("kr_spread", l))
                pe.wait_ge(*at("c_moved", l))
                for i in range(24):
                    g = 24 * l + i
                    kind, hd = i // 8, i % 8
                    q, kk, K = ((qf, kf, 65), (qm, km, 96), (qw, kw, 64))[kind]
                    kh = hd // 4 if kind == 2 else hd
                    if g >= 2:
                        pe.wait_ge(*at("s_masked", g - 2))
                    c = 0
                    for t0, nt in TT:
                        ins = pe.matmul(SB[g % 2][0:nt, c:c + t0 + nt], q[0:K, hd, t0:t0 + nt],
                                        kk[0:K, kh, 0:t0 + nt], start=True, stop=True)
                        c += t0 + nt
                    ins.then_inc(*sig("s_full", g))
                    if i > 0:
                        transposes(pe, g - 1)
                    if i % 4 == 0:
                        ch, (w,) = chunk(w_cols(win, l, 4520 + 128 * i, 4520 + 128 * i + 512))
                    feat(("g", l, i), ch, w, (i % 4) * P, P, h, TA)
                    if i > 0:
                        pv(pe, g - 1)
                transposes(pe, 24 * l + 23)
                pv(pe, 24 * l + 23)
                for n in range(3):
                    ch, (w,) = chunk([(0, 4, D, a["w_branch"][l, n].rearrange("(k p) c -> p k c", p=P))])
                    pe.wait_ge(*at("y_ready", 12 * l + 4 * n + 3))
                    for j in range(KT):
                        gemm(("br", l, n, j), [(w[:, k, j * P:(j + 1) * P], zs[:, 4 * n + k, :]) for k in range(4)],
                             lambda b: b[:, 0:TA], ch)
                pe.wait_ge(*at("merged_ready", l))
                for c in range(2):
                    ch, (w,) = chunk(w_cols(a["w_out"], l, 512 * c, 512 * c + 512))
                    for j in range(4):
                        feat(("wo", l, 4 * c + j), ch, w, j * P, P, sq, TA)
            sum_squares(("ss", DEPTH), DEPTH, TA)
            fresh.pop()

            def tok(name, ch, w, c0, m, src):
                for t in range(2):
                    gemm((*name, t), [(src[:, k, t * P:(t + 1) * P], w[:, k, c0:c0 + m]) for k in range(KT)],
                         lambda b: b[:, 0:m], ch)

            def norm2(key):
                sum_squares(("ss2", key), key, T)

            win = a["w_in_2"]
            for l in range(DEPTH):
                norm2(("mix", l))
                ch, (w,) = chunk(w_cols(win, l, 0, 512))
                for j, name in enumerate(("rq", l, i) for i in range(2)):
                    feat(name, ch, w, j * P, P, h2, T)
                for name, k in ((("rk", l, 0), 2), (("rk", l, 1), 3)):
                    rope2(("rq", l, k - 2))
                    feat(name, ch, w, k * P, P, h2, T)
                ch, (w,) = chunk(w_cols(win, l, 512, 1024))
                tok(("rv", l), ch, w, 0, 256, h2)
                rope2(("rk", l, 0))
                rope2(("rk", l, 1))
                for j in range(2):
                    feat(("gz", l, j), ch, w, 256 + j * P, P, h2, T)
                ch, (w,) = chunk(w_cols(win, l, 1024, 1536))
                for j in range(2):
                    feat(("gz", l, 2 + j), ch, w, j * P, P, h2, T)
                for j in range(2):
                    feat(("xbc", l, j), ch, w, 256 + j * P, P, h2, T)
                ch, (w,) = chunk(w_cols(win, l, 1536, 2052))
                for j in range(4):
                    feat(("xbc", l, 2 + j), ch, w, j * P, P, h2, T)
                feat(("sdt", l), ch, w, 512, 4, h2, T)
                ch, (w,) = chunk(w_cols(win, l, 3348, 3868))
                tok(("mv", l, 2), ch, w, 0, 256, h2)
                for j in range(2):
                    feat(("gz", l, 6 + j), ch, w, 256 + j * P, P, h2, T)
                feat(("mi", l), ch, w, 512, 4, h2, T)
                feat(("mf", l), ch, w, 516, 4, h2, T)
                ch, (w,) = chunk(w_cols(win, l, 2836, 3348))
                for j in range(4):
                    feat(("mqk", l, j), ch, w, j * P, P, h2, T)
                ch, (w,) = chunk(w_cols(win, l, 2564, 2836))
                for j in range(2):
                    feat(("gz", l, 4 + j), ch, w, j * P, P, h2, T)
                feat(("ga", l), ch, w, 256, 16, h2, T)
                ch, (w,) = chunk(w_cols(win, l, 2052, 2564))
                feat(("gq", l), ch, w, 0, P, h2, T)
                pe.wait_ge(*evacuated("ga", l))
                c = pcol2[f"w_alpha{l}"][0]
                gemm(("al", l), [(par2[0:16, c:c + P], rowa[0:16, :])], lambda b: b[:, 0:T])
                feat(("gk", l), ch, w, P, P, h2, T)
                tok(("gv", l), ch, w, 256, 256, h2)
                gate_no = [0]

                def gate_units(n):
                    for _ in range(n):
                        i = gate_no[0]
                        gate_no[0] += 1
                        if i % 4 == 0:
                            gate_chunk[:] = chunk(w_cols(win, l, 3868 + 128 * i, 3868 + 128 * i + 512))
                        feat(("g2", l, i), gate_chunk[0], gate_chunk[1][0], (i % 4) * P, P, h2, T)

                gate_chunk = []
                gate_units(2)
                pe.wait_ge(*at("rows_ready", l))
                bank = open_group(("rt", l))
                for t in range(2):
                    ins = pe.transpose(bank[:, 68 * t:68 * t + 68], rows[0:68, t * P:(t + 1) * P], const("ident", 68)[:, 0:68])
                ins.then_inc(*sig(f"acc_full{unit['rt', l] % 2}", "rt", l))
                pe.wait_ge(*at("conv_ready", l, 1))
                for t in range(2):
                    bank = open_group(("sxt", l, t))
                    for j in range(2):
                        ins = pe.transpose(bank[:, j * P:(j + 1) * P], conv[:, j, t * P:(t + 1) * P], const("ident"))
                    ins.then_inc(*sig(f"acc_full{unit['sxt', l, t] % 2}", "sxt", l, t))
                gate_units(1)
                pe.wait_ge(*at("conv_ready", l, 9))
                for i in range(12):
                    g = 12 * l + i
                    scores2(pe, l, i)
                    gate_units(1)
                    if i:
                        pv2(pe, l, i - 1)
                gate_units(1)
                pv2(pe, l, 11)
                for n in range(9):
                    levels2(pe, l, n)
                    gate_units(GATES_LEVEL[n])
                pe.wait_ge(*at("gla_picked", l, 8))
                for i in range(12, 16):
                    pv2(pe, l, i)
                gate_units(2)
                pe.wait_ge(*at("o_squares", l))
                for k, (mat, tiles) in enumerate(NORMS):
                    gemm(("ssm", l, k), [(const(mat), squ[:, t, :]) for t in tiles], lambda b: b[:, 0:T])
                gate_units(3)
                for n in range(0, 4, 2):
                    ch, ws = chunk([(2048 * m, 2, D, a["w_branch_2"][l, n + m].rearrange("(k p) c -> p k c", p=P))
                                    for m in range(2)])
                    for m in range(2):
                        pe.wait_ge(*at("y2_ready", l, n + m))
                        for j in range(KT):
                            gemm(("br2", l, n + m, j), [(ws[m][:, k, j * P:(j + 1) * P], zs2[:, 2 * (n + m) + k, :])
                                                        for k in range(2)], lambda b: b[:, 0:T], ch)
                pe.wait_ge(*at("merged_ready", DEPTH + l))
                for c in range(2):
                    ch, (w,) = chunk(w_cols(a["w_out_2"], l, 512 * c, 512 * c + 512))
                    for j in range(4):
                        feat(("wo2", l, 4 * c + j), ch, w, j * P, P, sq, T)
                if l and moe_on:
                    pe.sem_inc(family("m_slot_free"), 3)
                norm2(("ffn", l))
                if l == 0:
                    chunks_before_ffn[0] = len(chunks)
                    fresh.pop()
                    mlp(pe, l)
                elif moe_on:
                    moe_pe(pe, gemm, open_group)
            norm2(("final",))
            fresh.pop()
            pe.wait_ge(*at("y_normalised"))
            for t in range(2):
                for c in range(2):
                    bank = open_group(("yt", t, c))
                    for k in range(4):
                        ins = pe.transpose(bank[:, k * P:(k + 1) * P], h2[:, 4 * c + k, t * P:(t + 1) * P], const("ident"))
                    ins.then_inc(*sig(f"acc_full{unit['yt', t, c] % 2}", "yt", t, c))

        @block.sync
        def _(sp):
            def ring_chunk(n):
                if n >= NSLOT:
                    sp.wait_ge(*at(*last_use[n - NSLOT]))
                for o, k, c, src in chunks[n]:
                    sp.dma_start(wring[n % NSLOT][:, o:o + k * c].rearrange("p (k c) -> p k c", k=k), src)\
                        .then_inc(*sig(f"w_loaded{n % NSLOT}", n, by=16))

            def mlp_step(c):
                f0, nf = STEPS[c]
                if c >= 3:
                    sp.wait_ge(*at("mlp_down", c - 3))
                lo, hi = f0 * P, (f0 + nf) * P
                for m, w in enumerate((a["ffn_w1_2"], a["ffn_w3_2"])):
                    sp.dma_start(mring[c % 3][:, 2048 * m:2048 * m + KT * nf * P].rearrange("p (k c) -> p k c", k=KT),
                                 w[0][:, lo:hi].rearrange("(k p) c -> p k c", p=P)).then_inc(*sig(f"mlp_w13_{c % 3}", c, by=16))
                sp.dma_start(mring[c % 3][:, 4096:4096 + nf * D].rearrange("p (k c) -> p k c", k=nf),
                             a["ffn_w2_2"][0][lo:hi, :].rearrange("(k p) c -> p k c", p=P))\
                    .then_inc(*sig(f"mlp_w2_{c % 3}", c, by=16))

            xs = gates.rearrange("p a b -> p (a b)")
            sp.dma_start(xs[0:META, 0:D], a["meta_tokens"]).then_inc(*sig("x_loaded", 0, by=16))
            for t in range(2):
                sp.dma_start(xs[:, (t + 1) * D:(t + 2) * D], a["x"][0, t * P:(t + 1) * P, :])\
                    .then_inc(*sig("x_loaded", t + 1, by=16))
            sp.dma_start(cs, consts[:, 0:c_shared]).then_inc(*sig("tables", by=16))
            mid = chunks_before_ffn[0]
            for n in range(mid):
                ring_chunk(n)
            sp.wait_ge(*at("mix_done", 0))
            for c in range(3):
                mlp_step(c)
            for n in range(mid, mid + NSLOT):
                ring_chunk(n)
            for c in range(3, 12):
                mlp_step(c)
            for n in range(mid + NSLOT, len(chunks)):
                ring_chunk(n)
            if moe_on:
                moe_sync(sp)
            for t in range(2):
                for c in range(2):
                    sp.wait_ge(*evacuated("yt", t, c))
                    sp.dma_start(out[0, t * P:(t + 1) * P, 512 * c:512 * c + 512], ytok[:, t, 512 * c:512 * c + 512])\
                        .then_inc(*sig("out_stored", by=16))
            sp.wait_ge(*at("out_stored"))

        @block.gpsimd
        def _(pool):
            pl = Steps(pool, "pool_own")
            pl(pool.memset(eps[:, :], EPS))
            pl.settle()
            pl(pool.memset(stat[:, :, :], 0.0))
            pl.settle()
            pl(pool.memset(qf[64:65, :, :], 1.0), sig("memory_set"))
            for l in range(DEPTH):
                pool.wait_ge(*at("c_ready", l))
                for hd in range(HEADS):
                    pool.dma_start(kf[64:65, hd, :], tsc[hd:hd + 1, 3, :]).then_inc(*sig("c_moved", l, by=16))
                pool.wait_ge(*at("kr_ready", l))
                pool.tensor_copy(km[64:96, 1:8, :], km[64:96, 0:1, :].broadcast_to((32, 7, TA)))\
                    .then_inc(*sig("kr_spread", l))
            pool.wait_ge(*at("pt_act", 24 * DEPTH - 1))
            pool.wait_ge(*at("o_full", 12 * DEPTH - 1))
            pool.dma_start(cs2, consts[:, c_first:c_all]).then_inc(*sig("tables2", by=16))
            for i, (dst, src) in enumerate(param_dmas[n1:]):
                pool.dma_start(dst, src, allow_slow_non_contiguous=True).then_inc(*sig("params2", by=16))
            for v in (agla, xbc[:, :, 0:3], mqk[:, :, 0:3]):
                pl(pool.memset(v, 0.0))
                pl.settle()
            pool.wait_ge(*at("merged_ready", DEPTH - 1))
            pl(pool.memset(rows, 0.0), sig("memory_set2", 0))
            pool.wait_ge(*at("ffn_done"))
            for v in (agla, xbc[:, :, 0:3], mqk[:, :, 0:3], rows):
                pl(pool.memset(v, 0.0), sig("memory_set2", 1) if v is rows else None)
                pl.settle()

        @block.scalar
        def _(act):
            A, cp = nc.scalar.activation, nc.scalar.copy
            st = Steps(act, "act_own")
            for i, (dst, src) in enumerate(param_dmas[:n1]):
                act.dma_start(dst, src, allow_slow_non_contiguous=True).then_inc(*sig("params", i, by=16))
            act.dma_start(cs1, consts[:, c_shared:c_first]).then_inc(*sig("tables1", by=16))
            act.wait_ge(*at("memory_set"))

            def squares(key, src, n, ready, last=None):
                act.wait_ge(*(last or ready(0)))
                st(A(stat[0:1, 1, 14:15], eps[0:1, :], ACT.Sqrt))
                for k in range(KT):
                    act.wait_ge(*(ready(k)))
                    if k == 0:
                        act.wait_ge(*(last or ready(KT - 1)))
                    st(A(sq[:, k, 0:n], src[:, k, 0:n], ACT.Square), sig("squares", key, k))

            def root(name, slot, dim, n=TA):
                b = full(act, *name)
                st(A(rstd[:, slot, 0:n], b[:, 0:n], ACT.Sqrt, bias=eps[:, 0:1], scale=1.0 / dim), free(*name))

            for l in range(DEPTH):
                squares(l, x, TA, lambda k: evacuated("wo", l - 1, k) if l else evacuated("xt", k))
                root(("ss", l), 0, D)
                for nm, dst in (("fq", qf), ("fk", kf)):
                    for j in range(4):
                        b = full(act, nm, l, j)
                        st(cp(dst[0:64, 2 * j, :], b[0:64, 0:TA]))
                        st(cp(dst[0:64, 2 * j + 1, :], b[64:128, 0:TA]), free(nm, l, j))
                for t, (t0, nt) in enumerate(TT):
                    b = full(act, "fv", l, t)
                    st(cp(vf[0:nt, t, :], b[0:nt, 0:512]), free("fv", l, t))
                act.wait_ge(*evacuated("ff", l))
                st(A(asc[0:8, 0, :], tsc[0:8, 0, :], ACT.Abs))
                st.settle()
                st(A(asc[0:8, 1, :], asc[0:8, 0, :], ACT.Exp, scale=-1.0))
                st.settle()
                st(A(asc[0:8, 2, :], asc[0:8, 1, :], ACT.Ln, bias=1.0), sig("logf_ln", l))

                def z_tile(j):
                    b = full(act, "z", l, j)
                    st(A(zs[:, j, :], b[:, 0:TA], ACT.Tanh, scale=0.5), sig("z_tanh", l, j))
                for j in range(4):
                    z_tile(j)
                for j in range(5):
                    b = full(act, "cq", l, j)
                    st(cp(cqkv[:, j, :], b[:, 0:TA]))
                    st(A(sq[:, j, :], b[:, 0:TA], ACT.Square), free("cq", l, j))
                b = full(act, "kr", l)
                st(cp(asc[0:32, 3, :], b[0:32, 0:TA]), free("kr", l))
                z_tile(4)
                z_tile(5)
                root(("sscq", l), 0, 384)
                root(("ssckv", l), 1, 256)
                z_tile(6)
                z_tile(7)

                def rope_raw(name, m):
                    r = rope_no[name]
                    b = full(act, *name)
                    if r >= 2:
                        act.wait_ge(*at("rope_done", r - 2))
                    else:
                        act.wait_ge(*at("c_ready", 0))
                    st.settle()
                    st(cp(asc[0:m, r % 2, :], b[0:m, 0:TA]), free(*name))
                for j in range(4):
                    rope_raw(("wq", l, j), P)
                rope_raw(("wk", l), P)
                for t, (t0, nt) in enumerate(TT):
                    b = full(act, "wv", l, t)
                    st(cp(vw[0:nt, t, :], b[0:nt, 0:P]), free("wv", l, t))
                for j in range(8, 12):
                    z_tile(j)
                for j in range(HEADS):
                    rope_raw(("mq", l, j), 96)
                for j in range(HEADS):
                    b = full(act, "mk", l, j)
                    st(cp(km[0:64, j, :], b[0:64, 0:TA]), free("mk", l, j))
                for t, (t0, nt) in enumerate(TT):
                    b = full(act, "mv", l, t)
                    st(cp(vm[0:nt, t, :], b[0:nt, 0:512]), free("mv", l, t))

                def pt_copy(g):
                    act.wait_ge(*at("pt_full", g))
                    st(cp(ptm[g % 2][:, :], TB[g % 2][:, 0:W2B]), sig("pt_act", g))
                for i in range(24):
                    g = 24 * l + i
                    kind, hd = i // 8, i % 8
                    sc = (64 ** -0.5, 96 ** -0.5, 64 ** -0.5)[kind]
                    s_ = stat[:, g % 2, :]
                    act.wait_ge(*at("neg_max", g))
                    if kind == 2:
                        st(A(s_[:, 12:15], s_[:, 3:6], ACT.Exp, bias=pc(f"sinks{l}", hd)))
                    c = 0
                    for t, (t0, nt) in enumerate(TT):
                        n = t0 + nt
                        st(A(sm[g % 2][0:nt, c:c + n], sm[g % 2][0:nt, c:c + n], ACT.Exp, scale=sc,
                             bias=s_[0:nt, 3 + t:4 + t], accum_out=s_[0:nt, 6 + t:7 + t]),
                           sig("p_exp", g) if t == 2 else None)
                        c += n
                    if i:
                        pt_copy(g - 1)
                    b = full(act, "g", l, i)
                    st(A(gates[:, i, :], b[:, 0:TA], ACT.Tanh, scale=0.5), free("g", l, i))
                pt_copy(24 * l + 23)
            squares(DEPTH, x, TA, lambda k: evacuated("wo", DEPTH - 1, k))
            root(("ss", DEPTH), 0, D)

            act.wait_ge(*at("memory_set2", 0))
            for l in range(DEPTH):
                st(A(rstd[0:4, 1, 0:1], pc(f"a_log{l}", parts=4), ACT.Exp)) if False else None

            def norm2(key, ready, last=None):
                squares(key, x2, T, ready, last)
                root(("ss2", key), 0, D, T)

            def rope_raw2(name):
                r = rope_no[name]
                b = full(act, *name)
                act.wait_ge(*at("rope_done", r - 2))
                st.settle()
                st(cp(asc[:, r % 2, 0:T], b[:, 0:T]), free(*name))

            def gate2(l, j):
                b = full(act, "gz", l, j)
                st(A(zs2[:, j, :], b[:, 0:T], ACT.Tanh, scale=0.5), free("gz", l, j) if j >= 6 else sig("gz_tanh", l, j))

            def copy_unit(dst, name, part, scale=1.0):
                b = full(act, *name)
                st(A(dst, b[part, 0:dst.shape[-1]], ACT.Copy, scale=scale), free(*name))

            for l in range(DEPTH):
                norm2(("mix", l), lambda k: at("x2_ready", k) if l == 0 else at("mlp_added", 0, k))
                act.wait_ge(*at("memory_set2", l))
                act.wait_ge(*at("par2_ready"))
                for nm in ("rq", "rk"):
                    for j in range(2):
                        rope_raw2((nm, l, j))
                for t in range(2):
                    copy_unit(vtok[:, 0, t, :], ("rv", l, t), slice(0, P))
                for j in range(4):
                    gate2(l, j)
                for j in range(6):
                    copy_unit(xbc[:, j, 3:T + 3], ("xbc", l, j), slice(0, P))
                for t in range(2):
                    copy_unit(vtok[:, 3, t, :], ("mv", l, 2, t), slice(0, P))
                gate2(l, 6)
                gate2(l, 7)
                for j in range(4):
                    copy_unit(mqk[:, j, 3:T + 3], ("mqk", l, j), slice(0, P))
                gate2(l, 4)
                gate2(l, 5)
                copy_unit(rowa[0:16, :], ("ga", l), slice(0, 16))
                copy_unit(gla_q, ("gq", l), slice(0, P), scale=32 ** -0.5)
                copy_unit(gla_k, ("gk", l), slice(0, P))
                for t in range(2):
                    copy_unit(vtok[:, 2, t, :], ("gv", l, t), slice(0, P))
                gn = [0]

                def gate_tanh(n):
                    for _ in range(n):
                        i = gn[0]
                        gn[0] += 1
                        b = full(act, "g2", l, i)
                        st(A(gates2[:, i, :], b[:, 0:T], ACT.Tanh, scale=0.5), free("g2", l, i))
                act.wait_ge(*evacuated("mf", l))
                act.wait_ge(*evacuated("al", l))
                for src, dst, n in ((tsc[0:36, 0, 0:T], 0, 36), (lg, 1, P)):
                    st(A(asc[0:n, dst, 0:T], src, ACT.Abs))
                    st.settle()
                    st(A(asc[0:n, dst, 0:T], asc[0:n, dst, 0:T], ACT.Exp, scale=-1.0))
                st(A(stat[0:4, 1, 15:16], pc(f"a_log{l}", parts=4), ACT.Exp))
                st.settle()
                for dst, n in ((0, 36), (1, P)):
                    st(A(asc[0:n, dst, 0:T], asc[0:n, dst, 0:T], ACT.Ln, bias=1.0), sig("ln2", l, dst))
                gate_tanh(2)
                for j in range(10):
                    act.wait_ge(*at("conv_sum", l, j))
                    if j >= 2:
                        act.wait_ge(*at("conv_ready", l, j - 2))
                    st(A(asc[:, 2 + j % 2, 0:T], conv[:, j, :], ACT.Tanh, scale=0.5), sig("conv_tanh", l, j))
                act.wait_ge(*at("rows_ready", l))
                st(A(rowe[0:4, :], rowb[32:36, :], ACT.Exp, scale=-1.0), sig("rowe_ready", l))

                gate_tanh(1)
                for i in range(12):
                    g = 12 * l + i
                    if i >= 4:
                        act.wait_ge(*at("seg_arg", g))
                        st(A(seg[g % 2][:, :], seg[g % 2][:, :], ACT.Exp), sig("seg_exp", g))
                    gate_tanh(1)
                gate_tanh(1)
                for n in range(9):
                    if n < 8:
                        act.wait_ge(*at("level_arg", l, n + 1))
                        st(A(lx[(n + 1) % 2], lx[(n + 1) % 2], ACT.Exp), sig("level_exp", l, n + 1))
                    gate_tanh(GATES_LEVEL[n])
                act.wait_ge(*at("o2_done", l))
                st(A(squ, o2, ACT.Square), sig("o_squares", l))
                gate_tanh(2)
                for k in range(7):
                    name = ("ssm", l, k)
                    b = full(act, *name)
                    st(A(roots[:, k, :], b[:, 0:T], ACT.Sqrt, bias=eps[:, 0:1], scale=1.0 / (256 if k == 2 else 64)),
                       free(*name))
                gate_tanh(3)
                norm2(("ffn", l), lambda k: evacuated("wo2", l, k))
                if l == 0:
                    for F in range(NF):
                        act.wait_ge(*at("up0", F))
                        if F >= 2:
                            act.wait_ge(*at("hidden", F - 2))
                        else:
                            act.wait_ge(*at("h_ready", ("ffn", l), KT - 1))
                        st(A(hid[F % 2], UB[F % 2][0][:, 0:T], ACT.Tanh, scale=0.5), sig("up_tanh", F))
            if moe_on:
                moe_act(act)
            norm2(("final",), lambda k: at("moe_added"))
            for t in range(2):
                for c in range(2):
                    b = full(act, "yt", t, c)
                    cp(ytok[:, t, 512 * c:512 * c + 512], b[:, :]).then_inc(*free("yt", t, c))

        @block.vector
        def _(dve):
            V = nc.vector
            st = Steps(dve, "dve_own")
            dve.wait_ge(*at("memory_set"))
            for j in range(KT):
                b = full(dve, "xt", j)
                st(V.tensor_copy(x[:, j, :], b[:, 0:TA]), free("xt", j))
            dve.wait_ge(*at("params", n1 - 1))
            dve.wait_ge(*at("tables1"))
            for l in range(DEPTH):
                c = pcol1[f"negsink{l}"][0]
                st(V.tensor_scalar(par1[:, c:c + 8], par1[:, c - 8:c], -1.0, None, ALU.mult))

            def normalise(name, slot, gcol, src, dst, tiles, done, n=TA, d0=0):
                dve.wait_ge(*evacuated(*name))
                st.settle()
                st(V.reciprocal(rstd[:, slot, 0:n], rstd[:, slot, 0:n]))
                st.settle()
                for i, k in enumerate(tiles):
                    st(V.scalar_tensor_tensor(out=dst[:, k, 0:n - d0], in0=src[:, k, d0:n], scalar=pc(gcol, i),
                                              in1=rstd[:, slot, d0:n], op0=ALU.mult, op1=ALU.mult),
                       done(i) if done else None)

            def silu_tile(l, j):
                b = full(dve, "z", l, j)
                dve.wait_ge(*at("z_tanh", l, j))
                st(V.scalar_tensor_tensor(out=zs[:, j, :], in0=zs[:, j, :], scalar=1.0, in1=b[:, 0:TA],
                                          op0=ALU.add, op1=ALU.mult), free("z", l, j))

            for l in range(DEPTH):
                normalise(("ss", l), 0, f"norm_g{l}", x, h, range(KT), lambda k: sig("h_ready", l, k))
                b = full(dve, "ff", l)
                st.settle()
                if l:
                    dve.wait_ge(*at("c_moved", l - 1))
                st(V.tensor_scalar(tsc[0:8, 0, :], b[0:8, 0:TA], pc(f"b_f{l}", parts=8), None, ALU.add), free("ff", l))
                st.settle()
                st(V.tensor_scalar(tsc[0:8, 1, :], tsc[0:8, 0, :], 0.0, None, ALU.min))
                dve.wait_ge(*at("logf_ln", l))
                st.settle()
                st(V.tensor_tensor(tsc[0:8, 2, :], tsc[0:8, 1, :], asc[0:8, 2, :], ALU.subtract))
                st.settle()
                st(V.tensor_tensor_scan(tsc[0:8, 1, :], const("ones", 8)[:, 0:1].broadcast_to((8, TA)),
                                        tsc[0:8, 2, :], 0.0, ALU.mult, ALU.add))
                st.settle()
                st(V.tensor_scalar(tsc[0:8, 3, :], tsc[0:8, 1, :], -(64 ** 0.5), None, ALU.mult), sig("c_ready", l))
                for j in range(6):
                    silu_tile(l, j)

                def rope(name, m, cos, sin, mat_src, outs, done):
                    b = full(dve, *name)
                    st.settle()
                    st(V.tensor_tensor(tsc[0:m, 0, :], mat_src, cos, ALU.mult))
                    st(V.tensor_tensor(tsc[0:m, 1, :], b[0:m, 0:TA], sin, ALU.mult), free(*name))
                    st.settle()
                    for i, (dst, lo, hi) in enumerate(outs):
                        st(V.tensor_tensor(dst, tsc[lo:hi, 0, :], tsc[lo:hi, 1, :], ALU.add),
                           done() if i == len(outs) - 1 else None)

                rope(("krr", l), 32, const("cos32", 32), const("sin32", 32), asc[0:32, 3, :],
                     [(km[64:96, 0, :], 0, 32)], lambda: sig("kr_ready", l))
                normalise(("sscq", l), 0, f"g_cq{l}", cqkv, cqkv, range(3), None)
                normalise(("ssckv", l), 1, f"g_ckv{l}", cqkv, cqkv, (3, 4), lambda k: sig("lowrank_ready", l))
                silu_tile(l, 6)
                silu_tile(l, 7)
                for j in range(4):
                    r = rope_no["wq", l, j]
                    rope(("rot", "wq", l, j), P, const("cos64"), const("sin64"), asc[:, r % 2, :],
                         [(qw[0:64, 2 * j, :], 0, 64), (qw[0:64, 2 * j + 1, :], 64, 128)],
                         lambda: sig("rope_done", r))
                r = rope_no["wk", l]
                rope(("rot", "wk", l), P, const("cos64"), const("sin64"), asc[:, r % 2, :],
                     [(kw[0:64, 0, :], 0, 64), (kw[0:64, 1, :], 64, 128)], lambda: sig("rope_done", r))
                for j in range(8, 12):
                    silu_tile(l, j)
                for j in range(HEADS):
                    r = rope_no["mq", l, j]
                    rope(("rot", "mq", l, j), 96, const("cosm", 96), const("sinm", 96), asc[0:96, r % 2, :],
                         [(qm[0:96, j, :], 0, 96)], lambda: sig("rope_done", r))

                def pt_copy(g):
                    dve.wait_ge(*at("pt_full", g))
                    st(V.tensor_copy(ptx[g % 2][0:META, :], XB[0:META, 0:TA]), sig("pt_dve", g))

                def gated(pair):
                    dve.wait_ge(*at("o_full", pair))
                    j = pair % 12
                    st(V.scalar_tensor_tensor(out=zs[:, j, :], in0=OB[:, 0:TA], scalar=0.5, in1=zs[:, j, :],
                                              op0=ALU.mult, op1=ALU.mult), sig("y_ready", pair))
                for i in range(24):
                    g = 24 * l + i
                    kind, hd = i // 8, i % 8
                    sc = (64 ** -0.5, 96 ** -0.5, 64 ** -0.5)[kind]
                    s_ = stat[:, g % 2, :]
                    mask = const("band" if kind == 2 else "causal")
                    dve.wait_ge(*at("s_full", g))
                    if g >= 2:
                        dve.wait_ge(*at("pt_full", g - 2))
                        dve.wait_ge(*at("p_exp", g - 2))
                    c = 0
                    st.settle()
                    for t, (t0, nt) in enumerate(TT):
                        n = t0 + nt
                        st(V.tensor_tensor_reduce(out=sm[g % 2][0:nt, c:c + n], in0=SB[g % 2][0:nt, c:c + n],
                                                  in1=mask[0:nt, c:c + n], scale=1.0, scalar=-3e38, op0=ALU.add,
                                                  op1=ALU.max, accum_out=s_[0:nt, t:t + 1]),
                           sig("s_masked", g) if t == 2 else None)
                        c += n
                    st.settle()
                    if kind == 2:
                        st(V.tensor_scalar(s_[:, 3:6], s_[:, 0:3], -sc, pc(f"negsink{l}", hd), ALU.mult, ALU.min),
                           sig("neg_max", g))
                    else:
                        st(V.tensor_scalar(s_[:, 3:6], s_[:, 0:3], -sc, None, ALU.mult), sig("neg_max", g))
                    if i:
                        pt_copy(g - 1)
                    dve.wait_ge(*at("p_exp", g))
                    st.settle()
                    if kind == 2:
                        st(V.tensor_tensor(s_[:, 6:9], s_[:, 6:9], s_[:, 12:15], ALU.add))
                        st.settle()
                    st(V.reciprocal(s_[:, 9:12], s_[:, 6:9]))
                    st.settle()
                    c = 0
                    for t, (t0, nt) in enumerate(TT):
                        n = t0 + nt
                        st(V.tensor_scalar(sm[g % 2][0:nt, c:c + n], sm[g % 2][0:nt, c:c + n],
                                           s_[0:nt, 9 + t:10 + t], None, ALU.mult),
                           sig("p_ready", g) if t == 2 else None)
                        c += n
                    if i >= 2 and i % 2 == 0:
                        gated(g // 2 - 1)
                pt_copy(24 * l + 23)
                gated(12 * l + 11)
                for n in range(3):
                    for j in range(KT):
                        b = full(dve, "br", l, n, j)
                        if n == 0 and j == 0:
                            dve.wait_ge(*evacuated("g", l, 23))
                        st.settle()
                        dst = sq[:, j, :] if n == 0 else tsc[:, j % 4, :]
                        st(V.scalar_tensor_tensor(out=dst, in0=gates[:, n * 8 + j, :], scalar=1.0, in1=b[:, 0:TA],
                                                  op0=ALU.add, op1=ALU.mult), free("br", l, n, j))
                        if n:
                            st.settle()
                            st(V.tensor_tensor(sq[:, j, :], sq[:, j, :], dst, ALU.add),
                               sig("merged_ready", l) if n == 2 and j == 7 else None)
                for j in range(8):
                    b = full(dve, "wo", l, j)
                    st(V.scalar_tensor_tensor(out=x[:, j, :], in0=b[:, 0:TA], scalar=0.5, in1=x[:, j, :],
                                              op0=ALU.mult, op1=ALU.add), free("wo", l, j))
            normalise(("ss", DEPTH), 0, "final_g", x, h, range(KT), lambda k: sig("x2_ready", k), d0=META)

            S3, TS, TTn = V.scalar_tensor_tensor, V.tensor_scalar, V.tensor_tensor
            dve.wait_ge(*at("params2"))
            st.settle()
            for l in range(DEPTH):
                for nm, n in (("ret_g", 2), ("gla_g", 2), ("ml_g", 2), ("d", 2)):
                    c = pcol2[f"{nm}{l}"][0]
                    st(TS(par2[:, c:c + n], par2[:, c:c + n], 0.5, None, ALU.mult),
                       sig("par2_ready") if (l, nm) == (DEPTH - 1, "d") else None)

            def norm2(key, g, out_sig):
                name = ("ss2", key)
                dve.wait_ge(*evacuated(*name))
                st.settle()
                st(V.reciprocal(rstd[:, 0, 0:T], rstd[:, 0, 0:T]))
                st.settle()
                for k in range(KT):
                    st(S3(out=h2[:, k, :], in0=x2[:, k, :], scalar=pc(g, k), in1=rstd[:, 0, 0:T], op0=ALU.mult,
                          op1=ALU.mult), out_sig(k))

            def rope2(name, dst):
                b = full(dve, "rot", *name)
                st.settle()
                st(TTn(tsc[:, 2, 0:T], asc[:, rope_no[name] % 2, 0:T], const("cos64")[:, 0:T], ALU.mult))
                st(TTn(tsc[:, 3, 0:T], b[:, 0:T], const("sin64")[:, 0:T], ALU.mult), free("rot", *name))
                st.settle()
                st(TTn(dst, tsc[:, 2, 0:T], tsc[:, 3, 0:T], ALU.add), sig("rope_done", rope_no[name]))

            def gate2(l, j):
                b = full(dve, "gz", l, j)
                dve.wait_ge(*at("gz_tanh", l, j))
                st(S3(out=zs2[:, j, :], in0=zs2[:, j, :], scalar=1.0, in1=b[:, 0:T], op0=ALU.add, op1=ALU.mult),
                   free("gz", l, j))

            def conv_sum(l, j):
                src, nm, jj = (xbc[:, j, :], "ssd", j) if j < 6 else (mqk[:, j - 6, :], "ml", j - 6)
                dve.wait_ge(*(evacuated("xbc", l, j) if j < 6 else evacuated("mqk", l, jj)))
                st(TS(conv[:, j, :], src[:, 0:T], pc(f"{nm}_w{l}0", jj), pc(f"{nm}_b{l}", jj), ALU.mult, ALU.add))
                for i in range(1, 4):
                    st.settle()
                    st(S3(out=conv[:, j, :], in0=src[:, i:i + T], scalar=pc(f"{nm}_w{l}{i}", jj), in1=conv[:, j, :],
                          op0=ALU.mult, op1=ALU.add), sig("conv_sum", l, j) if i == 3 else None)

            def conv_silu(l, j):
                dve.wait_ge(*at("conv_tanh", l, j))
                st(S3(out=conv[:, j, :], in0=asc[:, 2 + j % 2, 0:T], scalar=1.0, in1=conv[:, j, :], op0=ALU.add,
                      op1=ALU.mult), sig("conv_ready", l, j))

            def scan(dst, src, op, n0, n1_):
                st(V.tensor_tensor_scan(dst, const("ones")[n0:n1_, 0:1].broadcast_to((n1_ - n0, T)), src, 0.0,
                                        ALU.mult, op))

            def pair_done(l, pair):
                m, p = ORDER2[pair // 2], pair % 2
                dve.wait_ge(*at("o2_full", 8 * l + pair))
                dst = o2[:, 2 * m + p, :]
                done = lambda: sig("o2_read", 8 * l + pair)
                if m in (0, 2):
                    st(V.tensor_copy(dst, OB[:, 0:T]), done())
                elif m == 1:
                    st(S3(out=tsc[:, 2, 0:T], in0=conv[:, p, :], scalar=pc(f"d{l}", p), in1=OB[:, 0:T], op0=ALU.mult,
                          op1=ALU.add))
                    st.settle()
                    st(S3(out=dst, in0=tsc[:, 2, 0:T], scalar=0.5, in1=zs2[:, 2 + p, :], op0=ALU.mult, op1=ALU.mult),
                       done())
                else:
                    st(TS(tsc[:, 2, 0:T], XB[:, 0:T], -1.0, None, ALU.mult))
                    st.settle()
                    st(TTn(tsc[:, 2, 0:T], tsc[:, 2, 0:T], XB[:, 0:T], ALU.max))
                    st.settle()
                    st(TTn(tsc[:, 2, 0:T], tsc[:, 2, 0:T], XB[:, 256:512], ALU.max))
                    st.settle()
                    st(V.reciprocal(tsc[:, 2, 0:T], tsc[:, 2, 0:T]))
                    st.settle()
                    st(TTn(dst, tsc[:, 2, 0:T], OB[:, 0:T], ALU.mult), done())

            for l in range(DEPTH):
                norm2(("mix", l), f"mix_g{l}", lambda k: sig("h_ready", ("mix", l), k))
                if l == 0:
                    dve.wait_ge(*at("tables2"))
                dve.wait_ge(*at("memory_set2", l))
                for j in range(2):
                    rope2(("rq", l, j), ret_q[:, j, :])
                for j in range(2):
                    rope2(("rk", l, j), ret_k[:, j, :])
                for j in range(4):
                    gate2(l, j)
                for j in range(6):
                    conv_sum(l, j)
                b = full(dve, "sdt", l)
                st(TS(tsc[0:4, 0, 0:T], b[0:4, 0:T], pc(f"dt_bias{l}", parts=4), None, ALU.add), free("sdt", l))
                b = full(dve, "mi", l)
                st(TS(tsc[32:36, 1, 0:T], b[0:4, 0:T], pc(f"b_i{l}", parts=4), None, ALU.add), free("mi", l))
                b = full(dve, "mf", l)
                st(TS(tsc[32:36, 0, 0:T], b[0:4, 0:T], pc(f"b_f2{l}", parts=4), None, ALU.add), free("mf", l))
                for j in range(6, 10):
                    conv_sum(l, j)
                gate2(l, 4)
                gate2(l, 5)
                b = full(dve, "al", l)
                st(TS(lg, b[:, 0:T], pc(f"b_alpha{l}"), None, ALU.add), free("al", l))
                dve.wait_ge(*at("ln2", l, 1))
                st.settle()
                st(TS(rowb[0:4, :], tsc[0:4, 0, 0:T], 0.0, None, ALU.max))
                st(TS(rowb[32:36, :], tsc[32:36, 0, 0:T], 0.0, None, ALU.min))
                st(TS(lx[0], lg, 0.0, None, ALU.min))
                st.settle()
                st(TTn(rows[64:68, :], rowb[0:4, :], asc[0:4, 0, 0:T], ALU.add))
                st(TTn(tsc[32:36, 2, 0:T], rowb[32:36, :], asc[32:36, 0, 0:T], ALU.subtract))
                st(TTn(lx[1], lx[0], asc[:, 1, 0:T], ALU.subtract))
                st.settle()
                st(TS(tsc[0:4, 3, 0:T], rows[64:68, :], stat[0:4, 1, 15:16], None, ALU.mult))
                st(TS(lx[0], lx[1], 1.0 / 16.0, None, ALU.mult))
                scan(rowb[32:36, :], tsc[32:36, 2, 0:T], ALU.add, 32, 36)
                st.settle()
                scan(rows[0:4, :], tsc[0:4, 3, 0:T], ALU.add, 0, 4)
                scan(lg, lx[0], ALU.add, 0, P)
                st(TTn(rows[32:36, :], tsc[32:36, 1, 0:T], rowb[32:36, :], ALU.subtract))
                st.settle()
                st(TS(rowa[0:4, :], rows[0:4, :], -1.0, None, ALU.mult))
                scan(tsc[32:36, 2, 0:T], rows[32:36, :], ALU.max, 32, 36)
                st.settle()
                st(TS(rowm[0:4, :], tsc[32:36, 2, 0:T], -1.0, None, ALU.mult))
                st(TTn(rowb[32:36, :], rowb[32:36, :], tsc[32:36, 2, 0:T], ALU.add), sig("rows_ready", l))
                for j in range(10):
                    conv_silu(l, j)
                b = full(dve, "rt", l)
                st(V.tensor_copy(cols2[:, :, :], b[:, 0:136].rearrange("p (t c) -> p t c", t=2)), free("rt", l))
                st.settle()
                for t in range(2):
                    b = full(dve, "sxt", l, t)
                    st(S3(out=vtok[:, 1, t, :].rearrange("p (h c) -> p h c", h=4),
                          in0=b[:, 0:256].rearrange("p (h c) -> p h c", h=4), scalar=0.5,
                          in1=cols2[:, t, 64:68].unsqueeze(2).broadcast_to((P, 4, 64)), op0=ALU.mult, op1=ALU.mult),
                       free("sxt", l, t))
                dve.wait_ge(*at("rowe_ready", l))
                for i in range(12):
                    g, m, hd = 12 * l + i, ORDER2[i // 4], i % 4
                    dve.wait_ge(*at("s2_full", g))
                    st.settle()
                    w = aw[g % 2]
                    if m == 0:
                        for c, n in ((0, T), (256, P)):
                            if c == 0 and g >= 2 and i >= 2:
                                pass
                            st(S3(out=w[:, c:c + n], in0=SB[g % 2][:, c:c + n], scalar=64 ** -0.5,
                                  in1=const("decay")[:, hd * T:hd * T + n], op0=ALU.mult, op1=ALU.mult),
                               sig("a_ready", g) if c else None)
                    else:
                        col = 0 if m == 1 else 32
                        for t, (c, n) in enumerate(((0, T), (256, P))):
                            st(S3(out=seg[g % 2][:, c:c + n], in0=TB[g % 2][:, c:c + n],
                                  scalar=cols2[:, t, col + hd:col + hd + 1], in1=const("segmask")[:, 0:n],
                                  op0=ALU.add, op1=ALU.add), sig("seg_arg", g) if c else None)
                        dve.wait_ge(*at("seg_exp", g))
                        st(S3(out=w[:, :], in0=SB[g % 2][:, 0:W2B], scalar=0.25 if m == 1 else 0.25 * 64 ** -0.5,
                              in1=seg[g % 2][:, :], op0=ALU.mult, op1=ALU.mult), sig("a_ready", g))
                    if i >= 3 and i % 2 == 1:
                        pair_done(l, i // 2 - 1)
                pair_done(l, 5)

                def level(n):
                    st.settle()
                    if n >= 2:
                        dve.wait_ge(*at("level_full", l, n - 2))
                    if n == 0:
                        st(V.tensor_copy(lq[0], gla_q))
                        st(V.tensor_copy(lk[0], gla_k), sig("level_ready", l, 0))
                        return
                    s_ = P >> (n - 1) if False else ([*LV, P])[n - 1]
                    g4 = lg.rearrange("p (n h s) -> p n h s", h=2, s=s_)
                    x4 = lx[n % 2].rearrange("p (n h s) -> p n h s", h=2, s=s_)
                    nb = T // (2 * s_)
                    mid = g4[:, :, 0, s_ - 1:s_].broadcast_to((P, nb, s_))
                    st(TTn(x4[:, :, 1, :], g4[:, :, 1, :], mid, ALU.subtract))
                    st(TTn(x4[:, :, 0, :], mid, g4[:, :, 0, :], ALU.subtract), sig("level_arg", l, n))
                    dve.wait_ge(*at("level_exp", l, n))
                    st(TTn(lq[n % 2], gla_q, lx[n % 2], ALU.mult))
                    st(TTn(lk[n % 2], gla_k, lx[n % 2], ALU.mult), sig("level_ready", l, n))

                def pick(n):
                    dve.wait_ge(*at("level_full", l, n))
                    for hd in range(4):
                        b = (*SB, *TB)[hd]
                        done = sig("gla_picked", l, n) if hd == 3 else None
                        if n == 8:
                            st(V.tensor_copy(agla[:, hd, P:T], b[:, 0:P]), done)
                        else:
                            w = agla[:, hd, :].rearrange("p (c k) -> p c k", c=3)[:, 0:3:2, :]
                            mk = const("levels")[:, n * P:(n + 1) * P].bitcast(U32)
                            st(V.copy_predicated(w, mk.unsqueeze(1).broadcast_to((P, 2, P)),
                                                 b[:, 0:T].rearrange("p (c k) -> p c k", c=2)), done)
                level(0)
                for n in range(9):
                    if n < 8:
                        level(n + 1)
                    pick(n)
                pair_done(l, 6)
                pair_done(l, 7)
                st.settle()
                st(V.tensor_copy(stat[0:1, 0, 14:15], stat[0:1, 0, 13:14]), sig("o2_done", l))
                for k in range(7):
                    dve.wait_ge(*evacuated("ssm", l, k))
                st(V.reciprocal(roots[:, :, :], roots[:, :, :]))
                st.settle()
                for m, (nm, k0) in enumerate((("ret", 0), ("ssd", 2), ("gla", 3), ("ml", 5))):
                    for p in range(2):
                        j = 2 * m + p
                        k = 2 if m == 1 else k0 + p
                        dst = zs2[:, j, :] if m == 1 else tsc[:, j % 4, 0:T]
                        st.settle()
                        st(S3(out=dst, in0=o2[:, j, :], scalar=pc(f"{nm}_g{l}", p), in1=roots[:, k, :], op0=ALU.mult,
                              op1=ALU.mult), sig("y2_ready", l, m) if m == 1 and p else None)
                        if m != 1:
                            st.settle()
                            st(S3(out=zs2[:, j, :], in0=zs2[:, j, :], scalar=1.0 if m == 3 else 0.0, in1=dst,
                                  op0=ALU.add, op1=ALU.mult), sig("y2_ready", l, m) if p else None)
                st.settle()
                for n in range(4):
                    for j in range(KT):
                        b = full(dve, "br2", l, n, j)
                        if n == 0 and j == 0:
                            dve.wait_ge(*evacuated("g2", l, 31))
                        st.settle()
                        dst = sq[:, j, 0:T] if n == 0 else tsc[:, j % 4, 0:T]
                        st(S3(out=dst, in0=gates2[:, n * 8 + j, :], scalar=1.0, in1=b[:, 0:T], op0=ALU.add,
                              op1=ALU.mult), free("br2", l, n, j))
                        if n:
                            st.settle()
                            st(TTn(sq[:, j, 0:T], sq[:, j, 0:T], dst, ALU.add),
                               sig("merged_ready", DEPTH + l) if n == 3 and j == 7 else None)
                st(V.tensor_copy(stat[0:1, 0, 14:15], stat[0:1, 0, 13:14]), sig("mix_done", l))
                for j in range(KT):
                    b = full(dve, "wo2", l, j)
                    st(S3(out=x2[:, j, :], in0=b[:, 0:T], scalar=0.5, in1=x2[:, j, :], op0=ALU.mult, op1=ALU.add),
                       free("wo2", l, j))
                norm2(("ffn", l), f"ffn_g{l}", lambda k: sig("h_ready", ("ffn", l), k))
                if l == 0:
                    for F in range(NF):
                        u1, u3 = (b_[:, 0:T] for b_ in UB[F % 2])
                        dve.wait_ge(*at("up_tanh", F))
                        st(S3(out=hid[2 + F % 2], in0=hid[F % 2], scalar=1.0, in1=u1, op0=ALU.add, op1=ALU.mult))
                        dve.wait_ge(*at("up1", F))
                        st.settle()
                        st(S3(out=actb[:, F, :], in0=hid[2 + F % 2], scalar=0.5, in1=u3, op0=ALU.mult, op1=ALU.mult),
                           sig("hidden", F))
                    dve.wait_ge(*at("mlp_down", 11))
                    st(V.tensor_copy(stat[0:1, 0, 14:15], stat[0:1, 0, 13:14]), sig("ffn_done"))
                    for j in range(KT):
                        st(TTn(x2[:, j, :], YB[j // 2][:, (j % 2) * T:(j % 2 + 1) * T], x2[:, j, :], ALU.add),
                           sig("mlp_added", 0, j))
                elif moe_on:
                    moe_dve(dve, st)
            norm2(("final",), "final_g2", lambda k: sig("y_normalised"))
        return new


def kernel(**inputs):
    import concourse.bacc as bacc
    from concourse.bass_utils import run_bass_kernel_spmd

    arrays = {name: np.ascontiguousarray(v) for name, v in inputs.items()}
    arrays["consts"] = constants()[1]
    events = {}
    for _ in range(2):
        nc = bacc.Bacc("TRN2", target_bir_lowering=False, num_devices=1)
        a = {name: nc.dram_tensor(f"in_{name}", v.shape, mybir.dt.from_np(v.dtype), kind="ExternalInput").ap()
             for name, v in arrays.items()}
        out = nc.dram_tensor("out_y", (1, SEQ, D), F32, kind="ExternalOutput").ap()
        events = build(nc, a, a["consts"], out, events)
    r = run_bass_kernel_spmd(nc, [{f"in_{name}": v for name, v in arrays.items()}], core_ids=[0])
    return r.results[0]["out_y"]
```

```python
from contextlib import ExitStack

import numpy as np

import concourse.bass as bass
from concourse import mybir

F32 = mybir.dt.float32
F32R = mybir.dt.float32r
U32 = mybir.dt.uint32
ALU = mybir.AluOpType
ACT = mybir.ActivationFunctionType
AX = mybir.AxisListType

P = 128
D = 1024
KT = D // P
DEPTH = 2
META = 16
SEQ = 256
TA = META + SEQ
EPS = 1e-6
NEG = -1e30
THETA = 10000.0
SLOT = 2080
NSLOT = 4
NHIGH = 2
AHEAD = NHIGH * 2
TT = [(0, META), (META, P), (META + P, P)]
HEADS = 8
LV = [64, 32, 16, 8, 4, 2, 1]
FF = 2816
EXPERTS = 8
NF = FF // P
CAP = 104
PASSES = -(-SEQ // CAP)
W2B = 384


def constants():
    f = np.float32
    cols, parts = {}, []

    def put(name, a):
        full = np.zeros((P, a.shape[1]), f)
        full[:a.shape[0]] = a
        at = sum(x.shape[1] for x in parts)
        cols[name] = (at, a.shape[1])
        parts.append(full)

    def rotation(n, half, lo):
        r = np.zeros((n, n), f)
        for base in range(lo, n, 2 * half):
            for i in range(half):
                r[base + half + i, base + i] = -1.0
                r[base + i, base + half + i] = 1.0
        return r

    def angles(half, n):
        inv = f(THETA) ** (-np.arange(half, dtype=f) / f(half))
        return np.arange(n, dtype=f)[None, :] * inv.astype(f)[:, None]

    i = np.arange(P)
    put("ident", np.eye(P, dtype=f))
    put("ones", np.ones((P, P), f))
    put("rot64", rotation(P, 32, 0))
    a64 = np.tile(angles(32, TA), (4, 1))
    put("cos64", np.cos(a64))
    put("sin64", np.sin(a64))
    shared = sum(x.shape[1] for x in parts)
    put("rotm", rotation(96, 16, 64))
    a32 = np.tile(angles(16, TA), (2, 1))
    put("cosm", np.concatenate([np.ones((64, TA), f), np.cos(a32)]))
    put("sinm", np.concatenate([np.zeros((64, TA), f), np.sin(a32)]))
    put("rot32", rotation(32, 16, 0))
    put("cos32", np.cos(a32))
    put("sin32", np.sin(a32))
    for name, window in (("causal", TA), ("band", P)):
        m = np.zeros((P, 0), f)
        for q0, nq in TT:
            rel = (q0 + i)[:, None] - np.arange(q0 + nq)[None, :]
            m = np.concatenate([m, np.where((rel >= 0) & (rel < window), 0, NEG).astype(f)], 1)
        put(name, m)
    first = sum(x.shape[1] for x in parts)
    put("blk64", np.kron(np.eye(2, dtype=f), np.ones((64, 64), f)))
    rel = np.arange(SEQ)[None, :] - i[:, None]
    put("segmask", np.where(rel >= 0, 0, NEG).astype(f))
    lg = np.log1p(-np.exp2(-5.0 - np.arange(4)))
    put("decay", np.concatenate([np.where(rel >= 0, np.exp(np.maximum(rel, 0) * g), 0) for g in lg], 1).astype(f))
    put("sel", np.kron(np.eye(4, dtype=f), np.ones((1, P), f)))
    put("selpair", np.kron(np.eye(4, dtype=f), np.ones((1, 64), f)))
    put("iota", np.tile(np.arange(1, CAP + 1, dtype=f), (P, 1)))
    put("first", np.tile(np.arange(8, 0, -1, dtype=f), (P, 1)))
    levels = [np.eye(P, dtype=f)]
    for s in LV:
        levels.append(((i[:, None] // (2 * s) == i[None, :] // (2 * s)) & (i[:, None] // s % 2 == 0)
                       & (i[None, :] // s % 2 == 1)).astype(f))
    put("levels", np.concatenate(levels, 1))
    return cols, np.concatenate(parts, 1), shared, first


def build(nc, a, consts, out, events):
    ccols, _, c_shared, c_first = constants()
    with ExitStack() as ctx:
        new = {}

        limit = nc.sbuf_bytes_remaining // 4 - 16
        n_low = (NSLOT + NHIGH) * SLOT + 2 * KT * TA
        with nc.sbuf_tensor("memr", [P, n_low], F32R) as memr:
            pass
        mem_low = ctx.enter_context(nc.sbuf_tensor("mem_low", [P, n_low], F32))
        mem_high = ctx.enter_context(nc.sbuf_tensor("mem_high", [P, limit - n_low], F32))
        top = [0]

        def shaped(v, shape):
            if len(shape) == 2:
                v = v.rearrange("p (a b) -> p a b", a=shape[0])
            if len(shape) == 3:
                v = v.rearrange("p (a b c) -> p a b c", a=shape[0], b=shape[1])
            return v

        def carve(*shape):
            n = int(np.prod(shape))
            top[0] += n
            first = top[0] - n
            assert top[0] <= limit and (first >= n_low or top[0] <= n_low), (first, n, limit)
            if first < n_low:
                return shaped(mem_low[:, first:top[0]], shape)
            return shaped(mem_high[:, first - n_low:top[0] - n_low], shape)

        def carve_both(*shape):
            v = carve(*shape)
            return v, shaped(memr[:, top[0] - int(np.prod(shape)):top[0]], shape)

        def high_places(*shape):
            _, v = carve_both(*shape)
            return v.bitcast(F32), v

        wring, wring_r = zip(*[carve_both(SLOT) for _ in range(NSLOT)])
        hring, hring_r = zip(*[high_places(SLOT) for _ in range(NHIGH)])
        ring_end = top[0]
        at_h = top[0]
        h, hl = carve_both(KT, TA)
        at_hh = top[0]
        hf, hh = high_places(KT, TA)
        assert top[0] == n_low
        x = carve(KT, TA)
        at_sq = top[0]
        sq = carve(KT, TA)
        rstd = carve(2, TA)
        eps = carve(1)
        cs = carve(c_shared)
        par = carve(80)
        tsc = carve(4, TA)
        asc = carve(4, TA)
        stat = carve(2, 16)
        mark = top[0]

        def const(name, parts=P):
            at, n = ccols[name]
            if at < c_shared:
                return cs[0:parts, at:at + n]
            if at < c_first:
                return cs1[0:parts, at - c_shared:at - c_shared + n]
            return cs2[0:parts, at - c_first:at - c_first + n]

        cs1 = carve(c_first - c_shared)
        gates = carve(24, TA)
        zs = carve(12, TA)
        after_z = top[0]
        qf, kf = carve(HEADS, TA), carve(HEADS, TA)
        qm, km = carve(HEADS, TA), carve(HEADS, TA)
        qw, kw = carve(HEADS, TA), carve(2, TA)
        vf, vm, vw = carve(3, 512), carve(3, 512), carve(3, P)
        cqkv = gates[:, 0:5, :]
        top[0] = at_sq
        sm = [carve(432) for _ in range(2)]
        ptm = [carve(W2B) for _ in range(2)]
        ptx = [carve(TA) for _ in range(2)]
        assert top[0] <= at_sq + KT * TA
        top[0] = mark
        T = SEQ
        c_all = sum(n for _, n in ccols.values())
        gates2 = carve(32, T)
        zs2 = carve(8, T)
        ret_q, ret_k = carve(2, T), carve(2, T)
        lg = carve(T)
        assert top[0] <= after_z
        top[0] = after_z
        cs2 = carve(c_all - c_first)
        par2 = carve(620)
        upper = top[0]
        vtok = carve(4, 2, 256)
        at_xbc = top[0]
        xbc = carve(6, T + 3)
        mqk = carve(4, T + 3)
        conv = carve(10, T)
        squ = conv[:, 0:8, :]
        gla_q, gla_k = carve(T), carve(T)
        aw = [carve(W2B) for _ in range(2)]
        seg = [carve(W2B) for _ in range(2)]
        agla = carve(4, W2B)
        rowa, rowm, rowe, rowb = carve(T), carve(T), carve(T), carve(T)
        rows = carve(T)
        cols2 = carve(2, 68)
        top[0] = at_xbc
        roots = carve(7, T)
        top[0] = at_xbc
        lx = [carve(T) for _ in range(2)]
        lq = [carve(T) for _ in range(2)]
        lk = [carve(T) for _ in range(2)]
        o2 = sq[:, :, 0:T]
        ytok = sq.rearrange("p a b -> p (a b)")[:, 0:2 * D].rearrange("p (t d) -> p t d", t=2)
        x2, h2 = x[:, :, META:TA], h[:, :, 0:T]
        top[0] = mark
        mring = [carve(6144)]
        actb = carve(NF, T)
        assert top[0] <= after_z
        top[0] = upper
        mring += [carve(6144), carve(6144)]
        hid = [tsc[:, i, 0:T] for i in range(4)]
        top[0] = at_hh
        he = carve(KT, CAP)
        act_f, act_h = high_places(4, CAP)
        act_l = high_places(4, CAP)[1]
        assert top[0] <= n_low
        top[0] = at_h
        w2_f, w2_h = high_places(2, D)
        top[0] = mark + 6144
        gall = carve(EXPERTS, 2, CAP)
        act_e = carve(2, CAP)
        htok = carve(2, D)
        assert top[0] <= after_z
        top[0] = 0
        ring4 = mring + [carve(6144)]
        pall = carve(EXPERTS + 1, 2, CAP)
        gt = carve(EXPERTS, T)
        route = carve(18, 16)
        w2_l = high_places(2, D)[1]
        assert top[0] <= ring_end
        ye = asc.rearrange("p a b -> p (a b)")[:, 0:D]
        passes = route[:, 17, 0:1].bitcast(mybir.dt.int32)

        banks = [ctx.enter_context(nc.psum_tensor(f"bank{i}", [P, 512], F32)) for i in range(8)]
        ACC = banks[0:2]
        SB = banks[2:4]
        TB = banks[4:6]
        XB = banks[6]
        OB = banks[7]

        sems, counts = {}, {}
        value_of = [None]

        def family(name):
            if name not in sems:
                sems[name] = ctx.enter_context(nc.semaphore(name))
                counts[name] = 0
            return sems[name]

        def sig(name, *key, by=1):
            s = family(name)
            counts[name] += by
            new[(name, *key)] = counts[name]
            value_of[0] = s, counts[name]
            return s, by

        def at(name, *key):
            return family(name), events.get((name, *key), 1)

        w_loaded = [family(f"w_loaded{i}") for i in range(NSLOT)]
        block = ctx.enter_context(nc.Block())

        unit = {}
        chunks_before_ffn = [0]
        chunks = []
        last_use = {}
        splits = []
        tiles = []
        tile_use = {}
        tile_of = {}
        phase_end = []

        def full(eng, *name):
            n = unit[name]
            eng.wait_ge(*at(f"acc_full{n % 2}", *name))
            return ACC[n % 2]

        def free(*name):
            n = unit[name]
            s = family(f"acc_free{n % 2}")
            value_of[0] = s, n // 2 + 1
            return s, 1

        def evacuated(*name):
            n = unit[name]
            return family(f"acc_free{n % 2}"), n // 2 + 1

        class Steps:

            def __init__(self, eng, own):
                self.eng, self.own, self.last = eng, own, None

            def __call__(self, ins, signal=None):
                s, by = signal or sig(self.own)
                ins.then_inc(s, by)
                self.last = value_of[0]

            def settle(self):
                if self.last:
                    self.eng.wait_ge(*self.last)

        pcol, pcol2, param_dmas = {}, {}, []

        def pput(name, n):
            pcol[name] = sum(k for _, k in pcol.values()), n
            assert sum(pcol[name]) <= par.shape[1], pcol[name]

        def pc(name, i=0, parts=P, at_=0):
            c, par_ = (pcol1[name][0] + i, par1) if name in pcol1 else (pcol2[name][0] + i, par2)
            return par_[at_:at_ + parts, c:c + 1]

        def vecs(names, src, n):
            for name in names:
                pput(name, n)
            c = pcol[names[0]][0]
            param_dmas.append((par[:, c:c + n * len(names)].rearrange("p (r n) -> p r n", n=n),
                               src.rearrange("r (n p) -> p r n", p=P)))

        def smalls(name, src, n):
            for l in range(DEPTH):
                pput(f"{name}{l}", 1)
            c = pcol[f"{name}0"][0]
            param_dmas.append((par[0:n, c:c + DEPTH], src.rearrange("l p -> p l")))

        def layers(name):
            return [f"{name}{l}" for l in range(DEPTH)]

        vecs(layers("norm_g"), a["norm_g"], 8)
        vecs(layers("g_cq"), a["g_cq"], 3)
        vecs(layers("g_ckv"), a["g_ckv"], 2)
        smalls("b_f", a["b_f"], 8)
        for l in range(DEPTH):
            pput(f"sinks{l}", 8)
            c = pcol[f"sinks{l}"][0]
            param_dmas.append((par[:, c:c + 8], a["sinks"][l:l + 1].broadcast_to((P, 8))))
            pput(f"negsink{l}", 8)
        vecs(["final_g"], a["final_g"].rearrange("(r d) -> r d", r=1), 8)

        n1, par1, pcol1 = len(param_dmas), par, pcol
        par, pcol = par2, pcol2
        vecs(layers("mix_g"), a["mix_norm_g_2"], 8)
        for nm in ("ret", "ssd", "gla", "ml"):
            vecs(layers(f"{nm}_g"), a[f"{nm}_norm_g_2"], 2)
        vecs([f"ssd_w{l}{i}" for l in range(DEPTH) for i in range(4)],
             a["ssd_conv_w_2"].rearrange("l i d -> (l i) d"), 6)
        vecs([f"ml_w{l}{i}" for l in range(DEPTH) for i in range(4)],
             a["ml_conv_w_2"].rearrange("l i d -> (l i) d"), 4)
        vecs(layers("ssd_b"), a["ssd_conv_b_2"], 6)
        vecs(layers("ml_b"), a["ml_conv_b_2"], 4)
        smalls("dt_bias", a["ssd_dt_bias_2"], 4)
        smalls("a_log", a["ssd_a_log_2"], 4)
        smalls("b_i", a["ml_b_i_2"], 4)
        smalls("b_f2", a["ml_b_f_2"], 4)
        smalls("b_alpha", a["gla_b_alpha_2"], P)
        for l in range(DEPTH):
            pput(f"d{l}", 2)
            c = pcol[f"d{l}"][0]
            for hd in range(4):
                param_dmas.append((par[64 * (hd % 2):64 * (hd % 2) + 64, c + hd // 2:c + hd // 2 + 1],
                                   a["ssd_d_2"][l:l + 1, hd:hd + 1].broadcast_to((64, 1))))
            pput(f"w_alpha{l}", P)
            c = pcol[f"w_alpha{l}"][0]
            param_dmas.append((par[0:16, c:c + P], a["gla_w_alpha_2"][l]))
        vecs(layers("ffn_g"), a["ffn_norm_g_2"], 8)
        vecs(["final_g2"], a["final_norm_g_2"].rearrange("(r d) -> r d", r=1), 8)
        pput("router", 64)
        c = pcol["router"][0]
        param_dmas.append((par[:, c:c + 64].rearrange("p (k c) -> p k c", k=KT),
                           a["router_w_2"][0].rearrange("(k p) c -> p k c", p=P)))

        def ropes(l):
            return [(("wq", l, j), P) for j in range(4)] + [(("wk", l), P)] + [(("mq", l, j), 96) for j in range(HEADS)]

        def ropes2(l):
            return [((nm, l, j), P) for nm in ("rq", "rk") for j in range(2)]

        R = [r for l in range(DEPTH) for r in ropes(l)] + [r for l in range(DEPTH) for r in ropes2(l)]
        rope_no = {name: i for i, (name, _) in enumerate(R)}

        GATES_BEFORE = (3, 2)
        GATES_LEVEL = (2, 1, 1, 1, 1, 1, 1, 1, 0)
        NORMS = [("blk64", (0,)), ("blk64", (1,)), ("ones", (2, 3)), ("blk64", (4,)), ("blk64", (5,)),
                 ("blk64", (6,)), ("blk64", (7,))]
        ORDER2 = (0, 1, 3, 2)

        def scores2(pe, l, i):
            g, m, hd = 12 * l + i, ORDER2[i // 4], i % 4
            if g >= 2:
                pe.wait_ge(*at("a_ready", g - 2))
            elif l == 0:
                pe.wait_ge(*at("y_ready", 12 * DEPTH - 1))
            lo = 64 * (hd % 2)
            k_, q_ = {0: (ret_k[lo:lo + 64, hd // 2, :], ret_q[lo:lo + 64, hd // 2, :]),
                      1: (conv[:, 2 + hd // 2, :], conv[:, 4 + hd // 2, :]),
                      3: (conv[lo:lo + 64, 8 + hd // 2, :], conv[lo:lo + 64, 6 + hd // 2, :])}[m]
            for c, j0, i0 in ((0, 0, 0), (256, P, P)):
                ins = pe.matmul(SB[g % 2][:, c:c + T - i0], k_[:, j0:j0 + P], q_[:, i0:T], start=True, stop=True)
            if m:
                row = (rowa, None, rowm)[m - 1]
                for c, i0 in ((0, 0), (256, P)):
                    ins = pe.matmul(TB[g % 2][:, c:c + T - i0], const("sel", 4)[:, hd * P:(hd + 1) * P],
                                    row[0:4, i0:T], start=True, stop=True)
            ins.then_inc(*sig("s2_full", g))

        def pv2(pe, l, i):
            m, hd = ORDER2[i // 4], i % 4
            g = 16 * l + i
            if m == 2:
                w = agla[:, hd, :]
            else:
                pe.wait_ge(*at("a_ready", 12 * l + i))
                w = aw[(12 * l + i) % 2]
            if hd % 2 == 0 and g >= 2:
                pe.wait_ge(*at("o2_read", g // 2 - 1))
            o0 = 64 * (hd % 2)
            for bank, lhs in ((OB, lambda t: vtok[:, m, t, 64 * hd:64 * hd + 64]), (XB, lambda t: const("ones")[:, 0:64])):
                if bank is OB or m == 3:
                    for t, c, i0 in ((0, 0, 0), (1, 256, P)):
                        ins = pe.matmul(bank[o0:o0 + 64, i0:T], lhs(t), w[:, c:c + T - i0],
                                        start=(t == 0), stop=(t == 1), skip_group_check=True)
            if hd % 2:
                if m == 3:
                    ins = pe.matmul(XB[:, 256:512], const("selpair", 4)[:, (hd // 2) * P:(hd // 2 + 1) * P],
                                    rowe[0:4, :], start=True, stop=True, skip_group_check=True)
                ins.then_inc(*sig("o2_full", g // 2))

        def levels2(pe, l, n):
            pe.wait_ge(*at("level_ready", l, n))
            if n:
                pe.wait_ge(*at("gla_picked", l, n - 1))
            else:
                pe.wait_ge(*at("a_ready", 12 * l + 11))
            for t in range(2 if n < 8 else 1):
                for hd in range(4):
                    k_, q_ = lk[n % 2][32 * hd:32 * hd + 32, :], lq[n % 2][32 * hd:32 * hd + 32, :]
                    q0 = t * P if n < 8 else P
                    ins = pe.matmul((*SB, *TB)[hd][:, t * P:(t + 1) * P], k_[:, t * P:(t + 1) * P], q_[:, q0:q0 + P],
                                    start=True, stop=True)
            ins.then_inc(*sig("level_full", l, n))

        YB = [*SB, *TB]
        UB = [(ACC[0], ACC[1]), (XB, OB)]
        STEPS = [(2 * c, 2) for c in range(10)] + [(20, 1), (21, 1)]

        def up_parts(F, m):
            c, (f0, nf) = next((c, s_) for c, s_ in enumerate(STEPS) if s_[0] <= F < s_[0] + s_[1])
            raw = mring[c % 3][:, 2048 * m:2048 * m + KT * nf * P].rearrange("p (k c) -> p k c", k=KT)
            rest = (v[:, KT * P * m:KT * P * (m + 1)].rearrange("p (k c) -> p k c", k=KT)
                    for v in (hring[F % NHIGH], hring_r[F % NHIGH], wring_r[F % NSLOT]))
            return c, raw[:, :, (F - f0) * P:(F - f0 + 1) * P], *rest

        def mlp(pe, l):
            def down(c):
                f0, nf = STEPS[c]
                w = mring[c % 3][:, 4096:4096 + nf * D].rearrange("p (k c) -> p k c", k=nf)
                pe.wait_ge(*at(f"mlp_w2_{c % 3}", c))
                for f in range(nf):
                    pe.wait_ge(*at("hidden", f0 + f))
                    for j in range(KT):
                        ins = pe.matmul(YB[j // 2][:, (j % 2) * T:(j % 2 + 1) * T], w[:, f, j * P:(j + 1) * P],
                                        actb[:, f0 + f, :], start=(f0 + f == 0 and j % 2 == 0),
                                        stop=(f0 + f == NF - 1), skip_group_check=True)
                ins.then_inc(*sig("mlp_down", c))
            for c, (f0, nf) in enumerate(STEPS):
                for f in range(nf):
                    F = f0 + f
                    if F >= 2:
                        pe.wait_ge(*at("hidden", F - 2))
                    pe.wait_ge(*at("up_split", F))
                    high, low = (v[:, 0:2 * KT * P].rearrange("p (m k c) -> p m k c", m=2, k=KT)
                                 for v in (hring_r[F % NHIGH], wring_r[F % NSLOT]))
                    for m in range(2):
                        kinds = ((high, hh, "h_high"), (high, hl, "h_ready"), (low, hh, None))
                        for k in range(KT):
                            for i, (w_, h_, event) in enumerate(kinds):
                                if F == 0 and m == 0 and event:
                                    pe.wait_ge(*at(event, ("ffn", l), k))
                                ins = pe.matmul(UB[F % 2][m][:, 0:T], w_[:, m, k, :], h_[:, k, 0:T],
                                                start=(k == 0 and i == 0), stop=(k == KT - 1 and i == 2))
                        ins.then_inc(*sig(f"up{m}", F))
                if c:
                    down(c - 1)
            down(11)

        def transposes(pe, g):
            pe.wait_ge(*at("p_ready", g))
            if g >= 1:
                pe.wait_ge(*at("pt_dve", g - 1))
            if g >= 2:
                pe.wait_ge(*at("pt_act", g - 2))
            c = 0
            p = sm[g % 2]
            for qt, (q0, nq) in enumerate(TT):
                for kt in range(qt + 1):
                    k0, nk = TT[kt]
                    dst = (XB[0:nk, q0:q0 + nq], TB[g % 2][0:nk, q0 - META:q0 - META + nq],
                           TB[g % 2][0:nk, 256:384])[kt]
                    ins = pe.transpose(dst, p[0:nq, c + k0:c + k0 + nk], const("ident", nq)[:, 0:nq])
                c += q0 + nq
            ins.then_inc(*sig("pt_full", g))

        def pv(pe, g):
            kind, hd = g % 24 // 8, g % 8
            pe.wait_ge(*at("pt_act", g))
            pe.wait_ge(*at("pt_dve", g))
            if g % 2 == 0 and g >= 2:
                pe.wait_ge(*at("y_ready", g // 2 - 1))
            v, v0 = ((vf, 64 * hd), (vm, 64 * hd), (vw, 64 * (hd // 4)))[kind]
            o0 = 64 * (hd % 2)
            for nk, t, rhs, q0 in ((META, 0, ptx[g % 2][0:META, :], 0), (P, 1, ptm[g % 2][:, 0:256], META),
                                   (P, 2, ptm[g % 2][:, 256:384], META + P)):
                ins = pe.matmul(OB[o0:o0 + 64, q0:TA], v[0:nk, t, v0:v0 + 64], rhs,
                                start=(t == 0), stop=(t == 2), skip_group_check=True)
            if hd % 2:
                ins.then_inc(*sig("o_full", g // 2))

        CREDITS, RING_SLOTS = 2, 4
        before_gates, after_gates = {}, {}

        def branch_slots(n):
            return range(4 * (n % 2), 4 * (n % 2) + 4)

        def merged_slot(j):
            return (j + 4) % KT

        def turns(eng, prologue, body):
            eng.wait_ge(*at("passes_known"))
            n = eng.value_load(passes[0:1, :], min_val=1, max_val=PASSES)
            with eng.Fori(0, n) as p:
                if prologue:
                    prologue(p)
                with eng.Fori(0, EXPERTS) as e:
                    body(p * EXPERTS + e, e, p)
            return n

        def moe_pe(pe, gemm, open_group):
            for t in range(2):
                gemm(("logit", t), [(h2[:, k, t * P:(t + 1) * P], par2[:, pcol2["router"][0] + 8 * k:pcol2["router"][0] + 8 * k + 8])
                                    for k in range(KT)], lambda b: b[:, 0:8])
            pe.sem_inc(family("m_slot_free"), 1)
            for t in range(2):
                for c in range(2):
                    bank = open_group(("htok", t, c))
                    for k in range(4):
                        ins = pe.transpose(bank[:, k * P:(k + 1) * P], h2[:, 4 * c + k, t * P:(t + 1) * P], const("ident"))
                    ins.then_inc(*sig(f"acc_full{unit['htok', t, c] % 2}", "htok", t, c))
            pe.wait_ge(*at("chosen"))
            sel0, sel1, tri = route[:, 4, 0:8], route[:, 4, 8:16], gt[:, 0, 0:P]
            gemm(("place", 0), [(tri, sel0)], lambda b: b[:, 0:8])
            gemm(("place", 1), [(const("ones"), sel0), (tri, sel1)], lambda b: b[:, 0:8])
            gemm(("total",), [(const("ones"), sel0), (const("ones"), sel1)], lambda b: b[:, 0:8])
            pe.wait_ge(*evacuated("total"))
            pe.wait_ge(*evacuated("htok", 1, 1))

            def prologue(p):
                for e in range(EXPERTS):
                    pe.wait_ge(family("m_placed"), p * EXPERTS + e + 1)
                    if e == 0:
                        gather(0)
                    pe.wait_ge(family("m_gt"), p * EXPERTS + e + 1)
                    for t in range(2):
                        ins = pe.transpose((XB, OB)[e % 2][0:CAP, t * P:(t + 1) * P], gall[:, e, t, :], const("ident"))
                    ins.then_inc(family("m_gt_full"), 1)

            def gather(e):
                for k in range(KT):
                    for t in range(2):
                        ins = pe.matmul(TB[k // 4][:, (k % 4) * CAP:(k % 4 + 1) * CAP], htok[:, t, k * P:(k + 1) * P],
                                        pall[:, bass.ds(e, 1), t, :], start=(t == 0), stop=(t == 1))
                ins.then_inc(family("m_gathered"), 1)

            def body(it, e, p):
                pe.wait_ge(family("m_he"), it + p + 1)

                def down(c):
                    f0, nf = STEPS[c]
                    pe.wait_ge(family("m_w2_split"), it * NF + f0 + nf)
                    pe.wait_ge(family("m_hidden"), it * NF + f0 + nf + CREDITS)
                    if c == 0:
                        pe.wait_ge(family("m_ya"), it + 1)
                        pe.wait_ge(family("m_yd"), it + 1)
                    for f in range(nf):
                        F = f0 + f
                        for half in range(2):
                            for i, (a_, w_) in enumerate(((act_h, w2_h), (act_h, w2_l), (act_l, w2_h))):
                                ins = pe.matmul(SB[half][0:CAP, :], a_[:, F % 4, :],
                                                w_[:, F % 2, 512 * half:512 * half + 512],
                                                start=(F == 0 and i == 0), stop=(F == NF - 1 and i == 2))
                    ins.then_inc(family("m_slot_free"), 1)
                for c, (f0, nf) in enumerate(STEPS):
                    pe.wait_ge(family(f"m_w13_{c % 4}"), it * 96 + 32 * (c // 4 + 1))
                    for f in range(nf):
                        F = f0 + f
                        pe.wait_ge(family("m_hidden"), it * NF + F + 1)
                        for m in range(2):
                            w = ring4[c % 4][:, 2048 * m:2048 * m + KT * nf * P].rearrange("p (k c) -> p k c", k=KT)
                            for k in range(KT):
                                ins = pe.matmul(ACC[F % 2][:, m * CAP:(m + 1) * CAP], w[:, k, f * P:(f + 1) * P],
                                                he[:, k, :], start=(k == 0), stop=(k == KT - 1))
                        ins.then_inc(family("m_up"), 1)
                    if c:
                        down(c - 1)
                down(11)
                gather(e + 1)
                pe.wait_ge(family("m_gt"), p * EXPERTS + EXPERTS + CREDITS)
                pe.wait_ge(family("m_ya"), it + 2)
                pe.wait_ge(family("m_yd"), it + 2)
                for r in range(4):
                    pe.wait_ge(family("m_added"), it * 4 + r + 1)
                    for j in range(2):
                        ins = pe.matmul((XB, OB)[r % 2][:, j * T:(j + 1) * T], ye[0:CAP, (2 * r + j) * P:(2 * r + j + 1) * P],
                                        gt[0:CAP, bass.ds(e, 1), :], start=True, stop=True)
                    ins.then_inc(family("m_scattered"), 1)
            turns(pe, prologue, body)

        SPLIT_BEHIND = [*((2 * c, 2 * c + 1) for c in range(10)), (20, 21), ()]

        def step_of(F):
            return F // 2 if F < 20 else F - 10

        def w2_free(it, F):
            done = it * 12 + step_of(F - 2) + 1 if F >= 2 else (it - 1) * 12 + step_of(NF - 2 + F) + 1
            return family("m_slot_free"), done + RING_SLOTS

        def w2_raw(F):
            c = step_of(F)
            at_ = 4096 + (F - STEPS[c][0]) * D
            return ring4[c % 4][:, at_:at_ + D]

        def moe_sync(sp):
            def body(it, e, p):
                for c, (f0, nf) in enumerate(STEPS):
                    sp.wait_ge(family("m_slot_free"), it * 12 + c + 1)
                    lo, hi = f0 * P, (f0 + nf) * P
                    for m, w in enumerate((a["moe_w1_2"], a["moe_w3_2"])):
                        sp.dma_start(ring4[c % 4][:, 2048 * m:2048 * m + KT * nf * P].rearrange("p (k c) -> p k c", k=KT),
                                     w[0, bass.ds(e, 1), :, lo:hi].rearrange("e (k p) c -> p (e k) c", p=P))\
                            .then_inc(family(f"m_w13_{c % 4}"), 16)
                    sp.dma_start(ring4[c % 4][:, 4096:4096 + nf * D].rearrange("p (k c) -> p k c", k=nf),
                                 a["moe_w2_2"][0, bass.ds(e, 1), lo:hi, :].rearrange("e (k p) c -> p (e k) c", p=P))\
                        .then_inc(family(f"m_w2_{c % 4}"), 16)
            turns(sp, None, body)

        def moe_act(act):
            A, cp = nc.scalar.activation, nc.scalar.copy
            for t in range(2):
                for c in range(2):
                    b = full(act, "htok", t, c)
                    cp(htok[:, t, 512 * c:512 * c + 512], b[:, :]).then_inc(*free("htok", t, c))
            act.wait_ge(*at("top_diff"))
            A(route[:, 7, 0:2], route[:, 6, 0:2], ACT.Exp).then_inc(*sig("top_exp"))

            def prologue(p):
                for e in range(EXPERTS):
                    act.wait_ge(family("m_gt_full"), p * EXPERTS + e + 1)
                    cp(gt[0:CAP, e, :], (XB, OB)[e % 2][0:CAP, 0:T]).then_inc(family("m_gt"), 1)

            def body(it, e, p):
                for c, (f0, nf) in enumerate(STEPS):
                    for F in range(f0, f0 + nf):
                        act.wait_ge(family("m_up"), it * NF + F + 1)
                        A(hid[F % 2][:, 0:CAP], ACC[F % 2][:, 0:CAP], ACT.Tanh, scale=0.5).then_inc(family("m_tanh"), 1)
                    for F in SPLIT_BEHIND[c]:
                        act.wait_ge(*w2_free(it, F))
                        act.wait_ge(family(f"m_w2_{step_of(F) % 4}"), it * 48 + 16 * (step_of(F) // 4 + 1))
                        cp(w2_h[:, F % 2, :], w2_raw(F)).then_inc(family("m_w2_high"), 1)
                act.wait_ge(family("m_slot_free"), it * 12 + 12 + RING_SLOTS)
                cp(ye[0:CAP, 0:512], SB[0][0:CAP, :]).then_inc(family("m_ya"), 1)
            turns(act, prologue, body)

        def moe_dve(dve, st):
            V = nc.vector
            S3, TS, TTn = V.scalar_tensor_tensor, V.tensor_scalar, V.tensor_tensor

            def both(i):
                return route[:, i, :].rearrange("p (t e) -> p t e", t=2)
            lt, eq, oh1, oh2, sel, gate, pos = both(0), both(1), both(2), both(3), both(4), both(5), both(8)
            m1, m2, dd, fm = route[:, 9, 0:2], route[:, 10, 0:2], route[:, 6, 0:2], route[:, 11, 0:2]

            def wide(v):
                return v.unsqueeze(2).broadcast_to((P, 2, 8))
            for t in range(2):
                b = full(dve, "logit", t)
                st(V.tensor_copy(lt[:, t, :], b[:, 0:8]), free("logit", t))

            def first_max(best, onehot):
                st.settle()
                st(V.tensor_reduce(best, lt, AX.X, ALU.max))
                st.settle()
                st(TTn(eq, lt, wide(best), ALU.is_equal))
                st.settle()
                for t in range(2):
                    st(TTn(eq[:, t, :], eq[:, t, :], const("first"), ALU.mult))
                st.settle()
                st(V.tensor_reduce(fm, eq, AX.X, ALU.max))
                st.settle()
                st(TTn(onehot, eq, wide(fm), ALU.is_equal))
                st.settle()
            first_max(m1, oh1)
            st(S3(out=lt, in0=oh1, scalar=NEG, in1=lt, op0=ALU.mult, op1=ALU.add))
            first_max(m2, oh2)
            st(TTn(dd, m2, m1, ALU.subtract), sig("top_diff"))
            st(TS(gt[:, 0, 0:P], const("segmask")[:, 0:P], 0.0, None, ALU.is_equal))
            st(TTn(sel, oh1, oh2, ALU.add), sig("chosen"))
            dve.wait_ge(*at("top_exp"))
            st(TS(route[:, 12, 0:2], route[:, 7, 0:2], 1.0, None, ALU.add))
            st.settle()
            st(V.reciprocal(route[:, 13, 0:2], route[:, 12, 0:2]))
            st.settle()
            st(TTn(route[:, 14, 0:2], route[:, 13, 0:2], route[:, 7, 0:2], ALU.mult))
            st.settle()
            st(TTn(gate, oh1, wide(route[:, 13, 0:2]), ALU.mult))
            st(TTn(eq, oh2, wide(route[:, 14, 0:2]), ALU.mult))
            st.settle()
            st(TTn(gate, gate, eq, ALU.add))
            for t in range(2):
                b = full(dve, "place", t)
                st(TTn(pos[:, t, :], sel[:, t, :], b[:, 0:8], ALU.mult), free("place", t))
            b = full(dve, "total")
            st(V.tensor_reduce(route[:, 15, 0:1], b[:, 0:8], AX.X, ALU.max), free("total"))
            st.settle()
            st(TS(route[:, 15, 1:2], route[:, 15, 0:1], CAP + 0.5, 1.0, ALU.is_gt, ALU.add))
            st(TS(route[:, 15, 2:3], route[:, 15, 0:1], 2 * CAP + 0.5, None, ALU.is_gt))
            st.settle()
            st(TTn(passes, route[:, 15, 1:2], route[:, 15, 2:3], ALU.add), sig("passes_known"))
            assert PASSES == 3
            for name, n in (("m_hidden", 2), ("m_added", 2), ("m_gt", 2), ("m_ya", 1), ("m_yd", 1)):
                st.settle()
                st(V.memset(route[:, 16, 0:1], 0.0))
                dve.sem_inc(family(name), n)

            st(V.memset(pall[:, EXPERTS, :, :], 0.0))

            def prologue(p):
                for e in range(EXPERTS):
                    for t in range(2):
                        TS(pall[:, e, t, :], const("iota"), pos[:, t, e:e + 1], None, ALU.is_equal)
                        ins = TS(gall[:, e, t, :], const("iota"), pos[:, t, e:e + 1], gate[:, t, e:e + 1],
                                 ALU.is_equal, ALU.mult)
                    ins.then_inc(family("m_placed"), 1)
                dve.wait_ge(family("m_placed"), p * EXPERTS + EXPERTS)
                TS(pos, pos, -float(CAP), None, ALU.add).then_inc(family("m_moved"), 1)
                gathered(p * (EXPERTS + 1) + 1)

            def gathered(n):
                dve.wait_ge(family("m_gathered"), n)
                for c in range(2):
                    ins = V.tensor_copy(he[:, 4 * c:4 * c + 4, :], TB[c][:, 0:4 * CAP].rearrange("p (k c) -> p k c", k=4))
                ins.then_inc(family("m_he"), 1)

            def body(it, e, p):
                def hidden(F):
                    dve.wait_ge(family("m_tanh"), it * NF + F + 1)
                    S3(out=hid[2 + F % 2][:, 0:CAP], in0=hid[F % 2][:, 0:CAP], scalar=1.0, in1=ACC[F % 2][:, 0:CAP],
                       op0=ALU.add, op1=ALU.mult).then_inc(family("m_silu"), 1)
                    dve.wait_ge(family("m_silu"), it * (3 * NF) + 3 * F + 1)
                    for dst in (act_e[:, F % 2, :], act_h[:, F % 4, :]):
                        S3(out=dst, in0=hid[2 + F % 2][:, 0:CAP], scalar=0.5, in1=ACC[F % 2][:, CAP:2 * CAP],
                           op0=ALU.mult, op1=ALU.mult).then_inc(family("m_silu"), 1)
                    dve.wait_ge(family("m_silu"), it * (3 * NF) + 3 * F + 3)
                    TTn(act_l[:, F % 4, :], act_e[:, F % 2, :], act_f[:, F % 4, :], ALU.subtract)\
                        .then_inc(family("m_hidden"), 1)

                for c, (f0, nf) in enumerate(STEPS):
                    for F in range(f0, f0 + nf):
                        hidden(F)
                    for F in SPLIT_BEHIND[c]:
                        dve.wait_ge(family("m_w2_high"), it * NF + F + 1)
                        TTn(w2_l[:, F % 2, :], w2_raw(F), w2_f[:, F % 2, :], ALU.subtract)\
                            .then_inc(family("m_w2_split"), 1)
                dve.wait_ge(family("m_slot_free"), it * 12 + 12 + RING_SLOTS)
                V.tensor_copy(ye[0:CAP, 512:1024], SB[1][0:CAP, :]).then_inc(family("m_yd"), 1)
                gathered(it + p + 2)
                for r in range(4):
                    dve.wait_ge(family("m_scattered"), it * 4 + r + 1)
                    v = x2[:, 2 * r:2 * r + 2, :]
                    TTn(v, (XB, OB)[r % 2][:, :].rearrange("p (j c) -> p j c", j=2), v, ALU.add)\
                        .then_inc(family("m_added"), 1)
            n = turns(dve, prologue, body)
            dve.wait_ge(family("m_added"), n * (EXPERTS * 4) + CREDITS)
            V.memset(route[:, 16, 1:2], 0.0).then_inc(*sig("moe_added"))

        fresh = []

        @block.tensor
        def _(pe):
            def open_group(name):
                n = unit[name] = len(unit)
                if n >= 2:
                    old = next(k for k, v in unit.items() if v == n - 2)
                    pe.wait_ge(*evacuated(*old))
                return ACC[n % 2]

            def gemm(name, mms, out, chunk=None):
                bank = open_group(name)
                key = fresh.pop() if fresh else None
                for i, (lhsT, rhs) in enumerate(mms):
                    if key is not None:
                        pe.wait_ge(*at("h_ready", key, i))
                    ins = pe.matmul(out(bank), lhsT, rhs, start=(i == 0), stop=(i == len(mms) - 1))
                ins.then_inc(*sig(f"acc_full{unit[name] % 2}", *name))
                if chunk is not None:
                    last_use[chunk] = (f"acc_full{unit[name] % 2}", *name)

            def chunk(pieces):
                n = len(chunks)
                chunks.append(pieces)
                pe.wait_ge(*at(f"w_loaded{n % NSLOT}", n))
                return n, [wring[n % NSLOT][:, o:o + k * c].rearrange("p (k c) -> p k c", k=k) for o, k, c, _ in pieces]

            def split_chunk(w, l, lo, hi):
                c = hi - lo
                return split_pieces(w[l][:, lo:hi], KT, c, (0, P, c) if c > P + 16 else (0, c))

            def split_pieces(src, kt, c, cuts):
                n, first = len(chunks), len(tiles)
                chunks.append([(0, kt, c, src.rearrange("(k p) c -> p k c", p=P))])
                splits.append((n, kt, c, first))
                tiles.extend((len(splits) - 1, c0, c1) for c0, c1 in zip(cuts, cuts[1:]))
                high, low = hring_r[(len(splits) - 1) % NHIGH], wring_r[n % NSLOT]
                return n, first, *(v[:, 0:kt * c].rearrange("p (k c) -> p k c", k=kt) for v in (high, low))

            seen = [-1]

            def gemm3(name, ch, c0, m, operands, out, slots=tuple(range(KT)), key=None):
                n, first, high, low = ch
                tile = max(i for i in range(first, len(tiles)) if tiles[i][1] < c0 + m)
                if tile > seen[0]:
                    pe.wait_ge(*at("w_split", tile))
                    seen[0] = tile
                bank = open_group(name)
                key = fresh.pop() if fresh else key
                kinds = ((high, hh, "h_high"), (high, hl, "h_ready"), (low, hh, None))
                kt = range(len(slots))
                order = [(k, i) for k in kt for i in range(3)]
                if key is not None:
                    order = [(k, i) for k in kt for i in (0, 2)] + [(k, 1) for k in kt]
                for k, i in order:
                    w_, h_, event = kinds[i]
                    if key is not None and event:
                        pe.wait_ge(*at(event, key, k))
                    lhsT, rhs = operands(w_[:, k, c0:c0 + m], h_[:, slots[k], :])
                    ins = pe.matmul(out(bank), lhsT, rhs, start=((k, i) == order[0]), stop=((k, i) == order[-1]))
                event = f"acc_full{unit[name] % 2}", *name
                ins.then_inc(*sig(*event))
                last_use[n] = event
                for i in range(first, tile + 1):
                    if tiles[i][2] > c0:
                        tile_use[i] = event
                tile_of[name] = tile

            def feat3(name, ch, c0, m, n, **kw):
                gemm3(name, ch, c0, m, lambda w_, h_: (w_, h_[:, 0:n]), lambda b: b[0:m, 0:n], **kw)

            def tok3(name, ch, c0, m, t0, nt):
                gemm3(name, ch, c0, m, lambda w_, h_: (h_[:, t0:t0 + nt], w_), lambda b: b[0:nt, 0:m])

            def feat(name, ch, w, c0, m, src, n, kt=KT):
                gemm(name, [(w[:, k, c0:c0 + m], src[:, k, 0:n]) for k in range(kt)], lambda b: b[0:m, 0:n], ch)

            pe.wait_ge(*at("tables"))
            pe.wait_ge(*at("x_loaded", 2))
            xs = gates.rearrange("p a b -> p (a b)")
            for j in range(KT):
                bank = open_group(("xt", j))
                for t, (t0, nt) in enumerate(TT):
                    ins = pe.transpose(bank[:, t0:t0 + nt], xs[0:nt, t * D + j * P:t * D + (j + 1) * P],
                                       const("ident", nt)[:, 0:nt])
                ins.then_inc(*sig(f"acc_full{j % 2}", "xt", j))

            def rope2(name):
                pe.wait_ge(*evacuated(*name))
                gemm(("rot", *name), [(const("rot64"), asc[:, rope_no[name] % 2, 0:T])], lambda b: b[:, 0:T])

            def sum_squares(name, key, n):
                bank = open_group(name)
                for k in range(KT):
                    pe.wait_ge(*at("squares", key, k))
                    ins = pe.matmul(bank[:, 0:n], const("ones"), sq[:, k, 0:n], start=(k == 0), stop=(k == KT - 1))
                ins.then_inc(*sig(f"acc_full{unit[name] % 2}", *name))
                fresh.append(key)

            for l in range(DEPTH):
                sum_squares(("ss", l), l, TA)
                win = a["w_in"]
                for nm, lo in (("fq", 0), ("fk", 512)):
                    for j in range(4):
                        if j % 2 == 0:
                            ch = split_chunk(win, l, lo + j * P, lo + (j + 2) * P)
                        feat3((nm, l, j), ch, j % 2 * P, P, TA)
                for c in range(2):
                    ch = split_chunk(win, l, 1024 + 256 * c, 1280 + 256 * c)
                    for t, (t0, nt) in enumerate(TT):
                        tok3(("fv", l, t, c), ch, 0, 256, t0, nt)
                ch = split_chunk(win, l, 1536, 1672)
                feat3(("ff", l), ch, 0, 8, TA)
                feat3(("z", l, 0), ch, 8, P, TA)
                ch = split_chunk(win, l, 1672, 1928)
                for j in range(2):
                    feat3(("z", l, 1 + j), ch, j * P, P, TA)
                ch = split_chunk(win, l, 1928, 2056)
                feat3(("z", l, 3), ch, 0, P, TA)
                for j in range(5):
                    if j % 2 == 0:
                        ch = split_chunk(win, l, 2056 + j * P, min(2056 + (j + 2) * P, 2728))
                    feat3(("cq", l, j), ch, j % 2 * P, P, TA)
                feat3(("kr", l), ch, P, 32, TA)
                for j in range(4):
                    if j % 2 == 0:
                        ch = split_chunk(win, l, 2728 + j * P, 2728 + (j + 2) * P)
                    feat3(("z", l, 4 + j), ch, j % 2 * P, P, TA)
                    if j == 1:
                        if l == 0:
                            pe.wait_ge(*at("tables1"))
                        pe.wait_ge(*evacuated("kr", l))
                        gemm(("krr", l), [(const("rot32", 32), asc[0:32, 3, :])], lambda b: b[0:32, 0:TA])
                        pe.wait_ge(*evacuated("cq", l, 4))
                        gemm(("sscq", l), [(const("ones"), sq[:, k, :]) for k in range(3)], lambda b: b[:, 0:TA])
                        gemm(("ssckv", l), [(const("ones"), sq[:, k, :]) for k in (3, 4)], lambda b: b[:, 0:TA])

                def rope_group(name, m, mat):
                    pe.wait_ge(*evacuated(*name))
                    gemm(("rot", *name), [(const(mat, m), asc[0:m, rope_no[name] % 2, :])], lambda b: b[0:m, 0:TA])

                for j in range(4):
                    if j % 2 == 0:
                        ch = split_chunk(win, l, 3240 + j * P, 3240 + (j + 2) * P)
                    feat3(("wq", l, j), ch, j % 2 * P, P, TA)
                    if j:
                        rope_group(("wq", l, j - 1), P, "rot64")
                ch = split_chunk(win, l, 3752, 4008)
                feat3(("wk", l), ch, 0, P, TA)
                rope_group(("wq", l, 3), P, "rot64")
                for t, (t0, nt) in enumerate(TT):
                    tok3(("wv", l, t), ch, P, P, t0, nt)
                rope_group(("wk", l), P, "rot64")
                for j in range(4):
                    if j % 2 == 0:
                        ch = split_chunk(win, l, 4008 + j * P, 4008 + (j + 2) * P)
                    feat3(("z", l, 8 + j), ch, j % 2 * P, P, TA)
                before_gates[l] = len(tiles)
                pe.wait_ge(*at("lowrank_ready", l))
                for j in range(HEADS):
                    if j % 4 == 0:
                        ch, (w,) = chunk([(0, 3, 384, a["w_uq"][l][:, 96 * j:96 * j + 384].rearrange("(k p) c -> p k c", p=P))])
                    feat(("mq", l, j), ch, w, (j % 4) * 96, 96, cqkv, TA, kt=3)
                    if j:
                        rope_group(("mq", l, j - 1), 96, "rotm")
                ch, (w,) = chunk([(0, 2, 1024, a["w_ukv"][l].rearrange("(k p) c -> p k c", p=P))])
                for j in range(HEADS):
                    gemm(("mk", l, j), [(w[:, k, j * P:j * P + 64], cqkv[:, 3 + k, :]) for k in range(2)],
                         lambda b: b[0:64, 0:TA], ch)
                    if j == 0:
                        rope_group(("mq", l, 7), 96, "rotm")
                for t, (t0, nt) in enumerate(TT):
                    gemm(("mv", l, t), [(cqkv[:, 3 + k, t0:t0 + nt],
                                         w[:, k, :].rearrange("p (h c) -> p h c", h=HEADS)[:, :, 64:128])
                                        for k in range(2)],
                         lambda b: b[0:nt, 0:512].rearrange("p (h c) -> p h c", h=HEADS), ch)
                pe.wait_ge(*evacuated("mv", l, 2))
                pe.wait_ge(*at("rope_done", len(ropes(l)) * (l + 1) - 1))
                pe.wait_ge(*at("kr_spread", l))
                pe.wait_ge(*at("c_moved", l))
                for i in range(24):
                    g = 24 * l + i
                    kind, hd = i // 8, i % 8
                    q, kk, K = ((qf, kf, 65), (qm, km, 96), (qw, kw, 64))[kind]
                    kh = hd // 4 if kind == 2 else hd
                    if g >= 2:
                        pe.wait_ge(*at("s_masked", g - 2))
                    c = 0
                    for t0, nt in TT:
                        ins = pe.matmul(SB[g % 2][0:nt, c:c + t0 + nt], q[0:K, hd, t0:t0 + nt],
                                        kk[0:K, kh, 0:t0 + nt], start=True, stop=True)
                        c += t0 + nt
                    ins.then_inc(*sig("s_full", g))
                    if i > 0:
                        transposes(pe, g - 1)
                    if i % 2 == 0:
                        ch = split_chunk(win, l, 4520 + 128 * i, 4520 + 128 * i + 256)
                    feat3(("g", l, i), ch, i % 2 * P, P, TA)
                    if i > 0:
                        pv(pe, g - 1)
                transposes(pe, 24 * l + 23)
                pv(pe, 24 * l + 23)
                after_gates[l] = len(tiles)
                for n in range(3):
                    for j in range(KT):
                        if j % 4 == 0:
                            ch = split_pieces(a["w_branch"][l, n][:, j * P:(j + 4) * P], 4, 512, (0, 256, 512))
                        feat3(("br", l, n, j), ch, j % 4 * P, P, TA, slots=branch_slots(n),
                              key=None if j else ("branch", l, n))
                for j in range(KT):
                    if j % 2 == 0:
                        ch = split_chunk(a["w_out"], l, j * P, (j + 2) * P)
                    feat3(("wo", l, j), ch, j % 2 * P, P, TA, slots=[merged_slot(k) for k in range(KT)],
                          key=None if j else ("merged", l))
                phase_end.append(len(tiles))
            sum_squares(("ss", DEPTH), DEPTH, TA)
            fresh.pop()

            def tok(name, ch, c0, m):
                for t in range(2):
                    tok3((*name, t), ch, c0, m, t * P, P)

            def norm2(key):
                sum_squares(("ss2", key), key, T)

            win = a["w_in_2"]
            for l in range(DEPTH):
                norm2(("mix", l))
                ch = split_chunk(win, l, 0, 256)
                for j in range(2):
                    feat3(("rq", l, j), ch, j * P, P, T)
                ch = split_chunk(win, l, 256, 512)
                for j in range(2):
                    rope2(("rq", l, j))
                    feat3(("rk", l, j), ch, j * P, P, T)
                tok(("rv", l), split_chunk(win, l, 512, 768), 0, 256)
                rope2(("rk", l, 0))
                rope2(("rk", l, 1))
                for j in range(4):
                    if j % 2 == 0:
                        ch = split_chunk(win, l, 768 + j * P, 768 + (j + 2) * P)
                    feat3(("gz", l, j), ch, j % 2 * P, P, T)
                for j in range(6):
                    if j % 2 == 0:
                        ch = split_chunk(win, l, 1280 + j * P, 1280 + (j + 2) * P + (4 if j == 4 else 0))
                    feat3(("xbc", l, j), ch, j % 2 * P, P, T)
                feat3(("sdt", l), ch, 2 * P, 4, T)
                tok(("mv", l, 2), split_chunk(win, l, 3348, 3604), 0, 256)
                feat3(("gz", l, 6), split_chunk(win, l, 3604, 3732), 0, P, T)
                ch = split_chunk(win, l, 3732, 3868)
                feat3(("gz", l, 7), ch, 0, P, T)
                feat3(("mi", l), ch, P, 4, T)
                feat3(("mf", l), ch, P + 4, 4, T)
                for j in range(4):
                    if j % 2 == 0:
                        ch = split_chunk(win, l, 2836 + j * P, 2836 + (j + 2) * P)
                    feat3(("mqk", l, j), ch, j % 2 * P, P, T)
                feat3(("gz", l, 4), split_chunk(win, l, 2564, 2692), 0, P, T)
                ch = split_chunk(win, l, 2692, 2836)
                feat3(("gz", l, 5), ch, 0, P, T)
                feat3(("ga", l), ch, P, 16, T)
                ch = split_chunk(win, l, 2052, 2308)
                feat3(("gq", l), ch, 0, P, T)
                pe.wait_ge(*evacuated("ga", l))
                c = pcol2[f"w_alpha{l}"][0]
                gemm(("al", l), [(par2[0:16, c:c + P], rowa[0:16, :])], lambda b: b[:, 0:T])
                feat3(("gk", l), ch, P, P, T)
                tok(("gv", l), split_chunk(win, l, 2308, 2564), 0, 256)
                gate_no = [0]

                def gate_units(n):
                    for _ in range(n):
                        i = gate_no[0]
                        gate_no[0] += 1
                        if i % 2 == 0:
                            gate_chunk[:] = split_chunk(win, l, 3868 + 128 * i, 3868 + 128 * i + 256)
                        feat3(("g2", l, i), gate_chunk, i % 2 * P, P, T)

                gate_chunk = []
                gate_units(GATES_BEFORE[0])
                pe.wait_ge(*at("rows_ready", l))
                bank = open_group(("rt", l))
                for t in range(2):
                    ins = pe.transpose(bank[:, 68 * t:68 * t + 68], rows[0:68, t * P:(t + 1) * P], const("ident", 68)[:, 0:68])
                ins.then_inc(*sig(f"acc_full{unit['rt', l] % 2}", "rt", l))
                pe.wait_ge(*at("conv_ready", l, 1))
                for t in range(2):
                    bank = open_group(("sxt", l, t))
                    for j in range(2):
                        ins = pe.transpose(bank[:, j * P:(j + 1) * P], conv[:, j, t * P:(t + 1) * P], const("ident"))
                    ins.then_inc(*sig(f"acc_full{unit['sxt', l, t] % 2}", "sxt", l, t))
                gate_units(GATES_BEFORE[1])
                pe.wait_ge(*at("conv_ready", l, 9))
                for i in range(12):
                    g = 12 * l + i
                    scores2(pe, l, i)
                    gate_units(1)
                    if i:
                        pv2(pe, l, i - 1)
                gate_units(1)
                pv2(pe, l, 11)
                for n in range(9):
                    levels2(pe, l, n)
                    gate_units(GATES_LEVEL[n])
                pe.wait_ge(*at("gla_picked", l, 8))
                for i in range(12, 16):
                    pv2(pe, l, i)
                gate_units(2)
                pe.wait_ge(*at("o_squares", l))
                for k, (mat, feature_tiles) in enumerate(NORMS):
                    gemm(("ssm", l, k), [(const(mat), squ[:, t, :]) for t in feature_tiles], lambda b: b[:, 0:T])
                gate_units(3)
                for n in range(4):
                    ch = split_pieces(a["w_branch_2"][l, n], 2, D, (0, 512, D))
                    for j in range(KT):
                        feat3(("br2", l, n, j), ch, j * P, P, T, slots=(2 * n, 2 * n + 1),
                              key=None if j else ("branch2", l, n))
                for j in range(KT):
                    if j % 2 == 0:
                        ch = split_chunk(a["w_out_2"], l, j * P, (j + 2) * P)
                    feat3(("wo2", l, j), ch, j % 2 * P, P, T, key=None if j else ("merged2", l))
                phase_end.append(len(tiles))
                if l:
                    pe.sem_inc(family("m_slot_free"), 3)
                norm2(("ffn", l))
                if l == 0:
                    chunks_before_ffn[0] = len(chunks)
                    fresh.pop()
                    mlp(pe, l)
                else:
                    moe_pe(pe, gemm, open_group)
            norm2(("final",))
            fresh.pop()
            pe.wait_ge(*at("y_normalised"))
            for t in range(2):
                for c in range(2):
                    bank = open_group(("yt", t, c))
                    for k in range(4):
                        ins = pe.transpose(bank[:, k * P:(k + 1) * P], h2[:, 4 * c + k, t * P:(t + 1) * P], const("ident"))
                    ins.then_inc(*sig(f"acc_full{unit['yt', t, c] % 2}", "yt", t, c))

        @block.sync
        def _(sp):
            def ring_chunk(n):
                if n >= NSLOT:
                    sp.wait_ge(*at(*last_use[n - NSLOT]))
                for o, k, c, src in chunks[n]:
                    sp.dma_start(wring[n % NSLOT][:, o:o + k * c].rearrange("p (k c) -> p k c", k=k), src)\
                        .then_inc(*sig(f"w_loaded{n % NSLOT}", n, by=16))

            def mlp_step(c):
                f0, nf = STEPS[c]
                if c >= 3:
                    sp.wait_ge(*at("mlp_down", c - 3))
                lo, hi = f0 * P, (f0 + nf) * P
                for m, w in enumerate((a["ffn_w1_2"], a["ffn_w3_2"])):
                    sp.dma_start(mring[c % 3][:, 2048 * m:2048 * m + KT * nf * P].rearrange("p (k c) -> p k c", k=KT),
                                 w[0][:, lo:hi].rearrange("(k p) c -> p k c", p=P)).then_inc(*sig(f"mlp_w13_{c % 3}", c, by=16))
                sp.dma_start(mring[c % 3][:, 4096:4096 + nf * D].rearrange("p (k c) -> p k c", k=nf),
                             a["ffn_w2_2"][0][lo:hi, :].rearrange("(k p) c -> p k c", p=P))\
                    .then_inc(*sig(f"mlp_w2_{c % 3}", c, by=16))

            xs = gates.rearrange("p a b -> p (a b)")
            sp.dma_start(xs[0:META, 0:D], a["meta_tokens"]).then_inc(*sig("x_loaded", 0, by=16))
            for t in range(2):
                sp.dma_start(xs[:, (t + 1) * D:(t + 2) * D], a["x"][0, t * P:(t + 1) * P, :])\
                    .then_inc(*sig("x_loaded", t + 1, by=16))
            sp.dma_start(cs, consts[:, 0:c_shared]).then_inc(*sig("tables", by=16))
            mid = chunks_before_ffn[0]
            for n in range(mid):
                ring_chunk(n)
            sp.wait_ge(*at("mix_done", 0))
            for c in range(3):
                mlp_step(c)
            for c in range(3, 12):
                mlp_step(c)
            sp.wait_ge(*at("up1", NF - 1))
            for n in range(mid, len(chunks)):
                ring_chunk(n)
            moe_sync(sp)
            for t in range(2):
                for c in range(2):
                    sp.wait_ge(*evacuated("yt", t, c))
                    sp.dma_start(out[0, t * P:(t + 1) * P, 512 * c:512 * c + 512], ytok[:, t, 512 * c:512 * c + 512])\
                        .then_inc(*sig("out_stored", by=16))
            sp.wait_ge(*at("out_stored"))

        @block.gpsimd
        def _(pool):
            pl = Steps(pool, "pool_own")
            pl(pool.memset(eps[:, :], EPS))
            pl.settle()
            pl(pool.memset(stat[:, :, :], 0.0))
            pl.settle()
            pl(pool.memset(qf[64:65, :, :], 1.0), sig("memory_set"))

            split_no = [0]

            def low_parts(until):
                while split_no[0] < until:
                    i = split_no[0]
                    split_no[0] += 1
                    s_, c0, c1 = tiles[i]
                    n, kt, c, _ = splits[s_]
                    pool.wait_ge(*at("w_high", i))
                    raw, high, low = (v[:, 0:kt * c].rearrange("p (k c) -> p k c", k=kt)[:, :, c0:c1]
                                      for v in (wring[n % NSLOT], hring[s_ % NHIGH], wring_r[n % NSLOT]))
                    pl.settle()
                    pl(pool.tensor_tensor(low, raw, high, ALU.subtract), sig("w_split", i))
            for l in range(DEPTH):
                low_parts(before_gates[l])
                pool.wait_ge(*at("c_ready", l))
                for hd in range(HEADS):
                    pool.dma_start(kf[64:65, hd, :], tsc[hd:hd + 1, 3, :]).then_inc(*sig("c_moved", l, by=16))
                pool.wait_ge(*at("kr_ready", l))
                pl.settle()
                pl(pool.tensor_copy(km[64:96, 1:8, :], km[64:96, 0:1, :].broadcast_to((32, 7, TA))),
                   sig("kr_spread", l))
                if l == 0:
                    low_parts(phase_end[l])
            low_parts(after_gates[DEPTH - 1] + 2 * AHEAD)
            pool.wait_ge(*at("pt_act", 24 * DEPTH - 1))
            pool.wait_ge(*at("o_full", 12 * DEPTH - 1))
            pool.dma_start(cs2, consts[:, c_first:c_all]).then_inc(*sig("tables2", by=16))
            for v in (agla, xbc[:, :, 0:3], mqk[:, :, 0:3]):
                low_parts(split_no[0] + 2)
                pl.settle()
                pl(pool.memset(v, 0.0))
                pl.settle()
            low_parts(phase_end[DEPTH - 1])
            pool.wait_ge(*at("merged", DEPTH - 1, KT - 1))
            pl.settle()
            pl(pool.memset(rows, 0.0), sig("memory_set2", 0))
            low_parts(phase_end[2])
            pool.wait_ge(*at(*last_use[chunks_before_ffn[0] - 1]))
            for F in range(NF):
                pool.wait_ge(*at("up_high", F))
                for m in range(2):
                    _, raw, high, _, low = up_parts(F, m)
                    pl.settle()
                    pl(pool.tensor_tensor(low, raw, high, ALU.subtract), sig("up_split", F) if m else None)
            low_parts(phase_end[2] + AHEAD)
            pool.wait_ge(*at("ffn_done"))
            pl.settle()
            for v in (agla, xbc[:, :, 0:3], mqk[:, :, 0:3], rows):
                pl(pool.memset(v, 0.0), sig("memory_set2", 1) if v is rows else None)
                pl.settle()
            low_parts(phase_end[3])

        @block.scalar
        def _(act):
            A, cp = nc.scalar.activation, nc.scalar.copy
            st = Steps(act, "act_own")
            for i, (dst, src) in enumerate(param_dmas[:n1]):
                act.dma_start(dst, src, allow_slow_non_contiguous=True).then_inc(*sig("params", i, by=16))
            act.dma_start(cs1, consts[:, c_shared:c_first]).then_inc(*sig("tables1", by=16))

            high_no = [0]

            def freed_by(i):
                s_, _, _ = tiles[i]
                if s_ < NHIGH:
                    return -1
                (_, *form, first), (_, *form_old, old), after = splits[s_], splits[s_ - NHIGH], splits[s_ - NHIGH + 1][3]
                return min(old + i - first, after - 1) if form_old == form else after - 1

            def high_parts(until, done=None):
                while high_no[0] < until and (done is None or freed_by(high_no[0]) <= done):
                    i = high_no[0]
                    high_no[0] += 1
                    s_, c0, c1 = tiles[i]
                    n, kt, c, first = splits[s_]
                    if i == first:
                        act.wait_ge(*at(f"w_loaded{n % NSLOT}", n))
                    if freed_by(i) >= 0:
                        act.wait_ge(*at(*tile_use[freed_by(i)]))
                    raw, high = (v[:, 0:kt * c].rearrange("p (k c) -> p k c", k=kt)[:, :, c0:c1]
                                 for v in (wring[n % NSLOT], hring_r[s_ % NHIGH]))
                    cp(high, raw).then_inc(*sig("w_high", i))

            def ahead(*name):
                if name in tile_of:
                    tile = tile_of[name]
                    high_parts(min(tile + 1 + AHEAD, min(e for e in (*phase_end[2:], *before_gates.values()) if e > tile)), tile)

            def follow(*name):
                full(act, *name)
                if tile_use[tile_of[name]][1:] == name:
                    ahead(*name)

            def high_tile(key, k, src, slot, n):
                st.settle()
                cp(hh[:, slot, 0:n], src).then_inc(*sig("h_high", key, k))

            def high_h(key, n):
                for k in range(KT):
                    act.wait_ge(*at("h_raw", key, k))
                    cp(hh[:, k, 0:n], h[:, k, 0:n]).then_inc(*sig("h_high", key, k))

            act.wait_ge(*at("memory_set"))

            def squares(key, src, n, ready, group=None):
                for k in range(KT):
                    if group:
                        follow(*group(k))
                    act.wait_ge(*ready(k))
                    if k == 0:
                        st(A(stat[0:1, 1, 14:15], eps[0:1, :], ACT.Sqrt))
                    st(A(sq[:, k, 0:n], src[:, k, 0:n], ACT.Square), sig("squares", key, k))

            def root(name, slot, dim, n=TA):
                b = full(act, *name)
                st(A(rstd[:, slot, 0:n], b[:, 0:n], ACT.Sqrt, bias=eps[:, 0:1], scale=1.0 / dim), free(*name))

            for l in range(DEPTH):
                squares(l, x, TA, lambda k: evacuated("wo", l - 1, k) if l else evacuated("xt", k),
                        (lambda k: ("wo", l - 1, k)) if l else None)
                if l == 0:
                    high_parts(AHEAD)
                root(("ss", l), 0, D)
                high_h(l, TA)
                for nm, dst in (("fq", qf), ("fk", kf)):
                    for j in range(4):
                        b = full(act, nm, l, j)
                        st(cp(dst[0:64, 2 * j, :], b[0:64, 0:TA]))
                        st(cp(dst[0:64, 2 * j + 1, :], b[64:128, 0:TA]), free(nm, l, j))
                        ahead(nm, l, j)
                for c in range(2):
                    for t, (t0, nt) in enumerate(TT):
                        b = full(act, "fv", l, t, c)
                        st(cp(vf[0:nt, t, 256 * c:256 * c + 256], b[0:nt, 0:256]), free("fv", l, t, c))
                    ahead("fv", l, 2, c)
                act.wait_ge(*evacuated("ff", l))
                st(A(asc[0:8, 0, :], tsc[0:8, 0, :], ACT.Abs))
                st.settle()
                st(A(asc[0:8, 1, :], asc[0:8, 0, :], ACT.Exp, scale=-1.0))
                st.settle()
                st(A(asc[0:8, 2, :], asc[0:8, 1, :], ACT.Ln, bias=1.0), sig("logf_ln", l))

                def z_tile(j):
                    b = full(act, "z", l, j)
                    st(A(zs[:, j, :], b[:, 0:TA], ACT.Tanh, scale=0.5), sig("z_tanh", l, j))
                    ahead("z", l, j)
                for j in range(4):
                    z_tile(j)
                for j in range(5):
                    b = full(act, "cq", l, j)
                    st(cp(cqkv[:, j, :], b[:, 0:TA]))
                    st(A(sq[:, j, :], b[:, 0:TA], ACT.Square), free("cq", l, j))
                    ahead("cq", l, j)
                b = full(act, "kr", l)
                st(cp(asc[0:32, 3, :], b[0:32, 0:TA]), free("kr", l))
                ahead("kr", l)
                z_tile(4)
                z_tile(5)
                root(("sscq", l), 0, 384)
                root(("ssckv", l), 1, 256)
                z_tile(6)
                z_tile(7)

                def rope_raw(name, m):
                    r = rope_no[name]
                    b = full(act, *name)
                    if r >= 2:
                        act.wait_ge(*at("rope_done", r - 2))
                    else:
                        act.wait_ge(*at("c_ready", 0))
                    st.settle()
                    st(cp(asc[0:m, r % 2, :], b[0:m, 0:TA]), free(*name))
                    ahead(*name)
                for j in range(4):
                    rope_raw(("wq", l, j), P)
                rope_raw(("wk", l), P)
                for t, (t0, nt) in enumerate(TT):
                    b = full(act, "wv", l, t)
                    st(cp(vw[0:nt, t, :], b[0:nt, 0:P]), free("wv", l, t))
                ahead("wv", l, 2)
                for j in range(8, 12):
                    z_tile(j)
                for j in range(HEADS):
                    rope_raw(("mq", l, j), 96)
                high_parts(before_gates[l] + 2)
                for j in range(HEADS):
                    b = full(act, "mk", l, j)
                    st(cp(km[0:64, j, :], b[0:64, 0:TA]), free("mk", l, j))
                high_parts(before_gates[l] + AHEAD)
                for t, (t0, nt) in enumerate(TT):
                    b = full(act, "mv", l, t)
                    st(cp(vm[0:nt, t, :], b[0:nt, 0:512]), free("mv", l, t))

                def pt_copy(g):
                    act.wait_ge(*at("pt_full", g))
                    st(cp(ptm[g % 2][:, :], TB[g % 2][:, 0:W2B]), sig("pt_act", g))
                for i in range(24):
                    g = 24 * l + i
                    kind, hd = i // 8, i % 8
                    sc = (64 ** -0.5, 96 ** -0.5, 64 ** -0.5)[kind]
                    s_ = stat[:, g % 2, :]
                    act.wait_ge(*at("neg_max", g))
                    if kind == 2:
                        st(A(s_[:, 12:15], s_[:, 3:6], ACT.Exp, bias=pc(f"sinks{l}", hd)))
                    c = 0
                    for t, (t0, nt) in enumerate(TT):
                        n = t0 + nt
                        st(A(sm[g % 2][0:nt, c:c + n], sm[g % 2][0:nt, c:c + n], ACT.Exp, scale=sc,
                             bias=s_[0:nt, 3 + t:4 + t], accum_out=s_[0:nt, 6 + t:7 + t]),
                           sig("p_exp", g) if t == 2 else None)
                        c += n
                    if i:
                        pt_copy(g - 1)
                    b = full(act, "g", l, i)
                    st(A(gates[:, i, :], b[:, 0:TA], ACT.Tanh, scale=0.5), free("g", l, i))
                    ahead("g", l, i)

                def high_branch(n):
                    act.wait_ge(*at("y_ready", 12 * l + 4 * n + 3))
                    for k, slot in enumerate(branch_slots(n)):
                        high_tile(("branch", l, n), k, zs[:, 4 * n + k, :], slot, TA)

                def high_merged(j):
                    act.wait_ge(*at("merged", l, j))
                    high_tile(("merged", l), j, sq[:, j, :], merged_slot(j), TA)
                high_branch(0)
                pt_copy(24 * l + 23)
                high_branch(1)
                later = []
                if l == DEPTH - 1:
                    act.wait_ge(*at("o_full", 12 * DEPTH - 1))
                    act.wait_ge(*at("y_ready", 12 * DEPTH - 1))
                    later = param_dmas[n1:]
                for n in range(3):
                    for j in range(KT):
                        follow("br", l, n, j)
                        for dst, src in later[(n * KT + j) * 2:(n * KT + j + 1) * 2]:
                            act.dma_start(dst, src, allow_slow_non_contiguous=True).then_inc(*sig("params2", by=16))
                        if n == 1 and j == 0:
                            high_branch(2)
                        if n == 2 and 1 <= j < 5:
                            high_merged(j - 1)
                assert len(later) <= 2 * 3 * KT
                for j in range(4, KT):
                    high_merged(j)
            squares(DEPTH, x, TA, lambda k: evacuated("wo", DEPTH - 1, k), lambda k: ("wo", DEPTH - 1, k))
            root(("ss", DEPTH), 0, D)

            act.wait_ge(*at("memory_set2", 0))
            def norm2(key, ready, group=None, then=None):
                squares(key, x2, T, ready, group)
                if then:
                    then()
                root(("ss2", key), 0, D, T)

            def rope_raw2(name):
                r = rope_no[name]
                b = full(act, *name)
                act.wait_ge(*at("rope_done", r - 2))
                st.settle()
                st(cp(asc[:, r % 2, 0:T], b[:, 0:T]), free(*name))
                ahead(*name)

            def gate2(l, j):
                b = full(act, "gz", l, j)
                st(A(zs2[:, j, :], b[:, 0:T], ACT.Tanh, scale=0.5), free("gz", l, j) if j >= 6 else sig("gz_tanh", l, j))
                ahead("gz", l, j)

            def copy_unit(dst, name, part, scale=1.0):
                b = full(act, *name)
                st(A(dst, b[part, 0:dst.shape[-1]], ACT.Copy, scale=scale), free(*name))
                ahead(*name)

            for l in range(DEPTH):
                if l:
                    high_parts(phase_end[DEPTH] + AHEAD)
                norm2(("mix", l), lambda k: at("x2_ready", k) if l == 0 else at("mlp_added", 0, k))
                high_h(("mix", l), T)
                act.wait_ge(*at("memory_set2", l))
                act.wait_ge(*at("par2_ready"))
                for nm in ("rq", "rk"):
                    for j in range(2):
                        rope_raw2((nm, l, j))
                for t in range(2):
                    copy_unit(vtok[:, 0, t, :], ("rv", l, t), slice(0, P))
                for j in range(4):
                    gate2(l, j)
                for j in range(6):
                    copy_unit(xbc[:, j, 3:T + 3], ("xbc", l, j), slice(0, P))
                for t in range(2):
                    copy_unit(vtok[:, 3, t, :], ("mv", l, 2, t), slice(0, P))
                gate2(l, 6)
                gate2(l, 7)
                for j in range(4):
                    copy_unit(mqk[:, j, 3:T + 3], ("mqk", l, j), slice(0, P))
                gate2(l, 4)
                gate2(l, 5)
                copy_unit(rowa[0:16, :], ("ga", l), slice(0, 16))
                copy_unit(gla_q, ("gq", l), slice(0, P), scale=32 ** -0.5)
                copy_unit(gla_k, ("gk", l), slice(0, P))
                for t in range(2):
                    copy_unit(vtok[:, 2, t, :], ("gv", l, t), slice(0, P))
                gn = [0]

                def gate_tanh(n):
                    for _ in range(n):
                        i = gn[0]
                        gn[0] += 1
                        b = full(act, "g2", l, i)
                        st(A(gates2[:, i, :], b[:, 0:T], ACT.Tanh, scale=0.5), free("g2", l, i))
                        ahead("g2", l, i)
                act.wait_ge(*evacuated("mf", l))
                act.wait_ge(*evacuated("al", l))
                for src, dst, n in ((tsc[0:36, 0, 0:T], 0, 36), (lg, 1, P)):
                    st(A(asc[0:n, dst, 0:T], src, ACT.Abs))
                    st.settle()
                    st(A(asc[0:n, dst, 0:T], asc[0:n, dst, 0:T], ACT.Exp, scale=-1.0))
                st(A(stat[0:4, 1, 15:16], pc(f"a_log{l}", parts=4), ACT.Exp))
                st.settle()
                for dst, n in ((0, 36), (1, P)):
                    st(A(asc[0:n, dst, 0:T], asc[0:n, dst, 0:T], ACT.Ln, bias=1.0), sig("ln2", l, dst))
                gate_tanh(GATES_BEFORE[0])
                for j in range(10):
                    act.wait_ge(*at("conv_sum", l, j))
                    if j >= 2:
                        act.wait_ge(*at("conv_ready", l, j - 2))
                    st(A(asc[:, 2 + j % 2, 0:T], conv[:, j, :], ACT.Tanh, scale=0.5), sig("conv_tanh", l, j))
                act.wait_ge(*at("rows_ready", l))
                st(A(rowe[0:4, :], rowb[32:36, :], ACT.Exp, scale=-1.0), sig("rowe_ready", l))

                gate_tanh(GATES_BEFORE[1])
                for i in range(12):
                    g = 12 * l + i
                    if i >= 4:
                        act.wait_ge(*at("seg_arg", g))
                        st(A(seg[g % 2][:, :], seg[g % 2][:, :], ACT.Exp), sig("seg_exp", g))
                    gate_tanh(1)
                gate_tanh(1)
                for n in range(9):
                    if n < 8:
                        act.wait_ge(*at("level_arg", l, n + 1))
                        st(A(lx[(n + 1) % 2], lx[(n + 1) % 2], ACT.Exp), sig("level_exp", l, n + 1))
                    gate_tanh(GATES_LEVEL[n])
                act.wait_ge(*at("o2_done", l))
                st(A(squ, o2, ACT.Square), sig("o_squares", l))
                gate_tanh(2)
                for k in range(7):
                    name = ("ssm", l, k)
                    b = full(act, *name)
                    st(A(roots[:, k, :], b[:, 0:T], ACT.Ln, bias=eps[:, 0:1], scale=1.0 / (256 if k == 2 else 64)),
                       free(*name))
                st.settle()
                st(A(roots, roots, ACT.Exp, scale=-0.5), sig("roots_ready", l))
                gate_tanh(3)

                def up_high(F):
                    if F >= NHIGH:
                        act.wait_ge(*at("up1", F - NHIGH))
                    for m in range(2):
                        c, raw, _, high, _ = up_parts(F, m)
                        act.wait_ge(*at(f"mlp_w13_{c % 3}", c))
                        st(cp(high, raw), sig("up_high", F) if m else None)
                for n in range(4):
                    act.wait_ge(*at("y2_ready", l, n))
                    for k in range(2):
                        high_tile(("branch2", l, n), k, zs2[:, 2 * n + k, :], 2 * n + k, T)

                def high_merged2(j):
                    act.wait_ge(*at("merged2", l, j))
                    high_tile(("merged2", l), j, sq[:, j, 0:T], j, T)
                for n in range(4):
                    for j in range(KT):
                        follow("br2", l, n, j)
                        if n == 3 and 1 <= j < 7:
                            high_merged2(j - 1)
                high_merged2(6)
                high_merged2(7)

                def first_up():
                    act.wait_ge(*at(*last_use[splits[tiles[phase_end[2] - 1][0]][0]]))
                    for F in range(NHIGH):
                        up_high(F)
                norm2(("ffn", l), lambda k: evacuated("wo2", l, k), lambda k: ("wo2", l, k), None if l else first_up)
                if l == 0:
                    high_h(("ffn", l), T)
                    for F in range(NF):
                        act.wait_ge(*at("up0", F))
                        if F >= 2:
                            act.wait_ge(*at("hidden", F - 2))
                        else:
                            act.wait_ge(*at("h_ready", ("ffn", l), KT - 1))
                        st(A(hid[F % 2], UB[F % 2][0][:, 0:T], ACT.Tanh, scale=0.5), sig("up_tanh", F))
                        if F + NHIGH < NF:
                            up_high(F + NHIGH)
                    act.wait_ge(*at("up1", NF - 1))
            moe_act(act)
            norm2(("final",), lambda k: at("moe_added"))
            for t in range(2):
                for c in range(2):
                    b = full(act, "yt", t, c)
                    cp(ytok[:, t, 512 * c:512 * c + 512], b[:, :]).then_inc(*free("yt", t, c))

        @block.vector
        def _(dve):
            V = nc.vector
            st = Steps(dve, "dve_own")
            dve.wait_ge(*at("memory_set"))
            for j in range(KT):
                b = full(dve, "xt", j)
                st(V.tensor_copy(x[:, j, :], b[:, 0:TA]), free("xt", j))
            dve.wait_ge(*at("params", n1 - 1))
            for l in range(DEPTH):
                c = pcol1[f"negsink{l}"][0]
                st(V.tensor_scalar(par1[:, c:c + 8], par1[:, c - 8:c], -1.0, None, ALU.mult))

            def normalise(name, slot, gcol, src, dst, tiles, done, n=TA, d0=0, then=None):
                dve.wait_ge(*evacuated(*name))
                st.settle()
                st(V.reciprocal(rstd[:, slot, 0:n], rstd[:, slot, 0:n]))
                st.settle()
                for i, k in enumerate(tiles):
                    st(V.scalar_tensor_tensor(out=dst[:, k, 0:n - d0], in0=src[:, k, d0:n], scalar=pc(gcol, i),
                                              in1=rstd[:, slot, d0:n], op0=ALU.mult, op1=ALU.mult),
                       done(i) if done else None)
                    if then and i:
                        then(i - 1)
                if then:
                    then(KT - 1)

            def low_tile(key, k, src, slot, n):
                dve.wait_ge(*at("h_high", key, k))
                st(V.tensor_tensor(hl[:, slot, 0:n], src, hf[:, slot, 0:n], ALU.subtract), sig("h_ready", key, k))

            def low_h(key, k, n):
                dve.wait_ge(*at("h_high", key, k))
                st(V.tensor_tensor(hl[:, k, 0:n], h[:, k, 0:n], hf[:, k, 0:n], ALU.subtract), sig("h_ready", key, k))

            def silu_tile(l, j):
                b = full(dve, "z", l, j)
                dve.wait_ge(*at("z_tanh", l, j))
                st(V.scalar_tensor_tensor(out=zs[:, j, :], in0=zs[:, j, :], scalar=1.0, in1=b[:, 0:TA],
                                          op0=ALU.add, op1=ALU.mult), free("z", l, j))

            for l in range(DEPTH):
                normalise(("ss", l), 0, f"norm_g{l}", x, h, range(KT), lambda k: sig("h_raw", l, k),
                          then=lambda k: low_h(l, k, TA))
                b = full(dve, "ff", l)
                st.settle()
                if l:
                    dve.wait_ge(*at("c_moved", l - 1))
                st(V.tensor_scalar(tsc[0:8, 0, :], b[0:8, 0:TA], pc(f"b_f{l}", parts=8), None, ALU.add), free("ff", l))
                st.settle()
                st(V.tensor_scalar(tsc[0:8, 1, :], tsc[0:8, 0, :], 0.0, None, ALU.min))
                dve.wait_ge(*at("logf_ln", l))
                st.settle()
                st(V.tensor_tensor(tsc[0:8, 2, :], tsc[0:8, 1, :], asc[0:8, 2, :], ALU.subtract))
                st.settle()
                st(V.tensor_tensor_scan(tsc[0:8, 1, :], const("ones", 8)[:, 0:1].broadcast_to((8, TA)),
                                        tsc[0:8, 2, :], 0.0, ALU.mult, ALU.add))
                st.settle()
                st(V.tensor_scalar(tsc[0:8, 3, :], tsc[0:8, 1, :], -(64 ** 0.5), None, ALU.mult), sig("c_ready", l))
                for j in range(6):
                    silu_tile(l, j)

                def rope(name, m, cos, sin, mat_src, outs, done):
                    b = full(dve, *name)
                    st.settle()
                    st(V.tensor_tensor(tsc[0:m, 0, :], mat_src, cos, ALU.mult))
                    st(V.tensor_tensor(tsc[0:m, 1, :], b[0:m, 0:TA], sin, ALU.mult), free(*name))
                    st.settle()
                    for i, (dst, lo, hi) in enumerate(outs):
                        st(V.tensor_tensor(dst, tsc[lo:hi, 0, :], tsc[lo:hi, 1, :], ALU.add),
                           done() if i == len(outs) - 1 else None)

                if l == 0:
                    dve.wait_ge(*at("tables1"))
                rope(("krr", l), 32, const("cos32", 32), const("sin32", 32), asc[0:32, 3, :],
                     [(km[64:96, 0, :], 0, 32)], lambda: sig("kr_ready", l))
                normalise(("sscq", l), 0, f"g_cq{l}", cqkv, cqkv, range(3), None)
                normalise(("ssckv", l), 1, f"g_ckv{l}", cqkv, cqkv, (3, 4), lambda k: sig("lowrank_ready", l))
                silu_tile(l, 6)
                silu_tile(l, 7)
                for j in range(4):
                    r = rope_no["wq", l, j]
                    rope(("rot", "wq", l, j), P, const("cos64"), const("sin64"), asc[:, r % 2, :],
                         [(qw[0:64, 2 * j, :], 0, 64), (qw[0:64, 2 * j + 1, :], 64, 128)],
                         lambda: sig("rope_done", r))
                r = rope_no["wk", l]
                rope(("rot", "wk", l), P, const("cos64"), const("sin64"), asc[:, r % 2, :],
                     [(kw[0:64, 0, :], 0, 64), (kw[0:64, 1, :], 64, 128)], lambda: sig("rope_done", r))
                for j in range(8, 12):
                    silu_tile(l, j)
                for j in range(HEADS):
                    r = rope_no["mq", l, j]
                    rope(("rot", "mq", l, j), 96, const("cosm", 96), const("sinm", 96), asc[0:96, r % 2, :],
                         [(qm[0:96, j, :], 0, 96)], lambda: sig("rope_done", r))

                def pt_copy(g):
                    dve.wait_ge(*at("pt_full", g))
                    st(V.tensor_copy(ptx[g % 2][0:META, :], XB[0:META, 0:TA]), sig("pt_dve", g))

                def gated(pair):
                    dve.wait_ge(*at("o_full", pair))
                    j = pair % 12
                    st(V.scalar_tensor_tensor(out=zs[:, j, :], in0=OB[:, 0:TA], scalar=0.5, in1=zs[:, j, :],
                                              op0=ALU.mult, op1=ALU.mult), sig("y_ready", pair))
                for i in range(24):
                    g = 24 * l + i
                    kind, hd = i // 8, i % 8
                    sc = (64 ** -0.5, 96 ** -0.5, 64 ** -0.5)[kind]
                    s_ = stat[:, g % 2, :]
                    mask = const("band" if kind == 2 else "causal")
                    dve.wait_ge(*at("s_full", g))
                    if g >= 2:
                        dve.wait_ge(*at("pt_full", g - 2))
                        dve.wait_ge(*at("p_exp", g - 2))
                    c = 0
                    st.settle()
                    for t, (t0, nt) in enumerate(TT):
                        n = t0 + nt
                        st(V.tensor_tensor_reduce(out=sm[g % 2][0:nt, c:c + n], in0=SB[g % 2][0:nt, c:c + n],
                                                  in1=mask[0:nt, c:c + n], scale=1.0, scalar=-3e38, op0=ALU.add,
                                                  op1=ALU.max, accum_out=s_[0:nt, t:t + 1]),
                           sig("s_masked", g) if t == 2 else None)
                        c += n
                    st.settle()
                    if kind == 2:
                        st(V.tensor_scalar(s_[:, 3:6], s_[:, 0:3], -sc, pc(f"negsink{l}", hd), ALU.mult, ALU.min),
                           sig("neg_max", g))
                    else:
                        st(V.tensor_scalar(s_[:, 3:6], s_[:, 0:3], -sc, None, ALU.mult), sig("neg_max", g))
                    if i:
                        pt_copy(g - 1)
                    dve.wait_ge(*at("p_exp", g))
                    st.settle()
                    if kind == 2:
                        st(V.tensor_tensor(s_[:, 6:9], s_[:, 6:9], s_[:, 12:15], ALU.add))
                        st.settle()
                    st(V.reciprocal(s_[:, 9:12], s_[:, 6:9]))
                    st.settle()
                    c = 0
                    for t, (t0, nt) in enumerate(TT):
                        n = t0 + nt
                        st(V.tensor_scalar(sm[g % 2][0:nt, c:c + n], sm[g % 2][0:nt, c:c + n],
                                           s_[0:nt, 9 + t:10 + t], None, ALU.mult),
                           sig("p_ready", g) if t == 2 else None)
                        c += n
                    if i >= 2 and i % 2 == 0:
                        gated(g // 2 - 1)
                def low_branch(n):
                    for k, slot in enumerate(branch_slots(n)):
                        low_tile(("branch", l, n), k, zs[:, 4 * n + k, :], slot, TA)

                def low_merged(j):
                    low_tile(("merged", l), j, sq[:, j, :], merged_slot(j), TA)
                pt_copy(24 * l + 23)
                low_branch(0)
                gated(12 * l + 11)
                low_branch(1)
                for n in range(3):
                    for j in range(KT):
                        b = full(dve, "br", l, n, j)
                        if n == 0 and j == 0:
                            dve.wait_ge(*evacuated("g", l, 23))
                        st.settle()
                        dst = sq[:, j, :] if n == 0 else tsc[:, j % 4, :]
                        st(V.scalar_tensor_tensor(out=dst, in0=gates[:, n * 8 + j, :], scalar=1.0, in1=b[:, 0:TA],
                                                  op0=ALU.add, op1=ALU.mult), free("br", l, n, j))
                        if n:
                            st.settle()
                            st(V.tensor_tensor(sq[:, j, :], sq[:, j, :], dst, ALU.add),
                               sig("merged", l, j) if n == 2 else None)
                        if n == 1 and j == 0:
                            low_branch(2)
                        if n == 2 and 1 <= j < 5:
                            low_merged(j - 1)
                for j in range(4, KT):
                    low_merged(j)
                for j in range(8):
                    b = full(dve, "wo", l, j)
                    st(V.scalar_tensor_tensor(out=x[:, j, :], in0=b[:, 0:TA], scalar=0.5, in1=x[:, j, :],
                                              op0=ALU.mult, op1=ALU.add), free("wo", l, j))
            normalise(("ss", DEPTH), 0, "final_g", x, x2, range(KT), lambda k: sig("x2_ready", k), d0=META)

            S3, TS, TTn = V.scalar_tensor_tensor, V.tensor_scalar, V.tensor_tensor
            dve.wait_ge(*at("params2"))
            st.settle()
            for l in range(DEPTH):
                for nm, n in (("ret_g", 2), ("gla_g", 2), ("ml_g", 2), ("d", 2)):
                    c = pcol2[f"{nm}{l}"][0]
                    st(TS(par2[:, c:c + n], par2[:, c:c + n], 0.5, None, ALU.mult),
                       sig("par2_ready") if (l, nm) == (DEPTH - 1, "d") else None)

            def norm2(key, g, out_sig, then=None):
                name = ("ss2", key)
                dve.wait_ge(*evacuated(*name))
                st.settle()
                st(V.reciprocal(rstd[:, 0, 0:T], rstd[:, 0, 0:T]))
                st.settle()
                for k in range(KT):
                    st(S3(out=h2[:, k, :], in0=x2[:, k, :], scalar=pc(g, k), in1=rstd[:, 0, 0:T], op0=ALU.mult,
                          op1=ALU.mult), out_sig(k))
                    if then and k:
                        then(k - 1)
                if then:
                    then(KT - 1)

            def rope2(name, dst):
                b = full(dve, "rot", *name)
                st.settle()
                st(TTn(tsc[:, 2, 0:T], asc[:, rope_no[name] % 2, 0:T], const("cos64")[:, 0:T], ALU.mult))
                st(TTn(tsc[:, 3, 0:T], b[:, 0:T], const("sin64")[:, 0:T], ALU.mult), free("rot", *name))
                st.settle()
                st(TTn(dst, tsc[:, 2, 0:T], tsc[:, 3, 0:T], ALU.add), sig("rope_done", rope_no[name]))

            def gate2(l, j):
                b = full(dve, "gz", l, j)
                dve.wait_ge(*at("gz_tanh", l, j))
                st(S3(out=zs2[:, j, :], in0=zs2[:, j, :], scalar=1.0, in1=b[:, 0:T], op0=ALU.add, op1=ALU.mult),
                   free("gz", l, j))

            def conv_sum(l, j):
                src, nm, jj = (xbc[:, j, :], "ssd", j) if j < 6 else (mqk[:, j - 6, :], "ml", j - 6)
                dve.wait_ge(*(evacuated("xbc", l, j) if j < 6 else evacuated("mqk", l, jj)))
                st(TS(conv[:, j, :], src[:, 0:T], pc(f"{nm}_w{l}0", jj), pc(f"{nm}_b{l}", jj), ALU.mult, ALU.add))
                for i in range(1, 4):
                    st.settle()
                    st(S3(out=conv[:, j, :], in0=src[:, i:i + T], scalar=pc(f"{nm}_w{l}{i}", jj), in1=conv[:, j, :],
                          op0=ALU.mult, op1=ALU.add), sig("conv_sum", l, j) if i == 3 else None)

            def conv_silu(l, j):
                dve.wait_ge(*at("conv_tanh", l, j))
                st(S3(out=conv[:, j, :], in0=asc[:, 2 + j % 2, 0:T], scalar=1.0, in1=conv[:, j, :], op0=ALU.add,
                      op1=ALU.mult), sig("conv_ready", l, j))

            def scan(dst, src, op, n0, n1_):
                st(V.tensor_tensor_scan(dst, const("ones")[n0:n1_, 0:1].broadcast_to((n1_ - n0, T)), src, 0.0,
                                        ALU.mult, op))

            def pair_done(l, pair):
                m, p = ORDER2[pair // 2], pair % 2
                dve.wait_ge(*at("o2_full", 8 * l + pair))
                dst = o2[:, 2 * m + p, :]
                done = lambda: sig("o2_read", 8 * l + pair)
                if m in (0, 2):
                    st(V.tensor_copy(dst, OB[:, 0:T]), done())
                elif m == 1:
                    st(S3(out=tsc[:, 2, 0:T], in0=conv[:, p, :], scalar=pc(f"d{l}", p), in1=OB[:, 0:T], op0=ALU.mult,
                          op1=ALU.add))
                    st.settle()
                    st(S3(out=dst, in0=tsc[:, 2, 0:T], scalar=0.5, in1=zs2[:, 2 + p, :], op0=ALU.mult, op1=ALU.mult),
                       done())
                else:
                    st(TS(tsc[:, 2, 0:T], XB[:, 0:T], -1.0, None, ALU.mult))
                    st.settle()
                    st(TTn(tsc[:, 2, 0:T], tsc[:, 2, 0:T], XB[:, 0:T], ALU.max))
                    st.settle()
                    st(TTn(tsc[:, 2, 0:T], tsc[:, 2, 0:T], XB[:, 256:512], ALU.max))
                    st.settle()
                    st(V.reciprocal(tsc[:, 2, 0:T], tsc[:, 2, 0:T]))
                    st.settle()
                    st(TTn(dst, tsc[:, 2, 0:T], OB[:, 0:T], ALU.mult), done())

            for l in range(DEPTH):
                norm2(("mix", l), f"mix_g{l}", lambda k: sig("h_raw", ("mix", l), k), lambda k: low_h(("mix", l), k, T))
                if l == 0:
                    dve.wait_ge(*at("tables2"))
                dve.wait_ge(*at("memory_set2", l))
                for j in range(2):
                    rope2(("rq", l, j), ret_q[:, j, :])
                for j in range(2):
                    rope2(("rk", l, j), ret_k[:, j, :])
                for j in range(4):
                    gate2(l, j)
                for j in range(6):
                    conv_sum(l, j)
                b = full(dve, "sdt", l)
                st(TS(tsc[0:4, 0, 0:T], b[0:4, 0:T], pc(f"dt_bias{l}", parts=4), None, ALU.add), free("sdt", l))
                b = full(dve, "mi", l)
                st(TS(tsc[32:36, 1, 0:T], b[0:4, 0:T], pc(f"b_i{l}", parts=4), None, ALU.add), free("mi", l))
                b = full(dve, "mf", l)
                st(TS(tsc[32:36, 0, 0:T], b[0:4, 0:T], pc(f"b_f2{l}", parts=4), None, ALU.add), free("mf", l))
                for j in range(6, 10):
                    conv_sum(l, j)
                gate2(l, 4)
                gate2(l, 5)
                b = full(dve, "al", l)
                st(TS(lg, b[:, 0:T], pc(f"b_alpha{l}"), None, ALU.add), free("al", l))
                dve.wait_ge(*at("ln2", l, 1))
                st.settle()
                st(TS(rowb[0:4, :], tsc[0:4, 0, 0:T], 0.0, None, ALU.max))
                st(TS(rowb[32:36, :], tsc[32:36, 0, 0:T], 0.0, None, ALU.min))
                st(TS(lx[0], lg, 0.0, None, ALU.min))
                st.settle()
                st(TTn(rows[64:68, :], rowb[0:4, :], asc[0:4, 0, 0:T], ALU.add))
                st(TTn(tsc[32:36, 2, 0:T], rowb[32:36, :], asc[32:36, 0, 0:T], ALU.subtract))
                st(TTn(lx[1], lx[0], asc[:, 1, 0:T], ALU.subtract))
                st.settle()
                st(TS(tsc[0:4, 3, 0:T], rows[64:68, :], stat[0:4, 1, 15:16], None, ALU.mult))
                st(TS(lx[0], lx[1], 1.0 / 16.0, None, ALU.mult))
                scan(rowb[32:36, :], tsc[32:36, 2, 0:T], ALU.add, 32, 36)
                st.settle()
                scan(rows[0:4, :], tsc[0:4, 3, 0:T], ALU.add, 0, 4)
                scan(lg, lx[0], ALU.add, 0, P)
                st(TTn(rows[32:36, :], tsc[32:36, 1, 0:T], rowb[32:36, :], ALU.subtract))
                st.settle()
                st(TS(rowa[0:4, :], rows[0:4, :], -1.0, None, ALU.mult))
                scan(tsc[32:36, 2, 0:T], rows[32:36, :], ALU.max, 32, 36)
                st.settle()
                st(TS(rowm[0:4, :], tsc[32:36, 2, 0:T], -1.0, None, ALU.mult))
                st(TTn(rowb[32:36, :], rowb[32:36, :], tsc[32:36, 2, 0:T], ALU.add), sig("rows_ready", l))
                for j in range(10):
                    conv_silu(l, j)
                b = full(dve, "rt", l)
                st(V.tensor_copy(cols2[:, :, :], b[:, 0:136].rearrange("p (t c) -> p t c", t=2)), free("rt", l))
                st.settle()
                for t in range(2):
                    b = full(dve, "sxt", l, t)
                    st(S3(out=vtok[:, 1, t, :].rearrange("p (h c) -> p h c", h=4),
                          in0=b[:, 0:256].rearrange("p (h c) -> p h c", h=4), scalar=0.5,
                          in1=cols2[:, t, 64:68].unsqueeze(2).broadcast_to((P, 4, 64)), op0=ALU.mult, op1=ALU.mult),
                       free("sxt", l, t))
                dve.wait_ge(*at("rowe_ready", l))
                for i in range(12):
                    g, m, hd = 12 * l + i, ORDER2[i // 4], i % 4
                    dve.wait_ge(*at("s2_full", g))
                    st.settle()
                    w = aw[g % 2]
                    if m == 0:
                        for c, n in ((0, T), (256, P)):
                            st(S3(out=w[:, c:c + n], in0=SB[g % 2][:, c:c + n], scalar=64 ** -0.5,
                                  in1=const("decay")[:, hd * T:hd * T + n], op0=ALU.mult, op1=ALU.mult),
                               sig("a_ready", g) if c else None)
                    else:
                        col = 0 if m == 1 else 32
                        for t, (c, n) in enumerate(((0, T), (256, P))):
                            st(S3(out=seg[g % 2][:, c:c + n], in0=TB[g % 2][:, c:c + n],
                                  scalar=cols2[:, t, col + hd:col + hd + 1], in1=const("segmask")[:, 0:n],
                                  op0=ALU.add, op1=ALU.add), sig("seg_arg", g) if c else None)
                        dve.wait_ge(*at("seg_exp", g))
                        st(S3(out=w[:, :], in0=SB[g % 2][:, 0:W2B], scalar=0.25 if m == 1 else 0.25 * 64 ** -0.5,
                              in1=seg[g % 2][:, :], op0=ALU.mult, op1=ALU.mult), sig("a_ready", g))
                    if i >= 3 and i % 2 == 1:
                        pair_done(l, i // 2 - 1)
                def level(n):
                    st.settle()
                    if n >= 2:
                        dve.wait_ge(*at("level_full", l, n - 2))
                    if n == 0:
                        st(V.tensor_copy(lq[0], gla_q))
                        st(V.tensor_copy(lk[0], gla_k), sig("level_ready", l, 0))
                        return
                    s_ = (*LV, P)[n - 1]
                    g4 = lg.rearrange("p (n h s) -> p n h s", h=2, s=s_)
                    x4 = lx[n % 2].rearrange("p (n h s) -> p n h s", h=2, s=s_)
                    nb = T // (2 * s_)
                    mid = g4[:, :, 0, s_ - 1:s_].broadcast_to((P, nb, s_))
                    st(TTn(x4[:, :, 1, :], g4[:, :, 1, :], mid, ALU.subtract))
                    st(TTn(x4[:, :, 0, :], mid, g4[:, :, 0, :], ALU.subtract), sig("level_arg", l, n))
                    dve.wait_ge(*at("level_exp", l, n))
                    st(TTn(lq[n % 2], gla_q, lx[n % 2], ALU.mult))
                    st(TTn(lk[n % 2], gla_k, lx[n % 2], ALU.mult), sig("level_ready", l, n))

                def pick(n):
                    dve.wait_ge(*at("level_full", l, n))
                    for hd in range(4):
                        b = (*SB, *TB)[hd]
                        done = sig("gla_picked", l, n) if hd == 3 else None
                        if n == 8:
                            st(V.tensor_copy(agla[:, hd, P:T], b[:, 0:P]), done)
                        else:
                            w = agla[:, hd, :].rearrange("p (c k) -> p c k", c=3)[:, 0:3:2, :]
                            mk = const("levels")[:, n * P:(n + 1) * P].bitcast(U32)
                            st(V.copy_predicated(w, mk.unsqueeze(1).broadcast_to((P, 2, P)),
                                                 b[:, 0:T].rearrange("p (c k) -> p c k", c=2)), done)
                level(0)
                for n in range(9):
                    if n < 8:
                        level(n + 1)
                    if n == 0:
                        pair_done(l, 5)
                    pick(n)
                pair_done(l, 6)
                pair_done(l, 7)
                st.settle()
                st(V.tensor_copy(stat[0:1, 0, 14:15], stat[0:1, 0, 13:14]), sig("o2_done", l))
                dve.wait_ge(*at("roots_ready", l))
                for m, (nm, k0) in enumerate((("ret", 0), ("ssd", 2), ("gla", 3), ("ml", 5))):
                    for p in range(2):
                        j = 2 * m + p
                        k = 2 if m == 1 else k0 + p
                        dst = zs2[:, j, :] if m == 1 else tsc[:, j % 4, 0:T]
                        st.settle()
                        st(S3(out=dst, in0=o2[:, j, :], scalar=pc(f"{nm}_g{l}", p), in1=roots[:, k, :], op0=ALU.mult,
                              op1=ALU.mult), sig("y2_ready", l, m) if m == 1 and p else None)
                        if m != 1:
                            st.settle()
                            st(S3(out=zs2[:, j, :], in0=zs2[:, j, :], scalar=1.0 if m == 3 else 0.0, in1=dst,
                                  op0=ALU.add, op1=ALU.mult), sig("y2_ready", l, m) if p else None)
                for j in range(KT):
                    low_tile(("branch2", l, j // 2), j % 2, zs2[:, j, :], j, T)

                def low_merged2(j):
                    low_tile(("merged2", l), j, sq[:, j, 0:T], j, T)
                st.settle()
                for n in range(4):
                    for j in range(KT):
                        b = full(dve, "br2", l, n, j)
                        if n == 0 and j == 0:
                            dve.wait_ge(*evacuated("g2", l, 31))
                        st.settle()
                        dst = sq[:, j, 0:T] if n == 0 else tsc[:, j % 4, 0:T]
                        st(S3(out=dst, in0=gates2[:, n * 8 + j, :], scalar=1.0, in1=b[:, 0:T], op0=ALU.add,
                              op1=ALU.mult), free("br2", l, n, j))
                        if n:
                            st.settle()
                            st(TTn(sq[:, j, 0:T], sq[:, j, 0:T], dst, ALU.add),
                               sig("merged2", l, j) if n == 3 else None)
                        if n == 3 and 1 <= j < 7:
                            low_merged2(j - 1)
                low_merged2(6)
                low_merged2(7)
                st(V.tensor_copy(stat[0:1, 0, 14:15], stat[0:1, 0, 13:14]), sig("mix_done", l))
                for j in range(KT):
                    b = full(dve, "wo2", l, j)
                    st(S3(out=x2[:, j, :], in0=b[:, 0:T], scalar=0.5, in1=x2[:, j, :], op0=ALU.mult, op1=ALU.add),
                       free("wo2", l, j))
                if l == 0:
                    norm2(("ffn", l), f"ffn_g{l}", lambda k: sig("h_raw", ("ffn", l), k),
                          lambda k: low_h(("ffn", l), k, T))
                else:
                    norm2(("ffn", l), f"ffn_g{l}", lambda k: sig("h_ready", ("ffn", l), k))
                if l == 0:
                    for F in range(NF):
                        u1, u3 = (b_[:, 0:T] for b_ in UB[F % 2])
                        dve.wait_ge(*at("up_tanh", F))
                        st(S3(out=hid[2 + F % 2], in0=hid[F % 2], scalar=1.0, in1=u1, op0=ALU.add, op1=ALU.mult))
                        dve.wait_ge(*at("up1", F))
                        st.settle()
                        st(S3(out=actb[:, F, :], in0=hid[2 + F % 2], scalar=0.5, in1=u3, op0=ALU.mult, op1=ALU.mult),
                           sig("hidden", F))
                    dve.wait_ge(*at("mlp_down", 11))
                    st(V.tensor_copy(stat[0:1, 0, 14:15], stat[0:1, 0, 13:14]), sig("ffn_done"))
                    for j in range(KT):
                        st(TTn(x2[:, j, :], YB[j // 2][:, (j % 2) * T:(j % 2 + 1) * T], x2[:, j, :], ALU.add),
                           sig("mlp_added", 0, j))
                else:
                    moe_dve(dve, st)
            norm2(("final",), "final_g2", lambda k: sig("y_normalised"))
        return new


def kernel(**inputs):
    import concourse.bacc as bacc
    from concourse.bass_utils import run_bass_kernel_spmd

    arrays = {name: np.ascontiguousarray(v) for name, v in inputs.items()}
    arrays["consts"] = constants()[1]
    events = {}
    for _ in range(2):
        nc = bacc.Bacc("TRN2", target_bir_lowering=False, num_devices=1)
        a = {name: nc.dram_tensor(f"in_{name}", v.shape, mybir.dt.from_np(v.dtype), kind="ExternalInput").ap()
             for name, v in arrays.items()}
        out = nc.dram_tensor("out_y", (1, SEQ, D), F32, kind="ExternalOutput").ap()
        events = build(nc, a, a["consts"], out, events)
    r = run_bass_kernel_spmd(nc, [{f"in_{name}": v for name, v in arrays.items()}], core_ids=[0])
    return r.results[0]["out_y"]
```
